# Optimizing a Trainium2 kernel written in Bass

```python
import jax, jax.numpy as jnp
from jax import lax
import numpy as np
import math

D_MODEL = 1024
BATCH = 1
SEQ = 512
DEPTH = 1

CTX_LEN = 256
GRID_W = 64
EPS = 1e-6
CHUNK = 128
A_GROUPS = 8
A_WIDTH = 1024
A_GROUP_DIM = A_WIDTH // A_GROUPS
N_HEADS = 16
N_KV_HEADS = 4
HEAD_DIM = 64
B_WIDTH = N_HEADS * HEAD_DIM
KV_WIDTH = N_KV_HEADS * HEAD_DIM
WINDOW = 128
BLOCK = 128
ROPE_BASE = 10000.0
N_EXPERTS = 16
CAPACITY_FACTOR = 2
D_EXPERT = 2048
OFF_U = 0
OFF_VA = OFF_U + A_WIDTH
OFF_Q = OFF_VA + A_WIDTH
OFF_K = OFF_Q + B_WIDTH
OFF_VB = OFF_K + KV_WIDTH
OFF_GATE = OFF_VB + KV_WIDTH
IN_COLS = OFF_GATE + 2 * D_MODEL


def rmsnorm(x, g):
    xf = x.astype(jnp.float32)
    y = xf * lax.rsqrt(jnp.mean(xf * xf, axis=-1, keepdims=True) + EPS)
    return (y * g.astype(jnp.float32)).astype(x.dtype)

def layernorm(x, g, b):
    xf = x.astype(jnp.float32)
    mu = jnp.mean(xf, axis=-1, keepdims=True)
    var = jnp.mean(jnp.square(xf - mu), axis=-1, keepdims=True)
    y = (xf - mu) * lax.rsqrt(var + EPS)
    return (y * g.astype(jnp.float32) + b.astype(jnp.float32)).astype(x.dtype)

def modulate(h, shift, scale):
    return h * (1 + scale) + shift

def _axis_angles(pos, dim):
    freqs = ROPE_BASE ** (-jnp.arange(0, dim, 2, dtype=jnp.float32) / dim)
    return pos.astype(jnp.float32)[:, None] * freqs[None, :]

def _rotate(x, ang):
    x1, x2 = jnp.split(x.astype(jnp.float32), 2, axis=-1)
    cos = jnp.cos(ang)[None, :, None, :]
    sin = jnp.sin(ang)[None, :, None, :]
    return jnp.concatenate([x1 * cos - x2 * sin, x1 * sin + x2 * cos], axis=-1)

def rope_2d(x, row, col):
    half = x.shape[-1] // 2
    xr, xc = x[..., :half], x[..., half:]
    out = jnp.concatenate([_rotate(xr, _axis_angles(row, half)),
                           _rotate(xc, _axis_angles(col, half))], axis=-1)
    return out.astype(x.dtype)

def chunk_gmlp(u, v, ln_g, ln_b, w_s, b_s):
    Bn, L, _ = v.shape
    v = layernorm(v, ln_g, ln_b)
    vc = v.reshape(Bn, L // CHUNK, CHUNK, A_GROUPS, A_GROUP_DIM)
    mixed = jnp.einsum('gpq,bnqgd->bnpgd', w_s, vc) + b_s.T[None, None, :, :, None]
    return u * mixed.reshape(Bn, L, A_WIDTH)

def window_gqa(q, k, v, k_ctx, v_ctx, sink):
    Bn, L, H, Dh = q.shape
    nb = L // BLOCK
    rep = H // N_KV_HEADS
    scale = HEAD_DIM ** -0.5
    qb = q.reshape(Bn, nb, BLOCK, N_KV_HEADS, rep, Dh)

    def band(t):
        tb = t.reshape(Bn, nb, BLOCK, N_KV_HEADS, Dh)
        tp = jnp.pad(tb, ((0, 0), (1, 1), (0, 0), (0, 0), (0, 0)))
        return jnp.concatenate([tp[:, :-2], tp[:, 1:-1], tp[:, 2:]], axis=2)

    kb, vb = band(k), band(v)
    a_idx = jnp.arange(BLOCK)[:, None]
    s_idx = jnp.arange(3 * BLOCK)[None, :]
    rel = s_idx - BLOCK - a_idx
    sink_l = sink.astype(jnp.float32).reshape(N_KV_HEADS, rep)[None, :, :, None, None]
    vals_ctx = v_ctx.astype(jnp.float32)

    def one_block(args):
        n, qn, kn, vn = args
        key_pos = (n - 1) * BLOCK + s_idx
        mask = (jnp.abs(rel) <= WINDOW) & (key_pos >= 0) & (key_pos < L)
        s_loc = jnp.einsum('bqkrd,bskd->bkrqs', qn, kn, preferred_element_type=jnp.float32) * scale
        s_loc = jnp.where(mask, s_loc, jnp.float32(-1e30))
        s_ctx = jnp.einsum('bqkrd,bskd->bkrqs', qn, k_ctx, preferred_element_type=jnp.float32) * scale
        logits = jnp.concatenate([s_loc, s_ctx], axis=-1)
        m = jnp.maximum(jnp.max(logits, axis=-1, keepdims=True), sink_l)
        p = jnp.exp(logits - m)
        denom = jnp.sum(p, axis=-1, keepdims=True) + jnp.exp(sink_l - m)
        vals = jnp.concatenate([vn.astype(jnp.float32), vals_ctx], axis=1)
        out = jnp.einsum('bkrqs,bskd->bqkrd', p / denom, vals)
        return out.astype(q.dtype)

    xs = (jnp.arange(nb), jnp.moveaxis(qb, 1, 0), jnp.moveaxis(kb, 1, 0), jnp.moveaxis(vb, 1, 0))
    out = lax.map(one_block, xs)
    return jnp.moveaxis(out, 0, 1).reshape(Bn, L, H * Dh)

def expert_choice_ffn(h, w_router, w_gate, w_up, w_down):
    Bn, N, D = h.shape
    cap = max(1, CAPACITY_FACTOR * N // N_EXPERTS)
    logits = jnp.einsum('bnd,de->bne', h, w_router, preferred_element_type=jnp.float32)
    aff = jax.nn.softmax(logits, axis=-1)
    top_w, top_idx = lax.top_k(jnp.swapaxes(aff, 1, 2), cap)
    xe = jax.vmap(lambda hb, ib: hb[ib])(h, top_idx)
    g = jnp.einsum('becd,edf->becf', xe, w_gate)
    u = jnp.einsum('becd,edf->becf', xe, w_up)
    y = jnp.einsum('becf,efd->becd', jax.nn.silu(g) * u, w_down)
    y = y * top_w[..., None].astype(y.dtype)
    return jax.vmap(lambda ib, yb: jnp.zeros((N, D), yb.dtype).at[ib.reshape(-1)].add(yb.reshape(-1, D)))(top_idx, y)

def first_inputs(seed: int = 0) -> dict:
    key = jax.random.key(seed)
    ks = jax.random.split(key, 24)
    f32 = jnp.float32
    D = D_MODEL

    def nrm(k, shape, s):
        return jax.random.normal(k, shape, f32) * s

    return {
        "x": nrm(ks[0], (BATCH, SEQ, D), 1.0),
        "c": nrm(ks[1], (BATCH, D), 1.0),
        "ctx": nrm(ks[2], (BATCH, CTX_LEN, D), 1.0),
        "c_ctx": nrm(ks[3], (D,), 1.0),
        "w_ada": nrm(ks[4], (DEPTH, D, 6 * D), 0.3 * D ** -0.5),
        "b_ada": nrm(ks[5], (DEPTH, 6 * D), 0.02),
        "norm1_g": 1.0 + nrm(ks[6], (DEPTH, D), 0.05),
        "w_in": nrm(ks[7], (DEPTH, D, IN_COLS), D ** -0.5),
        "b_merge_gate": nrm(ks[8], (DEPTH, 2 * D), 0.02),
        "gmlp_ln_g": 1.0 + nrm(ks[9], (DEPTH, A_WIDTH), 0.05),
        "gmlp_ln_b": nrm(ks[10], (DEPTH, A_WIDTH), 0.02),
        "w_spatial": nrm(ks[11], (DEPTH, A_GROUPS, CHUNK, CHUNK), CHUNK ** -0.5),
        "b_spatial": nrm(ks[12], (DEPTH, A_GROUPS, CHUNK), 0.02),
        "attn_sink": nrm(ks[13], (DEPTH, N_HEADS), 0.5),
        "w_proj_a": nrm(ks[14], (DEPTH, A_WIDTH, D), A_WIDTH ** -0.5),
        "w_proj_b": nrm(ks[15], (DEPTH, B_WIDTH, D), B_WIDTH ** -0.5),
        "w_out": nrm(ks[16], (DEPTH, D, D), D ** -0.5),
        "norm2_g": 1.0 + nrm(ks[17], (DEPTH, D), 0.05),
        "w_router": nrm(ks[18], (DEPTH, D, N_EXPERTS), D ** -0.5),
        "w_exp_gate": nrm(ks[19], (DEPTH, N_EXPERTS, D, D_EXPERT), D ** -0.5),
        "w_exp_up": nrm(ks[20], (DEPTH, N_EXPERTS, D, D_EXPERT), D ** -0.5),
        "w_exp_down": nrm(ks[21], (DEPTH, N_EXPERTS, D_EXPERT, D), D_EXPERT ** -0.5),
        "final_g": 1.0 + nrm(ks[22], (D,), 0.05),
    }

def first_block(x, c, ctx, c_ctx, w_ada, b_ada, norm1_g, w_in, b_merge_gate, gmlp_ln_g, gmlp_ln_b,
              w_spatial, b_spatial, attn_sink, w_proj_a, w_proj_b, w_out, norm2_g, w_router,
              w_exp_gate, w_exp_up, w_exp_down, final_g):
    Bn, L, D = x.shape
    rows = L // GRID_W
    row = jnp.repeat(jnp.arange(rows), GRID_W)
    col = jnp.tile(jnp.arange(GRID_W), rows)

    for l in range(DEPTH):
        mod = jax.nn.silu(c) @ w_ada[l] + b_ada[l]
        sh1, sc1, g1, sh2, sc2, g2 = jnp.split(mod[:, None, :], 6, axis=-1)
        mod_ctx = jax.nn.silu(c_ctx) @ w_ada[l] + b_ada[l]
        csh1, csc1 = mod_ctx[:D], mod_ctx[D:2 * D]

        h = modulate(rmsnorm(x, norm1_g[l]), sh1, sc1)
        proj = h @ w_in[l]
        u_a, v_a, q, k, v, gates = jnp.split(proj, [OFF_VA, OFF_Q, OFF_K, OFF_VB, OFF_GATE], axis=-1)

        hc = modulate(rmsnorm(ctx, norm1_g[l]), csh1, csc1)
        kv_ctx = hc @ w_in[l][:, OFF_K:OFF_GATE]
        k_ctx, v_ctx = jnp.split(kv_ctx.reshape(Bn, -1, 2 * N_KV_HEADS, HEAD_DIM), 2, axis=2)

        y_a = chunk_gmlp(jax.nn.gelu(u_a), jax.nn.gelu(v_a), gmlp_ln_g[l], gmlp_ln_b[l],
                         w_spatial[l], b_spatial[l])

        qh = rope_2d(q.reshape(Bn, L, N_HEADS, HEAD_DIM), row, col)
        kh = rope_2d(k.reshape(Bn, L, N_KV_HEADS, HEAD_DIM), row, col)
        vh = v.reshape(Bn, L, N_KV_HEADS, HEAD_DIM)
        y_b = window_gqa(qh, kh, vh, k_ctx, v_ctx, attn_sink[l])

        g_a, g_b = jnp.split(jax.nn.sigmoid(gates + b_merge_gate[l]), 2, axis=-1)
        merged = g_a * (y_a @ w_proj_a[l]) + g_b * (y_b @ w_proj_b[l])
        x = x + g1 * (merged @ w_out[l])

        h2 = modulate(rmsnorm(x, norm2_g[l]), sh2, sc2)
        x = x + g2 * expert_choice_ffn(h2, w_router[l], w_exp_gate[l], w_exp_up[l], w_exp_down[l])

    return rmsnorm(x, final_g)


N_META = 16
N_DIR = 2
RWKV_HEADS = 8
RWKV_WIDTH = RWKV_HEADS * HEAD_DIM
DECAY_LORA = 64
ICL_LORA = 64
GATE_LORA = 160
LNX_EPS = 64e-5
ATTN_Q_HEADS = 8
ATTN_KV_HEADS = 2
ATTN_GROUP = ATTN_Q_HEADS // ATTN_KV_HEADS
ATTN_Q_WIDTH = ATTN_Q_HEADS * HEAD_DIM
ATTN_KV_WIDTH = ATTN_KV_HEADS * HEAD_DIM
Q_BLOCK = 128
ROPE_THETA = 10000.0
AXIS_DIM = HEAD_DIM // 2
AXIS_FREQS = AXIS_DIM // 2
D_FF = 4 * D_MODEL
NORM_EPS = 1e-6
RWKV_IN_WIDTH = 3 * RWKV_WIDTH + N_DIR * DECAY_LORA + N_DIR * ICL_LORA + GATE_LORA
IN_WIDTH = RWKV_IN_WIDTH + ATTN_Q_WIDTH + 2 * ATTN_KV_WIDTH + 2 * D_MODEL
IN_SPLITS = [RWKV_IN_WIDTH,
             RWKV_IN_WIDTH + ATTN_Q_WIDTH,
             RWKV_IN_WIDTH + ATTN_Q_WIDTH + ATTN_KV_WIDTH,
             RWKV_IN_WIDTH + ATTN_Q_WIDTH + 2 * ATTN_KV_WIDTH,
             RWKV_IN_WIDTH + ATTN_Q_WIDTH + 2 * ATTN_KV_WIDTH + D_MODEL]
RWKV_SPLITS = [RWKV_WIDTH, 2 * RWKV_WIDTH, 3 * RWKV_WIDTH,
               3 * RWKV_WIDTH + N_DIR * DECAY_LORA,
               3 * RWKV_WIDTH + N_DIR * DECAY_LORA + N_DIR * ICL_LORA]


def rms_norm(x, g, eps=NORM_EPS):
    xf = x.astype(jnp.float32)
    y = xf * lax.rsqrt(jnp.mean(xf * xf, axis=-1, keepdims=True) + eps)
    return (y * g.astype(jnp.float32)).astype(x.dtype)

def centred_shift(p, mu):
    prev = jnp.pad(p[:, :-1], ((0, 0), (1, 0), (0, 0)))
    nxt = jnp.pad(p[:, 1:], ((0, 0), (0, 1), (0, 0)))
    return p + mu[0] * (prev - p) + mu[1] * (nxt - p)

def to_dirs(fwd, bwd):
    B, L, _ = fwd.shape
    t = jnp.stack([fwd, jnp.flip(bwd, axis=1)], axis=0).astype(jnp.float32)
    return t.reshape(N_DIR, B, L, RWKV_HEADS, HEAD_DIM).transpose(2, 0, 1, 3, 4)

def rwkv7_step(S, inp):
    r, w, k, v, kk, kka = inp
    sa = jnp.einsum('dbhij,dbhj->dbhi', S, -kk)
    S = S * w[..., None, :] + sa[..., :, None] * kka[..., None, :] + v[..., :, None] * k[..., None, :]
    y = jnp.einsum('dbhij,dbhj->dbhi', S, r)
    return S, y

def rwkv7_mixer(p, shift_mu, w0, w2, a0, a2, g2, k_k, k_a, r_k, lnx_g, lnx_b):
    B, L, _ = p.shape
    z = centred_shift(p, shift_mu)
    r, k, v, wd, ad, gd = jnp.split(z, RWKV_SPLITS, axis=-1)
    wd = wd.reshape(B, L, N_DIR, DECAY_LORA)
    ad = ad.reshape(B, L, N_DIR, ICL_LORA)
    w_log = -jax.nn.softplus(-(w0 + jnp.einsum('bldr,drc->bldc', jnp.tanh(wd), w2))) - 0.5
    decay = jnp.exp(-jnp.exp(w_log.astype(jnp.float32)))
    a = jax.nn.sigmoid(a0 + jnp.einsum('bldr,drc->bldc', ad, a2))
    g = jax.nn.sigmoid(gd) @ g2
    kk = (k * k_k).reshape(B, L, RWKV_HEADS, HEAD_DIM).astype(jnp.float32)
    kk = kk / jnp.maximum(jnp.linalg.norm(kk, axis=-1, keepdims=True), 1e-12)
    kk = kk.reshape(B, L, RWKV_WIDTH)
    k_dir = k[:, :, None, :] * (1.0 + (a - 1.0) * k_a)
    kka = kk[:, :, None, :] * a
    xs = (to_dirs(r, r), to_dirs(decay[:, :, 0], decay[:, :, 1]),
          to_dirs(k_dir[:, :, 0], k_dir[:, :, 1]), to_dirs(v, v), to_dirs(kk, kk),
          to_dirs(kka[:, :, 0], kka[:, :, 1]))
    S0 = jnp.zeros((N_DIR, B, RWKV_HEADS, HEAD_DIM, HEAD_DIM), jnp.float32)
    _, ys = lax.scan(rwkv7_step, S0, xs)
    ys = ys.transpose(1, 2, 0, 3, 4)
    y = ys[0] + jnp.flip(ys[1], axis=1)
    mu = jnp.mean(y, axis=-1, keepdims=True)
    var = jnp.mean(jnp.square(y - mu), axis=-1, keepdims=True)
    y = (y - mu) * lax.rsqrt(var + LNX_EPS)
    y = y * lnx_g.reshape(RWKV_HEADS, HEAD_DIM) + lnx_b.reshape(RWKV_HEADS, HEAD_DIM)
    rh = r.reshape(B, L, RWKV_HEADS, HEAD_DIM).astype(jnp.float32)
    kh = jnp.mean(k_dir, axis=2).reshape(B, L, RWKV_HEADS, HEAD_DIM).astype(jnp.float32)
    vh = v.reshape(B, L, RWKV_HEADS, HEAD_DIM).astype(jnp.float32)
    bonus = jnp.sum(rh * kh * r_k, axis=-1, keepdims=True) * vh
    out = (y + bonus).reshape(B, L, RWKV_WIDTH).astype(p.dtype)
    return out * g

def axial_rope_tables(n_tokens):
    rows = n_tokens // GRID_W
    inv_freq = ROPE_THETA ** (-jnp.arange(AXIS_FREQS, dtype=jnp.float32) * 2.0 / AXIS_DIM)
    row_ang = jnp.arange(rows, dtype=jnp.float32)[:, None] * inv_freq
    col_ang = jnp.arange(GRID_W, dtype=jnp.float32)[:, None] * inv_freq
    grid = jnp.stack([jnp.broadcast_to(row_ang[:, None, :], (rows, GRID_W, AXIS_FREQS)),
                      jnp.broadcast_to(col_ang[None, :, :], (rows, GRID_W, AXIS_FREQS))], axis=2)
    grid = grid.reshape(rows * GRID_W, 2, AXIS_FREQS)
    ang = jnp.concatenate([jnp.zeros((N_META, 2, AXIS_FREQS), jnp.float32), grid], axis=0)
    return jnp.cos(ang), jnp.sin(ang)

def apply_axial_rope(x, cos, sin):
    B, L, H, _ = x.shape
    xf = x.astype(jnp.float32).reshape(B, L, H, 2, 2, AXIS_FREQS)
    x1, x2 = xf[..., 0, :], xf[..., 1, :]
    c, s = cos[None, :, None], sin[None, :, None]
    out = jnp.stack([x1 * c - x2 * s, x2 * c + x1 * s], axis=-2)
    return out.reshape(B, L, H, HEAD_DIM).astype(x.dtype)

def gqa_axial_attention(q, k, v, q_norm_g, k_norm_g, cos, sin):
    B, L, _ = q.shape
    q = rms_norm(q.reshape(B, L, ATTN_Q_HEADS, HEAD_DIM), q_norm_g)
    k = rms_norm(k.reshape(B, L, ATTN_KV_HEADS, HEAD_DIM), k_norm_g)
    q = apply_axial_rope(q, cos, sin)
    k = apply_axial_rope(k, cos, sin)
    v = v.reshape(B, L, ATTN_KV_HEADS, HEAD_DIM)
    q = q.reshape(B, L, ATTN_KV_HEADS, ATTN_GROUP, HEAD_DIM) * (HEAD_DIM ** -0.5)

    def block_attn(qb):
        s = jnp.einsum('bqhgn,bkhn->bhgqk', qb, k).astype(jnp.float32)
        pr = jax.nn.softmax(s, axis=-1).astype(v.dtype)
        return jnp.einsum('bhgqk,bkhn->bqhgn', pr, v)

    meta_out = block_attn(q[:, :N_META])
    n_blk = (L - N_META) // Q_BLOCK
    qr = q[:, N_META:].reshape(B, n_blk, Q_BLOCK, ATTN_KV_HEADS, ATTN_GROUP, HEAD_DIM)
    real_out = lax.map(block_attn, qr.transpose(1, 0, 2, 3, 4, 5))
    real_out = real_out.transpose(1, 0, 2, 3, 4, 5).reshape(B, L - N_META, ATTN_Q_WIDTH)
    return jnp.concatenate([meta_out.reshape(B, N_META, ATTN_Q_WIDTH), real_out], axis=1)

def second_inputs(seed: int = 0) -> dict:
    key = jax.random.key(seed)
    ks = jax.random.split(key, 26)
    f32 = jnp.float32

    def nrm(k, shape, scale):
        return jax.random.normal(k, shape, f32) * scale

    ramp = jnp.linspace(-6.5, -1.5, RWKV_WIDTH, dtype=f32)
    return {
        "x": nrm(ks[0], (BATCH, SEQ, D_MODEL), 1.0),
        "meta_tokens": nrm(ks[1], (N_META, D_MODEL), 1.0),
        "mix_norm_g": 1.0 + nrm(ks[2], (DEPTH, D_MODEL), 0.02),
        "w_in": nrm(ks[3], (DEPTH, D_MODEL, IN_WIDTH), D_MODEL ** -0.5),
        "rwkv_shift": jax.random.uniform(ks[4], (DEPTH, 2, RWKV_IN_WIDTH), f32, 0.0, 0.5),
        "decay_w0": ramp + nrm(ks[5], (DEPTH, N_DIR, RWKV_WIDTH), 0.1),
        "decay_w2": nrm(ks[6], (DEPTH, N_DIR, DECAY_LORA, RWKV_WIDTH), 0.5 * DECAY_LORA ** -0.5),
        "icl_a0": nrm(ks[7], (DEPTH, N_DIR, RWKV_WIDTH), 0.1),
        "icl_a2": nrm(ks[8], (DEPTH, N_DIR, ICL_LORA, RWKV_WIDTH), 0.5 * ICL_LORA ** -0.5),
        "gate_w2": nrm(ks[9], (DEPTH, GATE_LORA, RWKV_WIDTH), GATE_LORA ** -0.5),
        "k_k": 0.85 + nrm(ks[10], (DEPTH, RWKV_WIDTH), 0.02),
        "k_a": 1.0 + nrm(ks[11], (DEPTH, RWKV_WIDTH), 0.02),
        "r_k": nrm(ks[12], (DEPTH, RWKV_HEADS, HEAD_DIM), 0.1),
        "lnx_g": 1.0 + nrm(ks[13], (DEPTH, RWKV_WIDTH), 0.02),
        "lnx_b": nrm(ks[14], (DEPTH, RWKV_WIDTH), 0.02),
        "q_norm_g": 1.0 + nrm(ks[15], (DEPTH, HEAD_DIM), 0.02),
        "k_norm_g": 1.0 + nrm(ks[16], (DEPTH, HEAD_DIM), 0.02),
        "w_branch_rwkv": nrm(ks[17], (DEPTH, RWKV_WIDTH, D_MODEL), RWKV_WIDTH ** -0.5),
        "w_branch_attn": nrm(ks[18], (DEPTH, ATTN_Q_WIDTH, D_MODEL), ATTN_Q_WIDTH ** -0.5),
        "w_out": nrm(ks[19], (DEPTH, D_MODEL, D_MODEL), D_MODEL ** -0.5),
        "ffn_norm_g": 1.0 + nrm(ks[20], (DEPTH, D_MODEL), 0.02),
        "w_ff1": nrm(ks[21], (DEPTH, D_MODEL, D_FF), D_MODEL ** -0.5),
        "w_ff2": nrm(ks[22], (DEPTH, D_FF, D_MODEL), D_FF ** -0.5),
        "final_norm_g": 1.0 + nrm(ks[23], (D_MODEL,), 0.02),
    }

def second_block(x, meta_tokens, mix_norm_g, w_in, rwkv_shift, decay_w0, decay_w2, icl_a0, icl_a2,
              gate_w2, k_k, k_a, r_k, lnx_g, lnx_b, q_norm_g, k_norm_g, w_branch_rwkv,
              w_branch_attn, w_out, ffn_norm_g, w_ff1, w_ff2, final_norm_g):
    B, n_tok, D = x.shape
    meta = jnp.broadcast_to(meta_tokens[None].astype(x.dtype), (B, N_META, D))
    h = jnp.concatenate([meta, x], axis=1)
    cos, sin = axial_rope_tables(n_tok)
    for i in range(DEPTH):
        u = rms_norm(h, mix_norm_g[i])
        proj = u @ w_in[i]
        p_rwkv, p_q, p_k, p_v, p_gate_a, p_gate_b = jnp.split(proj, IN_SPLITS, axis=-1)
        y_a = rwkv7_mixer(p_rwkv, rwkv_shift[i], decay_w0[i], decay_w2[i], icl_a0[i], icl_a2[i],
                          gate_w2[i], k_k[i], k_a[i], r_k[i], lnx_g[i], lnx_b[i])
        y_b = gqa_axial_attention(p_q, p_k, p_v, q_norm_g[i], k_norm_g[i], cos, sin)
        merged = (jax.nn.sigmoid(p_gate_a) * (y_a @ w_branch_rwkv[i])
                  + jax.nn.sigmoid(p_gate_b) * (y_b @ w_branch_attn[i]))
        h = h + merged @ w_out[i]
        f = rms_norm(h, ffn_norm_g[i]) @ w_ff1[i]
        h = h + jnp.square(jax.nn.relu(f)) @ w_ff2[i]
    return rms_norm(h, final_norm_g)[:, N_META:]


_first_inputs = second_inputs


def second_inputs(seed=0):
    import zlib

    import numpy as np

    out = dict(_first_inputs(seed))
    spreads = {}
    factors = {'mix_norm_g': 4.69,
     'decay_w2': 6.252,
     'icl_a0': 4.411,
     'k_k': 64.0,
     'k_a': 7.569,
     'lnx_g': 64.0,
     'lnx_b': 64.0,
     'q_norm_g': 30.998,
     'k_norm_g': 24.391,
     'ffn_norm_g': 19.872,
     'final_norm_g': 8.432}
    for name, (base, spread) in spreads.items():
        noise = np.random.default_rng([zlib.crc32(name.encode()), seed]).standard_normal(out[name].shape)
        drawn = base * np.exp(spread * noise) if base else spread * noise
        out[name] = __import__('jax').numpy.asarray(drawn.astype(out[name].dtype))
    for name, factor in factors.items():
        out[name] = (out[name] * factor).astype(out[name].dtype)
    return out


_narrow_inputs = second_inputs


def second_inputs(seed=0):

    out = dict(_narrow_inputs(seed))
    wider = {'k_k': 7.22, 'lnx_g': 4.07, 'lnx_b': 4.22, 'q_norm_g': 3.58, 'final_norm_g': 3.27}
    for name, times in wider.items():
        mean = out[name].mean()
        out[name] = (mean + times * (out[name] - mean)).astype(out[name].dtype)
    return out


DEPTH_3 = 2

RET_HEADS = 8
RET_DK = 64
RET_DV = 128
RET_CHUNK = 128
CONV_W = 1024
CONV_K = 3
MLA_HEADS = 8
MLA_NOPE = 128
MLA_ROPE = 64
MLA_DV = 128
Q_LORA = 384
KV_LORA = 256
ATTN_BLOCK = 128
N_EVEN = (DEPTH_3 + 1) // 2
N_ODD = DEPTH_3 // 2

RET_QK = RET_HEADS * RET_DK
RET_V = RET_HEADS * RET_DV
EVEN_SPLITS = (RET_QK, RET_QK, RET_V, RET_V, CONV_W, CONV_W, CONV_W, CONV_W)
EVEN_IN = sum(EVEN_SPLITS)
EVEN_MIX = RET_V + CONV_W
MLA_QK = MLA_NOPE + MLA_ROPE
MLA_V = MLA_HEADS * MLA_DV
ODD_SPLITS = (Q_LORA, KV_LORA, MLA_ROPE, MLA_V)
ODD_IN = sum(ODD_SPLITS)


def rms_norm_3(x, g):
    xf = x.astype(jnp.float32)
    y = xf * lax.rsqrt(jnp.mean(xf * xf, axis=-1, keepdims=True) + EPS)
    return (y * g.astype(jnp.float32)).astype(x.dtype)

def rope(x, positions):
    d = x.shape[-1]
    inv = ROPE_BASE ** (-jnp.arange(0, d, 2, dtype=jnp.float32) / d)
    ang = positions.astype(jnp.float32)[..., None] * inv
    cos = jnp.cos(ang)[:, :, None, :]
    sin = jnp.sin(ang)[:, :, None, :]
    xf = x.astype(jnp.float32)
    x1, x2 = xf[..., : d // 2], xf[..., d // 2:]
    out = jnp.concatenate([x1 * cos - x2 * sin, x1 * sin + x2 * cos], axis=-1)
    return out.astype(x.dtype)

def split_cols(h, sizes):
    return jnp.split(h, np.cumsum(sizes)[:-1].tolist(), axis=-1)

def retention(q, k, v):
    b, s, h, dk = q.shape
    dv = v.shape[-1]
    c = RET_CHUNK
    n = s // c
    dt = q.dtype
    log_gamma = jnp.log1p(-jnp.exp2(-5.0 - jnp.arange(h, dtype=jnp.float32)))
    i = jnp.arange(c, dtype=jnp.float32)
    rel = i[:, None] - i[None, :]
    intra = jnp.where(rel >= 0, jnp.exp(log_gamma[:, None, None] * jnp.maximum(rel, 0.0)), 0.0).astype(dt)
    xi = jnp.exp(log_gamma[:, None] * (i + 1.0)).astype(dt)
    zeta = jnp.exp(log_gamma[:, None] * (c - 1.0 - i)).astype(dt)
    gamma_c = jnp.exp(log_gamma * c).astype(dt)
    qc = q.reshape(b, n, c, h, dk)
    kc = k.reshape(b, n, c, h, dk)
    vc = v.reshape(b, n, c, h, dv)
    scores = jnp.einsum('bnihd,bnjhd->bnhij', qc, kc) * intra
    inner = jnp.einsum('bnhij,bnjhe->bnihe', scores, vc)
    kv = jnp.einsum('bnjhd,hj,bnjhe->nbhde', kc, zeta, vc)

    def step(state, kv_i):
        return gamma_c[None, :, None, None] * state + kv_i, state

    _, prev = lax.scan(step, jnp.zeros((b, h, dk, dv), dt), kv)
    cross = jnp.einsum('bnihd,nbhde,hi->bnihe', qc, prev, xi)
    return (inner + cross).reshape(b, s, h, dv)

def short_conv(u, w, bias):
    s = u.shape[1]
    up = jnp.pad(u, ((0, 0), (CONV_K - 1, 0), (0, 0)))
    out = up[:, 0:s] * w[0]
    for tap in range(1, CONV_K):
        out = out + up[:, tap:tap + s] * w[tap]
    return out + bias

def even_layer(h, positions, w_in, conv_w, conv_b, gn, w_out):
    b, s, _ = h.shape
    q, k, v, g_ret, cb, cc, cx, g_conv = split_cols(h @ w_in, EVEN_SPLITS)
    q = rope(q.reshape(b, s, RET_HEADS, RET_DK), positions)
    k = rope(k.reshape(b, s, RET_HEADS, RET_DK), positions) * (RET_DK ** -0.5)
    v = v.reshape(b, s, RET_HEADS, RET_DV)
    r = retention(q, k, v)
    r = rms_norm_3(r, gn.reshape(RET_HEADS, RET_DV)).reshape(b, s, RET_V)
    y_conv = cb * short_conv(cc * cx, conv_w, conv_b)
    mix = jnp.concatenate([r * jax.nn.silu(g_ret), y_conv * jax.nn.silu(g_conv)], axis=-1)
    return mix @ w_out

def causal_mla_attention(q_nope, q_rope, k_nope, k_rope, v):
    s = q_nope.shape[1]
    scale = MLA_QK ** -0.5
    outs = []
    for blk in range(s // ATTN_BLOCK):
        lo, hi = blk * ATTN_BLOCK, (blk + 1) * ATTN_BLOCK
        sc = (jnp.einsum('bqhd,bkhd->bhqk', q_nope[:, lo:hi].astype(jnp.float32), k_nope[:, :hi].astype(jnp.float32))
              + jnp.einsum('bqhd,bkd->bhqk', q_rope[:, lo:hi].astype(jnp.float32), k_rope[:, :hi].astype(jnp.float32))) * scale
        qpos = lo + jnp.arange(ATTN_BLOCK)
        kpos = jnp.arange(hi)
        sc = jnp.where(kpos[None, :] <= qpos[:, None], sc, -jnp.inf)
        p = jax.nn.softmax(sc, axis=-1).astype(v.dtype)
        outs.append(jnp.einsum('bhqk,bkhd->bqhd', p, v[:, :hi]))
    return jnp.concatenate(outs, axis=1)

def odd_layer(h, positions, w_in, q_a_norm, w_qb, kv_a_norm, w_kvb, w_out):
    b, s, _ = h.shape
    cq, ckv, k_rope, gate = split_cols(h @ w_in, ODD_SPLITS)
    q = (rms_norm_3(cq, q_a_norm) @ w_qb).reshape(b, s, MLA_HEADS, MLA_QK)
    q_nope = q[..., :MLA_NOPE]
    q_rope = rope(q[..., MLA_NOPE:], positions)
    kv = (rms_norm_3(ckv, kv_a_norm) @ w_kvb).reshape(b, s, MLA_HEADS, MLA_NOPE + MLA_DV)
    k_nope, v = kv[..., :MLA_NOPE], kv[..., MLA_NOPE:]
    k_rope = rope(k_rope[:, :, None, :], positions)[:, :, 0]
    o = causal_mla_attention(q_nope, q_rope, k_nope, k_rope, v)
    return (o.reshape(b, s, MLA_V) * jax.nn.silu(gate)) @ w_out

def third_inputs(seed: int = 0) -> dict:
    key = jax.random.key(seed)
    ks = jax.random.split(key, 16)
    f32 = jnp.float32
    nrm = lambda k, shape, scale: jax.random.normal(k, shape, f32) * scale
    x = jax.random.normal(ks[0], (BATCH, SEQ, D_MODEL), f32)
    offsets = jax.random.randint(ks[1], (BATCH, 1), 0, 1024, dtype=jnp.int32)
    positions = (offsets + jnp.arange(SEQ, dtype=jnp.int32)[None, :]).astype(jnp.int32)
    pre_norm = 1.0 + nrm(ks[2], (DEPTH_3, D_MODEL), 0.02)
    post_norm = 1.0 + nrm(ks[3], (DEPTH_3, D_MODEL), 0.02)
    even_w_in = nrm(ks[4], (N_EVEN, D_MODEL, EVEN_IN), D_MODEL ** -0.5)
    even_conv_w = nrm(ks[5], (N_EVEN, CONV_K, CONV_W), CONV_K ** -0.5)
    even_conv_b = nrm(ks[6], (N_EVEN, CONV_W), 0.01)
    ret_gn = 1.0 + nrm(ks[7], (N_EVEN, RET_V), 0.02)
    even_w_out = nrm(ks[8], (N_EVEN, EVEN_MIX, D_MODEL), EVEN_MIX ** -0.5)
    odd_w_in = nrm(ks[9], (N_ODD, D_MODEL, ODD_IN), D_MODEL ** -0.5)
    q_a_norm = 1.0 + nrm(ks[10], (N_ODD, Q_LORA), 0.02)
    w_qb = nrm(ks[11], (N_ODD, Q_LORA, MLA_HEADS * MLA_QK), Q_LORA ** -0.5)
    kv_a_norm = 1.0 + nrm(ks[12], (N_ODD, KV_LORA), 0.02)
    w_kvb = nrm(ks[13], (N_ODD, KV_LORA, MLA_HEADS * (MLA_NOPE + MLA_DV)), KV_LORA ** -0.5)
    odd_w_out = nrm(ks[14], (N_ODD, MLA_V, D_MODEL), MLA_V ** -0.5)
    return {"x": x, "positions": positions, "pre_norm": pre_norm, "post_norm": post_norm,
            "even_w_in": even_w_in, "even_conv_w": even_conv_w, "even_conv_b": even_conv_b,
            "ret_gn": ret_gn, "even_w_out": even_w_out, "odd_w_in": odd_w_in,
            "q_a_norm": q_a_norm, "w_qb": w_qb, "kv_a_norm": kv_a_norm, "w_kvb": w_kvb,
            "odd_w_out": odd_w_out}

def third_block(x, positions, pre_norm, post_norm, even_w_in, even_conv_w, even_conv_b, ret_gn,
              even_w_out, odd_w_in, q_a_norm, w_qb, kv_a_norm, w_kvb, odd_w_out):
    h = x
    for layer in range(DEPTH_3):
        u = rms_norm_3(h, pre_norm[layer])
        if layer % 2 == 0:
            e = layer // 2
            y = even_layer(u, positions, even_w_in[e], even_conv_w[e], even_conv_b[e], ret_gn[e], even_w_out[e])
        else:
            o = layer // 2
            y = odd_layer(u, positions, odd_w_in[o], q_a_norm[o], w_qb[o], kv_a_norm[o], w_kvb[o], odd_w_out[o])
        h = h + rms_norm_3(y, post_norm[layer])
    return h


def setup_inputs(seed=0):
    out = dict(first_inputs(seed))
    for name, value in second_inputs(seed + 1).items():
        if name != "x":
            out[name + "_2"] = value
    for name, value in third_inputs(seed + 2).items():
        if name != "x":
            out[name + "_3"] = value
    return out


def reference(
    x, c, ctx, c_ctx, w_ada, b_ada, norm1_g, w_in, b_merge_gate, gmlp_ln_g, gmlp_ln_b,
    w_spatial, b_spatial, attn_sink, w_proj_a, w_proj_b, w_out, norm2_g, w_router, w_exp_gate,
    w_exp_up, w_exp_down, final_g, meta_tokens_2, mix_norm_g_2, w_in_2, rwkv_shift_2,
    decay_w0_2, decay_w2_2, icl_a0_2, icl_a2_2, gate_w2_2, k_k_2, k_a_2, r_k_2, lnx_g_2,
    lnx_b_2, q_norm_g_2, k_norm_g_2, w_branch_rwkv_2, w_branch_attn_2, w_out_2, ffn_norm_g_2,
    w_ff1_2, w_ff2_2, final_norm_g_2, positions_3, pre_norm_3, post_norm_3, even_w_in_3,
    even_conv_w_3, even_conv_b_3, ret_gn_3, even_w_out_3, odd_w_in_3, q_a_norm_3, w_qb_3,
    kv_a_norm_3, w_kvb_3, odd_w_out_3,
):
    x = first_block(
        x, c, ctx, c_ctx, w_ada, b_ada, norm1_g, w_in, b_merge_gate, gmlp_ln_g, gmlp_ln_b,
        w_spatial, b_spatial, attn_sink, w_proj_a, w_proj_b, w_out, norm2_g, w_router,
        w_exp_gate, w_exp_up, w_exp_down, final_g,
    )
    x = second_block(
        x, meta_tokens_2, mix_norm_g_2, w_in_2, rwkv_shift_2, decay_w0_2, decay_w2_2, icl_a0_2,
        icl_a2_2, gate_w2_2, k_k_2, k_a_2, r_k_2, lnx_g_2, lnx_b_2, q_norm_g_2, k_norm_g_2,
        w_branch_rwkv_2, w_branch_attn_2, w_out_2, ffn_norm_g_2, w_ff1_2, w_ff2_2,
        final_norm_g_2,
    )
    return third_block(
        x, positions_3, pre_norm_3, post_norm_3, even_w_in_3, even_conv_w_3, even_conv_b_3,
        ret_gn_3, even_w_out_3, odd_w_in_3, q_a_norm_3, w_qb_3, kv_a_norm_3, w_kvb_3,
        odd_w_out_3,
    )


_drawn_inputs = setup_inputs


def setup_inputs(seed=0):
    import zlib

    import numpy as np

    out = dict(_drawn_inputs(seed))
    spreads = {}
    factors = {'norm1_g': 2.829,
     'b_merge_gate': 8.0,
     'gmlp_ln_g': 4.497,
     'gmlp_ln_b': 8.0,
     'b_spatial': 8.0,
     'attn_sink': 64.0,
     'norm2_g': 3.139,
     'k_norm_g_2': 2.892,
     'pre_norm_3': 8.0,
     'post_norm_3': 8.0,
     'even_conv_b_3': 64.0,
     'ret_gn_3': 200.0,
     'q_a_norm_3': 8.0,
     'kv_a_norm_3': 8.0}
    for name, (base, spread) in spreads.items():
        noise = np.random.default_rng([zlib.crc32(name.encode()), seed]).standard_normal(out[name].shape)
        drawn = base * np.exp(spread * noise) if base else spread * noise
        out[name] = __import__('jax').numpy.asarray(drawn.astype(out[name].dtype))
    for name, factor in factors.items():
        out[name] = (out[name] * factor).astype(out[name].dtype)
    return out
```

```python
from contextlib import ExitStack, contextmanager

import numpy as np

import concourse.bass as bass
from concourse import mybir

ALU = mybir.AluOpType
ACT = mybir.ActivationFunctionType
AX = mybir.AxisListType
F32 = mybir.dt.float32
I32 = mybir.dt.int32

P = 128
D = 1024
KC = D // P
SEQ = 512
CTX = 256
META = 16
TOK2 = SEQ + META
SLOTS = 4
SLOT_COLS = 512
BANKS = 8
EXPERTS, CAP, DFF = 16, 64, 2048
LB = 32
NBLK = 17
WIDE = NBLK * LB


def common_constants():
    p = np.arange(P)
    ident = np.eye(P)
    ones = np.ones((P, P))
    head = (p[:, None] // 64 == p[None] // 64)
    rot16, rot32 = np.zeros((P, P)), np.zeros((P, P))
    for half, m in ((16, rot16), (32, rot32)):
        for d in range(P):
            if d % (2 * half) < half:
                m[d + half, d] = -1.0
            else:
                m[d - half, d] = 1.0
    swap = (p[:, None] == (p[None] + 64) % P)
    return [("ident", ident), ("ones", ones), ("head", head), ("rot16", rot16), ("rot32", rot32), ("swap", swap),
            ("eye64", p[:, None] % 64 == p[None, :64])]


def grid_tables():
    d = np.arange(P) % 64
    freq = (10000.0 ** (-(np.arange(0, 32, 2, dtype=np.float32)) / 32)).astype(np.float32)
    t = np.arange(SEQ)
    pos = np.where((d < 32)[:, None], t[None] // 64, t[None] % 64).astype(np.float32)
    ang = pos * freq[d % 16][:, None]
    cos = np.concatenate([np.ones((P, META)), np.cos(ang)], 1)
    sin = np.concatenate([np.zeros((P, META)), np.sin(ang)], 1)
    return [("cos", cos), ("sin", sin)]


def first_constants():
    a = np.arange(P)
    neg = np.float32(-1e30)
    before = np.where(a[None] >= a[:, None], 0, neg)
    after = np.where(a[None] <= a[:, None], 0, neg)
    return [*grid_tables(), ("window", np.concatenate([before, np.zeros((P, P)), after], 1)),
            ("earlier", (a[:, None] < a[None])), ("iota", np.tile(np.arange(CAP), (P, 1)))]


def second_constants():
    p, f = np.arange(P)[:, None], np.arange(P)[None]
    same = p // LB == f // LB
    before = [p < f, p > f]
    out = [("strict", np.stack([same & o for o in before], 1)),
           ("upto", np.stack([same & (o | (p == f)) for o in before], 1))]
    b = 1
    while b < LB:
        pair = (p // (2 * b) == f // (2 * b)) & (p // b != f // b)
        out.append((f"level{b}", np.stack([pair & o for o in before], 1)))
        b *= 2
    return [(n, a.reshape(P, -1)) for n, a in out]


LOG_GAMMA = np.log1p(-np.exp2(-5.0 - np.arange(8)))


def third_constants():
    a = np.arange(P)
    neg = np.float32(-1e30)
    causal = np.concatenate([np.zeros((P, 3 * P)), np.where(a[None] <= a[:, None], 0, neg)], 1)
    rel = a[None] - a[:, None]
    intra = [np.where(rel >= 0, np.exp(g * np.maximum(rel, 0)), 0) / 8 for g in LOG_GAMMA]
    xi = [np.exp(LOG_GAMMA[2 * m + a // 64][:, None] * (a[None] + 1.0)) for m in range(4)]
    zeta = np.exp(LOG_GAMMA[None] * (P - 1.0 - a[:, None])) / 8
    gamma = np.exp(np.stack([LOG_GAMMA[2 * m + a // 64] for m in range(4)], 1) * P)
    inv = (10000.0 ** (-(np.arange(0, 64, 2, dtype=np.float32)) / 64)).astype(np.float32)
    return [("causal", causal), ("intra", np.concatenate(intra, 1)), ("xi", np.concatenate(xi, 1)),
            ("zeta", zeta), ("gamma", gamma), ("inv", inv[a % 32][:, None])]


def packed(parts):
    return np.ascontiguousarray(np.concatenate([np.asarray(a, np.float32) for _, a in parts], 1))


def columns(parts):
    at, where = 0, {}
    for name, a in parts:
        where[name] = (at, at + a.shape[1])
        at += a.shape[1]
    return where, at


PARAMS = {
    "p1": [("cc", 16), ("b_ada", 48), ("g1", 8), ("b_gate", 16), ("g2", 8), ("final", 8), ("sink", 16)],
    "p2": [("mix_g", 8), ("mu0", 16), ("mu1", 16), ("w0", 8), ("a0", 8), ("k_k", 4), ("k_a", 4), ("r_k", 4),
           ("lnx_g", 4), ("lnx_b", 4), ("qg", 1), ("kg", 1), ("ffn_g", 8), ("final", 8)],
    "p3": [("pre", 16), ("post", 16), ("conv_w", 24), ("conv_b", 8), ("gn", 8), ("qa", 3), ("kva", 2)],
}


class Count:

    def __init__(self, sem):
        self.sem, self.base, self.sent = sem, 0, 0

    def add(self, by):
        self.sent += by
        return by

    def at(self, n):
        return self.base + n

    def close(self):
        self.base += self.sent
        self.sent = 0


class Chain:

    def __init__(self, engine, count):
        self.engine, self.count = engine, count

    def __call__(self, ins):
        ins.then_inc(self.count.sem, self.count.add(1))
        self.engine.wait_ge(self.count.sem, self.count.at(self.count.sent))


class Core:

    def __init__(self, nc, ctx, dram):
        self.nc, self.dram = nc, dram
        sb = lambda name, shape, dt=F32: ctx.enter_context(nc.sbuf_tensor(name, shape, dt))
        self.ring = [sb(f"ring{i}", [P, KC, SLOT_COLS]) for i in range(SLOTS)]
        self.slab_cols = KC * TOK2
        self.slabs = sb("slabs", [P, 7 * self.slab_cols])
        self.slab = [self.slabs[:, i * self.slab_cols:(i + 1) * self.slab_cols] for i in range(7)]
        self.common = sb("common", [P, columns(common_constants())[1]])
        self.area = sb("area", [P, 2560])
        self.param = sb("param", [P, 120])
        self.mod = sb("mod", [P, 48, 2])
        self.gains = sb("gains", [P, 24])
        self.rstd = sb("rstd", [P, TOK2])
        self.small = sb("small", [P, 64])
        self.work = sb("work", [P, 2300])
        self.bank = [ctx.enter_context(nc.psum_tensor(f"bank{i}", [P, 512], F32)) for i in range(BANKS)]
        self.eps = {e: self.small[:, 60 + i:61 + i] for i, e in enumerate((1e-6, 64e-5))}
        self.counts = []

        def count(name):
            s = Count(ctx.enter_context(nc.semaphore(name)))
            self.counts.append(s)
            return s

        self.group_full = count("group_full")
        self.read_act, self.read_dve = count("read_by_act"), count("read_by_dve")
        self.dve_step, self.act_step, self.pool_step = count("dve_step"), count("act_step"), count("pool_step")
        self.a2p, self.v2p, self.p2v, self.p2a = count("act_to_pe"), count("dve_to_pe"), count("pe_to_dve"), count("pe_to_act")
        self.row_tile = count("row_tile_done")
        self.v2a, self.a2v = count("dve_to_act"), count("act_to_dve")
        self.loaded, self.stored = count("inputs_loaded"), count("outputs_stored")
        self.att = {k: count(f"att_{k}") for k in ("s_ready", "s_read", "m_ready", "e_ready", "n_ready", "t_ready", "t_read", "o_ready", "o_read")}
        self.moe = {k: count(f"moe_{k}") for k in ("fetched", "silu", "hidden", "turned", "turned_read", "result_read")}
        self.weight_in = [count(f"weight_in_slot{i}") for i in range(SLOTS)]
        self.weight_used = count("weight_used")
        self.tiles, self.named, self.issued, self.used = [], {}, 0, 0
        self.maps, self.third_cols = {}, {}

    def place(self, name, parts, tensor):
        self.maps[name] = (columns(parts)[0], tensor)

    def c(self, area, name, rows=slice(0, P)):
        where, tensor = self.maps[area]
        a, b = where[name]
        return tensor[rows, a:b]

    def col(self, name, i, rows=slice(0, P)):
        at = self.pcols[name] + i
        return self.param[rows, at:at + 1]

    def use_params(self, which):
        at, self.pcols = 0, {}
        for name, n in PARAMS[which]:
            self.pcols[name] = at
            at += n
        return at

    def plan(self, name, w, c0, c1, k0=0, k1=None, wide=SLOT_COLS):
        k1 = w.shape[0] if k1 is None else k1
        groups = []
        for c in range(c0, c1, wide):
            cw = min(wide, c1 - c)
            group = []
            for k in range(k0, k1, KC * P):
                rows = min(KC * P, k1 - k)
                src = w[k:k + rows, c:c + cw].rearrange("(k p) c -> p k c", p=P)
                group.append((len(self.tiles), (k - k0) // P, rows // P, cw))
                self.tiles.append((src, rows // P, cw))
            groups.append((c - c0, cw, group))
        self.named[name] = groups

    def issue_weights(self, engine, upto):
        upto = min(upto + SLOTS, len(self.tiles))
        while self.issued < upto:
            n = self.issued
            src, kc, cw = self.tiles[n]
            if n >= SLOTS:
                engine.wait_ge(self.weight_used.sem, n - SLOTS + 1)
            engine.dma_start(self.ring[n % SLOTS][:, 0:kc, 0:cw], src).then_inc(self.weight_in[n % SLOTS].sem, 16)
            self.issued += 1

    def weight_ready(self, engine, n):
        engine.wait_ge(self.weight_in[n % SLOTS].sem, 16 * (n // SLOTS + 1))

    @contextmanager
    def stage(self):
        with self.nc.Block() as block:
            yield block
        for s in self.counts:
            s.close()


def splits_of(tokens):
    return [(0, tokens)] if tokens <= SEQ else [(0, tokens // 2), (tokens // 2, tokens)]


def run_groups(core, name, groups_for):
    nc = core.nc
    work, count, full = [], {"act": 0, "dve": 0}, 0
    for c0, cw, group in core.named[name]:
        gs = []
        todo = list(groups_for(c0, cw))
        for i, g in enumerate(todo):
            count[g[3]] += 1
            last = i == len(todo) - 1
            full += not last
            gs.append((*g, count[g[3]], group[-1][0] + 1 if last else None, full))
        work.append((group, gs))
    flat = [g for _, gs in work for g in gs]
    reads = {"act": core.read_act, "dve": core.read_dve}
    with core.stage() as block:
        @block.tensor
        def _(pe):
            at = 0
            for group, gs in work:
                kcs = sum(kc for _, _, kc, _ in group)
                assert len(group) == 1 or len(gs) <= BANKS
                for n, kk0, kc, cw in group:
                    core.weight_ready(pe, n)
                    w = core.ring[n % SLOTS]
                    for i, (m, nn, operands, *_) in enumerate(gs):
                        out = core.bank[(at + i) % BANKS][0:m, 0:nn]
                        if kk0 == 0 and at + i >= BANKS:
                            old = flat[at + i - BANKS]
                            pe.wait_ge(reads[old[3]].sem, reads[old[3]].at(old[5]))
                        for k in range(kc):
                            lhsT, rhs = operands(w, k, kk0 + k)
                            mm = nc.tensor.matmul(out, lhsT, rhs, start=(kk0 + k == 0), stop=(kk0 + k == kcs - 1))
                        if kk0 + kc == kcs and i < len(gs) - 1:
                            mm.then_inc(core.group_full.sem, core.group_full.add(1))
                    mm.then_inc(core.weight_used.sem, 1)
                at += len(gs)

        @block.sync
        def _(sp):
            core.issue_weights(sp, core.named[name][-1][2][-1][0] + 1)

        def reader(which, engine):
            for i, g in enumerate(flat):
                if g[3] == which:
                    if g[6] is None:
                        engine.wait_ge(core.group_full.sem, core.group_full.at(g[7]))
                    else:
                        engine.wait_ge(core.weight_used.sem, g[6])
                    g[4](which, core.bank[i % BANKS][0:g[0], 0:g[1]]).then_inc(reads[which].sem, reads[which].add(1))

        @block.scalar
        def _(act):
            reader("act", act)

        @block.vector
        def _(dve):
            reader("dve", dve)


def dense(core, name, x, tokens, read, by="act", width=P):
    def groups_for(c0, cw):
        for c in range(0, cw, width):
            for t0, t1 in splits_of(tokens):
                m = min(width, cw - c)
                yield (m, t1 - t0,
                       lambda w, k, kk, c=c, m=m, t0=t0, t1=t1: (w[:, k, c:c + m], x[:, kk, t0:t1]),
                       by(((c0 + c) // width)) if callable(by) else by,
                       lambda eng, ps, ch=(c0 + c) // width, t0=t0, t1=t1: read(eng, ps, ch, t0, t1))
    run_groups(core, name, groups_for)


def token_groups(x, tokens, c, cw, read, by, c0=0):
    for t in range(0, tokens, P):
        m = min(P, tokens - t)
        yield (m, cw, lambda w, k, kk, t=t, m=m: (x[:, kk, t:t + m], w[:, k, c:c + cw]), by,
               lambda eng, ps, t=t // P: read(eng, ps, t, c0))


def copy_to(core, dst):
    def read(eng, ps, ch, t0, t1):
        to = dst[0:ps.shape[0], ch, t0:t1]
        if eng == "act":
            return core.nc.scalar.copy(to, ps)
        return core.nc.vector.tensor_copy(to, ps)
    return read


def root(core, out, sums, n, eps):
    return core.nc.scalar.activation(out, sums, ACT.Sqrt, scale=1.0 / n, bias=core.eps[eps][0:out.shape[0]])


def rms_norm(core, x, kc, tokens, squares, out, gain, n, eps=1e-6, shift=None, post=None):
    nc, ones, sp_ = core.nc, core.c("common", "ones"), splits_of(tokens)
    rstd = core.rstd[:, 0:tokens]
    with core.stage() as block:
        @block.scalar
        def _(act):
            for k in range(kc):
                nc.scalar.activation(squares[:, k, 0:tokens], x[:, k, 0:tokens], ACT.Square).then_inc(core.a2p.sem, core.a2p.add(1))
            act.wait_ge(core.p2a.sem, core.p2a.at(1))
            for s, (a, b) in enumerate(sp_):
                root(core, rstd[:, a:b], core.bank[s][:, 0:b - a], n, eps).then_inc(core.a2v.sem, core.a2v.add(1))
            if shift is not None:
                for k in range(kc):
                    act.wait_ge(core.v2a.sem, core.v2a.at(k + 1))
                    nc.scalar.activation(out[:, k, 0:tokens], out[:, k, 0:tokens], ACT.Identity, bias=shift(k))

        @block.tensor
        def _(pe):
            for k in range(kc):
                pe.wait_ge(core.a2p.sem, core.a2p.at(k + 1))
                for s, (a, b) in enumerate(sp_):
                    mm = nc.tensor.matmul(core.bank[s][:, 0:b - a], ones, squares[:, k, a:b], start=k == 0, stop=k == kc - 1)
            mm.then_inc(core.p2a.sem, core.p2a.add(1))

        @block.vector
        def _(dve):
            step = Chain(dve, core.dve_step)
            dve.wait_ge(core.a2v.sem, core.a2v.at(len(sp_)))
            step(nc.vector.reciprocal(rstd, rstd))
            for k in range(kc):
                nc.vector.scalar_tensor_tensor(out=out[:, k, 0:tokens], in0=x[:, k, 0:tokens], scalar=gain(k),
                                                            in1=rstd, op0=ALU.mult, op1=ALU.mult).then_inc(core.v2a.sem, core.v2a.add(1))
                if post is not None:
                    dve.wait_ge(core.v2a.sem, core.v2a.at(core.v2a.sent))
                    post(k)


def head_norm(core, x, chunks, tokens, squares, lhs, n, eps, gain, out, mean=False):
    nc, sp_ = core.nc, splits_of(tokens)
    per = len(sp_)
    roots = [core.work[:, 512 * i:512 * i + 512] for i in range(2)]
    with core.stage() as block:
        @block.scalar
        def _(act):
            for c in range(chunks):
                nc.scalar.activation(squares[:, c, 0:tokens], x[:, c, 0:tokens], ACT.Square).then_inc(core.a2p.sem, core.a2p.add(1))
            for g in range(chunks * per):
                a, b = sp_[g % per]
                act.wait_ge(core.p2a.sem, core.p2a.at(g + 1))
                if g >= 2:
                    act.wait_ge(core.v2p.sem, core.v2p.at(g - 1))
                root(core, roots[g % 2][:, 0:b - a], core.bank[g % BANKS][:, 0:b - a], n, eps).then_inc(core.a2v.sem, core.a2v.add(1))

        @block.tensor
        def _(pe):
            for c in range(chunks):
                pe.wait_ge(core.a2p.sem, core.a2p.at(c + 1))
                for s, (a, b) in enumerate(sp_):
                    g = c * per + s
                    if g >= BANKS:
                        pe.wait_ge(core.v2p.sem, core.v2p.at(g - BANKS + 1))
                    nc.tensor.matmul(core.bank[g % BANKS][:, 0:b - a], lhs, squares[:, c, a:b], start=True, stop=True).then_inc(core.p2a.sem, core.p2a.add(1))

        @block.vector
        def _(dve):
            step = Chain(dve, core.dve_step)
            for c in range(chunks):
                for s, (a, b) in enumerate(sp_):
                    g = c * per + s
                    r = roots[g % 2][:, 0:b - a]
                    dve.wait_ge(core.a2v.sem, core.a2v.at(g + 1))
                    step(nc.vector.reciprocal(r, r))
                    ins = nc.vector.scalar_tensor_tensor(out=out[:, c, a:b], in0=x[:, c, a:b], scalar=gain(c),
                                                         in1=r, op0=ALU.mult, op1=ALU.mult)
                    ins.then_inc(core.v2p.sem, core.v2p.add(1))
                    dve.wait_ge(core.v2p.sem, core.v2p.at(core.v2p.sent))


def rope(core, x, chunks, tokens, rot, cos, sin, rows=P):
    nc, sp_ = core.nc, splits_of(tokens)
    per = len(sp_)
    tmp = core.work[:, 0:2 * 512].rearrange("p (b n) -> p b n", b=2)
    with core.stage() as block:
        @block.tensor
        def _(pe):
            for c in range(chunks):
                for s, (a, b) in enumerate(sp_):
                    g = c * per + s
                    if g >= BANKS:
                        pe.wait_ge(core.v2p.sem, core.v2p.at(g - BANKS + 1))
                    nc.tensor.matmul(core.bank[g % BANKS][0:rows, 0:b - a], rot, x[0:rows, c, a:b], start=True, stop=True).then_inc(core.p2v.sem, core.p2v.add(1))

        @block.vector
        def _(dve):
            step = Chain(dve, core.dve_step)
            for c in range(chunks):
                for s, (a, b) in enumerate(sp_):
                    g = c * per + s
                    t = tmp[0:rows, g % 2, 0:b - a]
                    dve.wait_ge(core.p2v.sem, core.p2v.at(g + 1))
                    nc.vector.tensor_tensor(t, core.bank[g % BANKS][0:rows, 0:b - a], sin[0:rows, a:b], ALU.mult).then_inc(core.v2p.sem, core.v2p.add(1))
                    dve.wait_ge(core.v2p.sem, core.v2p.at(core.v2p.sent))
                    step(nc.vector.tensor_tensor(x[0:rows, c, a:b], x[0:rows, c, a:b], cos[0:rows, a:b], ALU.mult))
                    step(nc.vector.tensor_tensor(x[0:rows, c, a:b], x[0:rows, c, a:b], t, ALU.add))


def exchange_halves(core, x, out, chunks, tokens):
    nc, sp_ = core.nc, splits_of(tokens)
    with core.stage() as block:
        @block.tensor
        def _(pe):
            for c in range(chunks):
                for s, (a, b) in enumerate(sp_):
                    nc.tensor.matmul(core.bank[c * len(sp_) + s][:, 0:b - a], core.c("common", "swap"), x[:, c, a:b],
                                                  start=True, stop=True).then_inc(core.p2v.sem, core.p2v.add(1))

        @block.vector
        def _(dve):
            for c in range(chunks):
                for s, (a, b) in enumerate(sp_):
                    g = c * len(sp_) + s
                    dve.wait_ge(core.p2v.sem, core.p2v.at(g + 1))
                    nc.vector.tensor_copy(out[:, c, a:b], core.bank[g][:, 0:b - a])


def load(core, pairs):
    with core.stage() as block:
        @block.sync
        def _(sp):
            for dst, src in pairs:
                sp.dma_start(dst, src).then_inc(core.loaded.sem, core.loaded.add(16))
            sp.wait_ge(core.loaded.sem, core.loaded.at(16 * len(pairs)))


def attention(core, units, scale, scores_at, probs_at, wide=640):
    nc, ident = core.nc, core.c("common", "ident")
    n = len(units)
    row = [scores_at[:, wide * i:wide * (i + 1)] for i in range(3)]
    prob = [probs_at[:, wide * i:wide * (i + 1)] for i in range(2)]
    stat = [core.small[:, 8 * i:8 * i + 8] for i in range(3)]
    s_ready, s_read, m_ready, e_ready, n_ready, t_ready, t_read, o_ready, o_read = (
        core.att[k] for k in ("s_ready", "s_read", "m_ready", "e_ready", "n_ready", "t_ready", "t_read", "o_ready", "o_read"))
    with core.stage() as block:
        @block.tensor
        def _(pe):
            def scores(i):
                m, segs = units[i][0], units[i][1]
                if i >= 2:
                    pe.wait_ge(s_read.sem, s_read.at(i - 1))
                for s, (products, cols, _) in enumerate(segs):
                    for j, (lhsT, rhs) in enumerate(products):
                        mm = nc.tensor.matmul(core.bank[2 * (i % 2) + s][0:m, 0:cols], lhsT, rhs, start=j == 0,
                                              stop=j == len(products) - 1)
                mm.then_inc(s_ready.sem, s_ready.add(1))

            def turn(i):
                m, blocks = units[i][0], units[i][2]
                pe.wait_ge(n_ready.sem, n_ready.at(i + 1))
                if i >= 1:
                    pe.wait_ge(t_read.sem, t_read.at(i))
                for b, (_, kp) in enumerate(blocks):
                    out = core.bank[4 + b // 4][0:kp, (b % 4) * P:(b % 4) * P + m]
                    mm = nc.tensor.transpose(out, row[i % 3][0:m, b * P:b * P + kp], ident[0:m, 0:m])
                mm.then_inc(t_ready.sem, t_ready.add(1))

            def values(i):
                m, _, blocks, dv, po = units[i][:5]
                pe.wait_ge(t_read.sem, t_read.at(i + 1))
                if i >= 2:
                    pe.wait_ge(o_read.sem, o_read.at(i - 1))
                for b, (v, kp) in enumerate(blocks):
                    mm = nc.tensor.matmul(core.bank[6 + i % 2][po:po + dv, 0:m], v, prob[i % 2][0:kp, b * P:b * P + m],
                                          start=b == 0, stop=b == len(blocks) - 1)
                mm.then_inc(o_ready.sem, o_ready.add(1))

            scores(0)
            scores(1)
            for i in range(n):
                if i + 2 < n:
                    scores(i + 2)
                turn(i)
                if i >= 1:
                    values(i - 1)
            values(n - 1)

        @block.vector
        def _(dve):
            step = Chain(dve, core.dve_step)

            def take(i):
                m, segs, _, _, _, _, sink = units[i]
                dve.wait_ge(s_ready.sem, s_ready.at(i + 1))
                if i >= 3:
                    dve.wait_ge(t_ready.sem, t_ready.at(i - 2))
                at = 0
                for s, (_, cols, mask) in enumerate(segs):
                    to, ps = row[i % 3][0:m, at:at + cols], core.bank[2 * (i % 2) + s][0:m, 0:cols]
                    ins = nc.vector.tensor_tensor(to, ps, mask, ALU.add) if mask is not None else nc.vector.tensor_copy(to, ps)
                    at += cols
                ins.then_inc(s_read.sem, s_read.add(1))
                dve.wait_ge(s_read.sem, s_read.at(s_read.sent))
                st = stat[i % 3]
                step(nc.vector.reduce_max(st[0:m, 0:1], row[i % 3][0:m, 0:at], AX.X))
                if sink is None:
                    nc.vector.tensor_scalar(st[0:m, 1:2], st[0:m, 0:1], -scale, None, ALU.mult).then_inc(m_ready.sem, m_ready.add(1))
                else:
                    step(nc.vector.tensor_scalar(st[0:m, 2:3], st[0:m, 0:1], scale, sink[0:m], ALU.mult, ALU.max))
                    nc.vector.tensor_scalar(st[0:m, 1:2], st[0:m, 2:3], -1.0, None, ALU.mult).then_inc(m_ready.sem, m_ready.add(1))

            def normalise(i):
                m, segs, _, _, _, _, sink = units[i]
                cols = sum(s[1] for s in segs)
                st = stat[i % 3]
                dve.wait_ge(e_ready.sem, e_ready.at(i + 1))
                if sink is not None:
                    step(nc.vector.tensor_tensor(st[0:m, 3:4], st[0:m, 3:4], st[0:m, 4:5], ALU.add))
                step(nc.vector.reciprocal(st[0:m, 5:6], st[0:m, 3:4]))
                nc.vector.tensor_scalar(row[i % 3][0:m, 0:cols], row[i % 3][0:m, 0:cols], st[0:m, 5:6], None, ALU.mult).then_inc(n_ready.sem, n_ready.add(1))

            def keep(i):
                m, _, _, dv, po, dest, _ = units[i]
                dve.wait_ge(o_ready.sem, o_ready.at(i + 1))
                nc.vector.tensor_copy(dest, core.bank[6 + i % 2][po:po + dv, 0:m]).then_inc(o_read.sem, o_read.add(1))

            take(0)
            take(1)
            normalise(0)
            for i in range(n):
                if i + 2 < n:
                    take(i + 2)
                if i + 1 < n:
                    normalise(i + 1)
                if i >= 2:
                    keep(i - 2)
            keep(n - 2)
            keep(n - 1)

        @block.scalar
        def _(act):
            def exponentials(i):
                m, segs, _, _, _, _, sink = units[i]
                cols = sum(s[1] for s in segs)
                st, r = stat[i % 3], row[i % 3]
                act.wait_ge(m_ready.sem, m_ready.at(i + 1))
                if sink is not None:
                    nc.scalar.activation(st[0:m, 4:5], sink[0:m], ACT.Exp, bias=st[0:m, 1:2])
                nc.scalar.activation(r[0:m, 0:cols], r[0:m, 0:cols], ACT.Exp, bias=st[0:m, 1:2], scale=scale,
                                                 accum_out=st[0:m, 3:4]).then_inc(e_ready.sem, e_ready.add(1))

            def copy_turned(i):
                m, blocks = units[i][0], units[i][2]
                act.wait_ge(t_ready.sem, t_ready.at(i + 1))
                if i >= 2:
                    act.wait_ge(o_ready.sem, o_ready.at(i - 1))
                for b, (_, kp) in enumerate(blocks):
                    if b == 0 or b == 4 or kp < P:
                        run = 1
                        while kp == P and b + run < min(len(blocks), 4 * (b // 4 + 1)) and blocks[b + run][1] == P and m == P:
                            run += 1
                        lo = (b % 4) * P
                        ins = nc.scalar.copy(prob[i % 2][0:kp, b * P:(b + run - 1) * P + m], core.bank[4 + b // 4][0:kp, lo:lo + (run - 1) * P + m])
                    elif m < P:
                        lo = (b % 4) * P
                        ins = nc.scalar.copy(prob[i % 2][0:kp, b * P:b * P + m], core.bank[4 + b // 4][0:kp, lo:lo + m])
                ins.then_inc(t_read.sem, t_read.add(1))

            exponentials(0)
            for i in range(n):
                if i + 1 < n:
                    exponentials(i + 1)
                copy_turned(i)


def first_block(core):
    nc, dram = core.nc, core.dram
    X, H, S2, S3, S4, S5, S6 = [s[:, :].rearrange("p (k t) -> p k t", k=KC) for s in core.slab]
    x, h = X[:, :, META:], H[:, :, 0:SEQ]
    flat = [s[:, :] for s in core.slab]
    ones, ident = core.c("common", "ones"), core.c("common", "ident")
    core.use_params("p1")
    cols = lambda name, i0, i1: core.param[:, core.pcols[name] + i0:core.pcols[name] + i1]

    consts = first_constants()
    where, width = columns(consts)
    core.place("first", consts, core.area)
    grid = grid_tables()
    ctx_x = S2[:, :, 0:CTX]
    with core.stage() as block:
        @block.sync
        def _(sp):
            pairs = [(core.common[:, :], dram["common"]), (core.area[:, 0:width], dram["first"]), (core.param[:, :], dram["p1"]),
                     (x, dram["x"]), (ctx_x, dram["ctx"])]
            for dst, src in pairs:
                sp.dma_start(dst, src).then_inc(core.loaded.sem, core.loaded.add(16))
            core.issue_weights(sp, 0)
            sp.wait_ge(core.loaded.sem, core.loaded.at(16 * len(pairs)))

        @block.vector
        def _(dve):
            for e, at in core.eps.items():
                nc.vector.memset(at, e)

    cc = core.small[:, 0:16]
    with core.stage() as block:
        @block.scalar
        def _(act):
            nc.scalar.activation(cc, cols("cc", 0, 16), ACT.Silu)
    silu_c = cc.rearrange("p (k j) -> p k j", j=2)
    bada = cols("b_ada", 0, 48)
    dense(core, "ada", silu_c, 2, lambda eng, ps, ch, t0, t1: nc.vector.tensor_scalar(
        core.mod[:, ch, :], ps, bada[:, ch:ch + 1], None, ALU.add), by="dve")
    with core.stage() as block:
        @block.vector
        def _(dve):
            for at, j, chunk, gain in ((0, 0, 8, "g1"), (8, 1, 8, "g1"), (16, 0, 32, "g2")):
                nc.vector.scalar_tensor_tensor(out=core.gains[:, at:at + 8], in0=core.mod[:, chunk:chunk + 8, j], scalar=1.0,
                                               in1=cols(gain, 0, 8), op0=ALU.add, op1=ALU.mult)
    gain = lambda at: (lambda k: core.gains[:, at + k:at + k + 1])
    shift = lambda chunk, j: (lambda k: core.mod[:, chunk + k, j:j + 1])

    hc = S2[:, :, 264:264 + CTX]
    rms_norm(core, x, KC, SEQ, S3, h, gain(0), D, shift=shift(0, 0))
    rms_norm(core, ctx_x, KC, CTX, S3, hc, gain(8), D, shift=shift(0, 1))

    kT = S3[:, 0:2, 0:SEQ]
    kS = S3[:, 2:4, 0:SEQ]
    kcT, kcS = S3[:, 4:6, 0:CTX], S3[:, 6:8, 0:CTX]
    v = S3[:, 4:6, 264:264 + CTX]
    vtok = flat[4][:, 0:4 * CTX].rearrange("p (t c) -> p t c", t=4)
    vctx = flat[4][:, 4 * CTX:6 * CTX].rearrange("p (t c) -> p t c", t=2)

    def kv_groups(c0, cw):
        for c in range(2):
            for src, n, dst in ((h, SEQ, kT), (hc, CTX, kcT)):
                yield (P, n, lambda w, k, kk, c=c, src=src, n=n: (w[:, k, c * P:(c + 1) * P], src[:, kk, 0:n]), "act",
                       lambda eng, ps, c=c, n=n, dst=dst: nc.scalar.copy(dst[:, c, 0:n], ps))
        for src, n, dst in ((h, SEQ, vtok), (hc, CTX, vctx)):
            yield from token_groups(src, n, 2 * P, CTX, lambda eng, ps, t, c0, dst=dst: nc.vector.tensor_copy(dst[:, t, :], ps), "dve")
    run_groups(core, "kv", kv_groups)

    q = S5[:, :, 0:SEQ]
    dense(core, "q", h, SEQ, copy_to(core, q))
    cos, sin = core.c("first", "cos")[:, META:], core.c("first", "sin")[:, META:]
    rope(core, q, KC, SEQ, core.c("common", "rot16"), cos, sin)
    rope(core, kT, 2, SEQ, core.c("common", "rot16"), cos, sin)
    exchange_halves(core, kT, kS, 2, SEQ)
    exchange_halves(core, kcT, kcS, 2, CTX)

    yb = S6[:, :, 0:SEQ]
    window = core.c("first", "window")
    units = []
    for head in range(16):
        kv, po = head // 4, 64 * (head % 2)
        same = head % 2 == kv % 2
        keys, ckeys = (kT, kcT) if same else (kS, kcS)
        rows = slice(po, po + 64)
        for n in range(4):
            lo, hi = max(n - 1, 0), min(n + 1, 3)
            query = q[rows, head // 2, n * P:(n + 1) * P]
            segs = [([(query, keys[rows, kv // 2, lo * P:(hi + 1) * P])], (hi + 1 - lo) * P, window[:, (lo - n + 1) * P:(hi - n + 2) * P]),
                    ([(query, ckeys[rows, kv // 2, :])], CTX, None)]
            blocks = [(vtok[:, b, kv * 64:kv * 64 + 64], P) for b in range(lo, hi + 1)] + \
                     [(vctx[:, b, kv * 64:kv * 64 + 64], P) for b in range(2)]
            units.append((P, segs, blocks, 64, po, yb[rows, head // 2, n * P:(n + 1) * P], core.col("sink", head)))
    attention(core, units, 64 ** -0.5, flat[2], flat[4][:, 6 * CTX:6 * CTX + 1280])

    va = flat[2][:, 0:4 * D].rearrange("p (t c) -> p t c", t=4)
    u = S3[:, :, 0:SEQ]
    tables = flat[4]
    gB, bB, bsB = tables[:, 0:D], tables[:, D:2 * D], tables[:, 2 * D:3 * D]
    scratch = tables[:, 3 * D:4 * D]
    ws = flat[5][:, 0:D].rearrange("p (g q) -> p g q", g=8)
    load(core, [(gB, dram["gmlp_ln_g"].partition_broadcast(P)), (bB, dram["gmlp_ln_b"].partition_broadcast(P)),
                (bsB, dram["b_spatial"].partition_broadcast(P)), (ws, dram["w_spatial"])])
    sums = core.small[:, 16:24]
    run_groups(core, "va", lambda c0, cw: token_groups(h, SEQ, 0, cw, lambda eng, ps, t, c0: nc.scalar.activation(
        va[:, t, c0:c0 + SLOT_COLS], ps, ACT.Gelu_apprx_tanh,
        accum_out=sums[:, 2 * t + c0 // SLOT_COLS:2 * t + c0 // SLOT_COLS + 1]), "act", c0))
    dense(core, "u", h, SEQ, lambda eng, ps, ch, t0, t1: nc.scalar.activation(u[:, ch, t0:t1], ps, ACT.Gelu_apprx_tanh))
    mean, var = core.small[:, 24:28], core.small[:, 28:32]
    with core.stage() as block:
        @block.vector
        def _(dve):
            step = Chain(dve, core.dve_step)
            s3 = sums.rearrange("p (t j) -> p t j", j=2)
            step(nc.vector.tensor_tensor(mean, s3[:, :, 0], s3[:, :, 1], ALU.add))
            step(nc.vector.tensor_scalar(mean, mean, 1.0 / D, None, ALU.mult))
            for t in range(4):
                nc.vector.tensor_scalar(va[:, t, :], va[:, t, :], mean[:, t:t + 1], None, ALU.subtract).then_inc(core.v2a.sem, core.v2a.add(1))
            dve.wait_ge(core.a2v.sem, core.a2v.at(5))
            step(nc.vector.reciprocal(var, var))
            for t in range(4):
                step(nc.vector.scalar_tensor_tensor(out=va[:, t, :], in0=va[:, t, :], scalar=var[:, t:t + 1], in1=gB,
                                                    op0=ALU.mult, op1=ALU.mult))
                nc.vector.tensor_tensor(va[:, t, :], va[:, t, :], bB, ALU.add).then_inc(core.v2p.sem, core.v2p.add(1))
            for g in range(8):
                dve.wait_ge(core.p2v.sem, core.p2v.at(g + 1))
                mixed = scratch[:, 0:SEQ].rearrange("p (n q) -> p n q", n=4)
                step(nc.vector.tensor_tensor(mixed, core.bank[g][:, :].rearrange("p (n q) -> p n q", n=4),
                                             bsB[:, g * P:(g + 1) * P].unsqueeze(1).broadcast_to([P, 4, P]), ALU.add))
                step(nc.vector.tensor_tensor(u[:, g, :], u[:, g, :], scratch[:, 0:SEQ], ALU.mult))

        @block.scalar
        def _(act):
            for t in range(4):
                act.wait_ge(core.v2a.sem, core.v2a.at(t + 1))
                nc.scalar.activation(flat[5][:, D:2 * D], va[:, t, :], ACT.Square, accum_out=var[:, t:t + 1]).then_inc(core.a2v.sem, core.a2v.add(1))
                act.wait_ge(core.a2v.sem, core.a2v.at(core.a2v.sent))
            root(core, var, var, D, 1e-6).then_inc(core.a2v.sem, core.a2v.add(1))

        @block.tensor
        def _(pe):
            pe.wait_ge(core.v2p.sem, core.v2p.at(4))
            for g in range(8):
                for n in range(4):
                    mm = nc.tensor.matmul(core.bank[g][:, n * P:(n + 1) * P], va[:, n, g * P:(g + 1) * P], ws[:, g, :], start=True, stop=True)
                mm.then_inc(core.p2v.sem, core.p2v.add(1))

    bg = cols("b_gate", 0, 16)
    merge_branches(core, h, SEQ, [("ga", "pa", u, 0), ("gb", "pb", yb, 8)], S4[:, :, 0:SEQ], S5[:, :, 0:SEQ],
                   lambda i: bg[:, i:i + 1])
    dense(core, "wo", S4[:, :, 0:SEQ], SEQ, lambda eng, ps, ch, t0, t1: nc.vector.scalar_tensor_tensor(
        out=x[:, ch, t0:t1], in0=ps, scalar=core.mod[:, 16 + ch, 0:1], in1=x[:, ch, t0:t1], op0=ALU.mult, op1=ALU.add), by="dve")
    rms_norm(core, x, KC, SEQ, S2, h, gain(16), D, shift=shift(24, 0))
    expert_choice(core, x, h)
    rms_norm(core, x, KC, SEQ, S2, x, lambda k: core.col("final", k), D)


def merge_branches(core, h, tokens, branches, merged, gate, bias):
    nc = core.nc
    for i, (gname, pname, y, g0) in enumerate(branches):
        dense(core, gname, h, tokens, lambda eng, ps, ch, t0, t1: nc.scalar.activation(
            gate[:, ch, t0:t1], ps, ACT.Sigmoid, bias=0.0 if bias is None else bias(g0 + ch)))

        def join(eng, ps, ch, t0, t1):
            if i == 0:
                return nc.vector.tensor_tensor(merged[:, ch, t0:t1], ps, gate[:, ch, t0:t1], ALU.mult)
            nc.vector.tensor_tensor(gate[:, ch, t0:t1], ps, gate[:, ch, t0:t1], ALU.mult).then_inc(core.dve_step.sem, core.dve_step.add(1))
            nc.vector.wait_ge(core.dve_step.sem, core.dve_step.at(core.dve_step.sent))
            return nc.vector.tensor_tensor(merged[:, ch, t0:t1], merged[:, ch, t0:t1], gate[:, ch, t0:t1], ALU.add)
        dense(core, pname, y, tokens, join, by="dve")


def expert_choice(core, x, h):
    nc, dram = core.nc, core.dram
    flat = [s[:, :] for s in core.slab]
    ones, ident = core.c("common", "ones"), core.c("common", "ident")
    earlier, iota = core.c("first", "earlier"), core.c("first", "iota")
    htok = flat[2][:, 0:4 * D].rearrange("p (t c) -> p t c", t=4)
    wr = core.work[:, 0:P].rearrange("p (k e) -> p k e", k=KC)
    aff = core.work[:, 128:192].rearrange("p (t e) -> p t e", t=4)
    chosen = core.work[:, 192:256].rearrange("p (t e) -> p t e", t=4)
    rank = core.work[:, 256:320].rearrange("p (t e) -> p t e", t=4)
    tmax = core.work[:, 320:336]
    by_expert = core.work[0:EXPERTS, 512:1024]
    left = core.work[0:EXPERTS, 1024:1536]
    best = core.work[0:EXPERTS, 1536:1544]
    load(core, [(wr, dram["w_router"].rearrange("(k p) e -> p k e", p=P))])
    lb = core.bank[0][:, 0:64].rearrange("p (t e) -> p t e", t=4)
    with core.stage() as block:
        @block.tensor
        def _(pe):
            for t in range(4):
                for k in range(KC):
                    mm = nc.tensor.matmul(lb[:, t, :], h[:, k, t * P:(t + 1) * P], wr[:, k, :], start=k == 0, stop=k == KC - 1)
            mm.then_inc(core.p2v.sem, core.p2v.add(1))
            for t in range(4):
                for half in range(2):
                    b = 1 + (2 * t + half) % 4
                    if 2 * t + half >= 4:
                        pe.wait_ge(core.a2p.sem, core.a2p.at(2 * t + half - 3))
                    for c in range(4):
                        mm = nc.tensor.transpose(core.bank[b][:, c * P:(c + 1) * P], h[:, 4 * half + c, t * P:(t + 1) * P], ident)
                    mm.then_inc(core.p2a.sem, core.p2a.add(1))
            pe.wait_ge(core.v2p.sem, core.v2p.at(1))
            for t in range(4):
                mm = nc.tensor.transpose(core.bank[5][0:EXPERTS, t * P:(t + 1) * P], aff[:, t, :], ident)
            mm.then_inc(core.p2v.sem, core.p2v.add(1))
            pe.wait_ge(core.v2p.sem, core.v2p.at(2))
            for t in range(4):
                mm = nc.tensor.transpose(core.bank[6][:, t * EXPERTS:(t + 1) * EXPERTS], by_expert[:, t * P:(t + 1) * P], ident[0:EXPERTS, 0:EXPERTS])
            mm.then_inc(core.p2v.sem, core.p2v.add(1))
            pe.wait_ge(core.v2p.sem, core.v2p.at(3))
            for t in range(4):
                for s in range(t + 1):
                    mm = nc.tensor.matmul(core.bank[7][:, t * EXPERTS:(t + 1) * EXPERTS], earlier if s == t else ones, chosen[:, s, :],
                                          start=s == 0, stop=s == t)
            mm.then_inc(core.p2v.sem, core.p2v.add(1))

        @block.scalar
        def _(act):
            for g in range(8):
                act.wait_ge(core.p2a.sem, core.p2a.at(g + 1))
                nc.scalar.copy(htok[:, g // 2, (g % 2) * 512:(g % 2) * 512 + 512], core.bank[1 + g % 4][:, :]).then_inc(core.a2p.sem, core.a2p.add(1))
            act.wait_ge(core.v2a.sem, core.v2a.at(1))
            nc.scalar.activation(aff, aff, ACT.Exp).then_inc(core.a2v.sem, core.a2v.add(1))

        @block.vector
        def _(dve):
            step = Chain(dve, core.dve_step)
            dve.wait_ge(core.p2v.sem, core.p2v.at(1))
            step(nc.vector.tensor_reduce(tmax[:, 0:4], lb, AX.X, ALU.max))
            nc.vector.tensor_tensor(aff, lb, tmax[:, 0:4].unsqueeze(2).broadcast_to([P, 4, EXPERTS]), ALU.subtract).then_inc(core.v2a.sem, core.v2a.add(1))
            dve.wait_ge(core.a2v.sem, core.a2v.at(1))
            step(nc.vector.tensor_reduce(tmax[:, 4:8], aff, AX.X, ALU.add))
            step(nc.vector.reciprocal(tmax[:, 8:12], tmax[:, 4:8]))
            nc.vector.tensor_tensor(aff, aff, tmax[:, 8:12].unsqueeze(2).broadcast_to([P, 4, EXPERTS]), ALU.mult).then_inc(core.v2p.sem, core.v2p.add(1))
            dve.wait_ge(core.p2v.sem, core.p2v.at(2))
            step(nc.vector.tensor_copy(left, core.bank[5][0:EXPERTS, :]))
            for r in range(CAP // 8):
                step(nc.vector.max(best, left))
                step(nc.vector.match_replace(left, best, left, -1.0))
            nc.vector.tensor_scalar(by_expert, left, 0.0, None, ALU.is_lt).then_inc(core.v2p.sem, core.v2p.add(1))
            dve.wait_ge(core.p2v.sem, core.p2v.at(3))
            nc.vector.tensor_copy(chosen, core.bank[6][:, 0:64].rearrange("p (t e) -> p t e", t=4)).then_inc(core.v2p.sem, core.v2p.add(1))
            dve.wait_ge(core.v2p.sem, core.v2p.at(3))
            dve.wait_ge(core.p2v.sem, core.p2v.at(4))
            step(nc.vector.tensor_scalar(rank, core.bank[7][:, 0:64].rearrange("p (t e) -> p t e", t=4), 1.0, None, ALU.add))
            step(nc.vector.tensor_tensor(rank, rank, chosen, ALU.mult))
            step(nc.vector.tensor_scalar(rank, rank, -1.0, None, ALU.add))

    onehot = flat[3][:, 0:4 * D].rearrange("p (t e s) -> p t e s", t=4, e=EXPERTS)
    xe = core.slabs[:, 4 * core.slab_cols:4 * core.slab_cols + 8 * D].rearrange("p (k s) -> p k s", k=KC)
    with core.stage() as block:
        @block.vector
        def _(dve):
            for t in range(4):
                nc.vector.tensor_tensor(onehot[:, t], iota.unsqueeze(1).broadcast_to([P, EXPERTS, CAP]),
                                                     rank[:, t, :].unsqueeze(2).broadcast_to([P, EXPERTS, CAP]), ALU.is_equal).then_inc(core.v2p.sem, core.v2p.add(1))
            dve.wait_ge(core.p2a.sem, core.p2a.at(16))
            for t in range(4):
                nc.vector.tensor_tensor(onehot[:, t], onehot[:, t], aff[:, t, :].unsqueeze(2).broadcast_to([P, EXPERTS, CAP]), ALU.mult).then_inc(core.v2p.sem, core.v2p.add(1))

        @block.tensor
        def _(pe):
            for t in range(4):
                pe.wait_ge(core.v2p.sem, core.v2p.at(t + 1))
            g = 0
            for c in range(KC):
                for half in range(2):
                    if g >= BANKS:
                        pe.wait_ge(core.a2p.sem, core.a2p.at(g - BANKS + 1))
                    for t in range(4):
                        mm = nc.tensor.matmul(core.bank[g % BANKS][:, :], htok[:, t, c * P:(c + 1) * P],
                                              flat[3][:, t * D + half * 512:t * D + half * 512 + 512], start=t == 0, stop=t == 3)
                    mm.then_inc(core.p2a.sem, core.p2a.add(1))
                    g += 1
            pe.wait_ge(core.v2p.sem, core.v2p.at(8))
            for pair in range(8):
                if g >= BANKS:
                    pe.wait_ge(core.a2p.sem, core.a2p.at(g - BANKS + 1))
                for t in range(4):
                    mm = nc.tensor.transpose(core.bank[g % BANKS][:, t * P:(t + 1) * P], flat[3][:, t * D + pair * P:t * D + (pair + 1) * P], ident)
                mm.then_inc(core.p2a.sem, core.p2a.add(1))
                g += 1

        @block.scalar
        def _(act):
            for g in range(16):
                act.wait_ge(core.p2a.sem, core.p2a.at(g + 1))
                nc.scalar.copy(xe[:, g // 2, (g % 2) * 512:(g % 2 + 1) * 512], core.bank[g % BANKS][:, :]).then_inc(core.a2p.sem, core.a2p.add(1))
            for pair in range(8):
                act.wait_ge(core.p2a.sem, core.p2a.at(16 + pair + 1))
                nc.scalar.copy(flat[2][:, pair * 512:(pair + 1) * 512], core.bank[(16 + pair) % BANKS][:, :]).then_inc(core.a2p.sem, core.a2p.add(1))

    y = [flat[3][:, 0:4 * D].rearrange("p (e c) -> p e c", e=8), flat[1][:, 0:4 * D].rearrange("p (e c) -> p e c", e=8)]
    experts(core, xe, y)

    with core.stage() as block:
        @block.tensor
        def _(pe):
            for ch in range(KC):
                for pair in range(8):
                    mm = nc.tensor.matmul(core.bank[ch][:, :], y[ch // 4][:, pair, (ch % 4) * P:(ch % 4 + 1) * P],
                                          flat[2][:, pair * 512:(pair + 1) * 512], start=pair == 0, stop=pair == 7)
                mm.then_inc(core.p2v.sem, core.p2v.add(1))

        @block.vector
        def _(dve):
            for ch in range(KC):
                dve.wait_ge(core.p2v.sem, core.p2v.at(ch + 1))
                nc.vector.scalar_tensor_tensor(out=x[:, ch, :], in0=core.bank[ch][:, :], scalar=core.mod[:, 40 + ch, 0:1],
                                               in1=x[:, ch, :], op0=ALU.mult, op1=ALU.add)


def experts(core, xe, y):
    nc, dram = core.nc, core.dram
    ident = core.c("common", "ident")
    flat = [s[:, :] for s in core.slab]
    TILES, PAIRS, CREDIT = 12, EXPERTS // 2, 2
    n0 = core.expert_tile
    xcur = [flat[6][:, 512 * i:512 * (i + 1)].rearrange("p (k s) -> p k s", k=KC) for i in range(2)]
    sg = [flat[6][0:CAP, 1024 + 512 * i:1536 + 512 * i] for i in range(2)]
    hid = [core.work[:, 512 * i:512 * i + 512] for i in range(2)]
    hT = [flat[6][:, 2048 + 1024 * i:3072 + 1024 * i].rearrange("p (f s) -> p f s", s=CAP) for i in range(2)]
    pairs = {k: dram[k].rearrange("(a s) k c -> a s k c", s=2) for k in ("w_gate", "w_up", "w_down")}
    used, moe = core.weight_used, core.moe
    G, U, T, Y = core.bank[0:2], core.bank[2:4], core.bank[4:6], core.bank[6:8]
    slot = lambda j: (n0 + j) % SLOTS

    def at_least(engine, raised, pair, per, n):
        engine.wait_ge(raised.sem, pair * per + (n + CREDIT))

    with core.stage() as block:
        @block.sync
        def _(sp):
            def issue(pair, s, j):
                if j < 8:
                    w = pairs[("w_gate", "w_up")[j % 2]]
                    src = w[bass.ds(pair, 1), s, :, (j // 2) * 512:(j // 2 + 1) * 512]
                else:
                    rows, half = (j - 8) // 2, (j - 8) % 2
                    src = pairs["w_down"][bass.ds(pair, 1), s, rows * D:(rows + 1) * D, half * 512:(half + 1) * 512]
                sp.wait_ge(used.sem, pair * (2 * TILES) + (n0 + s * TILES + j - SLOTS + 1))
                sp.dma_start(core.ring[slot(j)][:, :, :], src.rearrange("a (k p) c -> p (a k) c", p=P)).then_inc(
                    core.weight_in[slot(j)].sem, 16)

            for j in range(SLOTS, TILES):
                issue(0, 0, j)
            for j in range(TILES):
                issue(0, 1, j)
            with sp.Fori(1, PAIRS) as pair:
                for s in range(2):
                    for j in range(TILES):
                        issue(pair, s, j)
            core.issued = n0 + EXPERTS * TILES
            core.issue_weights(sp, n0 + EXPERTS * TILES)

        @block.tensor
        def _(pe):
            def product(pair, s, j, out, lhsT, first, last):
                pe.wait_ge(core.weight_in[slot(j)].sem, pair * (2 * TILES // SLOTS * 16) + 16 * ((n0 + s * TILES + j) // SLOTS + 1))
                for k in range(KC):
                    mm = nc.tensor.matmul(out, lhsT[:, k, :], core.ring[slot(j)][:, k, :], start=first and k == 0,
                                          stop=last and k == KC - 1)
                mm.then_inc(used.sem, 1)

            def turn(pair, s, h):
                at_least(pe, moe["hidden"], pair, 8, 4 * s + 2 * h + 2)
                at_least(pe, moe["turned_read"], pair, 4, 2 * s + h - 1)
                for c in range(4):
                    mm = nc.tensor.transpose(T[h][:, c * P:(c + 1) * P], hid[h][:, c * P:(c + 1) * P], ident)
                mm.then_inc(moe["turned"].sem, 1)

            with pe.Fori(0, PAIRS) as pair:
                for s in range(2):
                    at_least(pe, moe["fetched"], pair, 2, s + 1)
                    for f in range(4):
                        at_least(pe, moe["hidden"], pair, 8, 4 * s + f - 1)
                        product(pair, s, 2 * f, G[f % 2][0:CAP, :], xcur[s], True, True)
                        product(pair, s, 2 * f + 1, U[f % 2][0:CAP, :], xcur[s], True, True)
                        if f == 2:
                            turn(pair, s, 0)
                    at_least(pe, moe["result_read"], pair, 2, s - 1)
                    for rows in range(2):
                        if rows == 1:
                            turn(pair, s, 1)
                        at_least(pe, moe["turned_read"], pair, 4, 2 * s + rows + 1)
                        for half in range(2):
                            product(pair, s, 8 + 2 * rows + half, Y[half][64 * s:64 * s + CAP, :], hT[s][:, 8 * rows:8 * rows + 8, :],
                                    rows == 0, rows == 1)

        @block.scalar
        def _(act):
            def turned(pair, s, h):
                at_least(act, moe["turned"], pair, 4, 2 * s + h + 1)
                if h == 0:
                    at_least(act, moe["result_read"], pair, 2, s - 1)
                nc.scalar.copy(hT[s][:, 8 * h:8 * h + 8, :].rearrange("p (f c) s -> p c f s", f=2),
                               T[h][:, :].rearrange("p (c f s) -> p c f s", c=4, f=2)).then_inc(moe["turned_read"].sem, 1)

            act.sem_inc(moe["turned_read"].sem, CREDIT)
            act.sem_inc(moe["silu"].sem, CREDIT)
            with act.Fori(0, PAIRS) as pair:
                for s in range(2):
                    for f in range(4):
                        g = 4 * s + f
                        act.wait_ge(used.sem, pair * (2 * TILES) + (n0 + s * TILES + 2 * f + 1))
                        at_least(act, moe["hidden"], pair, 8, g - 1)
                        nc.scalar.activation(sg[f % 2], G[f % 2][0:CAP, :], ACT.Silu).then_inc(moe["silu"].sem, 1)
                        if f == 2:
                            turned(pair, s, 0)
                    turned(pair, s, 1)

        @block.vector
        def _(dve):
            dve.sem_inc(moe["fetched"].sem, CREDIT)
            dve.sem_inc(moe["hidden"].sem, CREDIT)
            dve.sem_inc(moe["result_read"].sem, CREDIT)
            with dve.Fori(0, PAIRS) as pair:
                for s in range(2):
                    dve.wait_ge(used.sem, pair * (2 * TILES) + (n0 + (s - 2) * TILES + 8))
                    nc.vector.tensor_copy(xcur[s], xe[:, :, bass.ds(pair * (2 * CAP) + s * CAP, CAP)]).then_inc(moe["fetched"].sem, 1)
                    for f in range(4):
                        g = 4 * s + f
                        dve.wait_ge(used.sem, pair * (2 * TILES) + (n0 + s * TILES + 2 * f + 2))
                        at_least(dve, moe["silu"], pair, 8, g + 1)
                        at_least(dve, moe["turned"], pair, 4, 2 * s + f // 2 - 1)
                        nc.vector.tensor_tensor(hid[f // 2][64 * (f % 2):64 * (f % 2) + CAP, :], sg[f % 2], U[f % 2][0:CAP, :], ALU.mult).then_inc(moe["hidden"].sem, 1)
                    dve.wait_ge(used.sem, pair * (2 * TILES) + (n0 + (s + 1) * TILES))
                    for half in range(2):
                        ins = nc.vector.tensor_copy(y[half][64 * s:64 * s + CAP, bass.ds(pair, 1), :],
                                                    Y[half][64 * s:64 * s + CAP, :].unsqueeze(1))
                    ins.then_inc(moe["result_read"].sem, 1)
            dve.wait_ge(moe["result_read"].sem, CREDIT + EXPERTS)

        @block.gpsimd
        def _(pool):
            pool.sem_inc(moe["turned"].sem, CREDIT)


RW, LORA = 512, 64
Q0, K0, G0 = 1952, 2464, 2720
DECAY_SCALE = -float(np.exp(-0.5))


def plan_second(core):
    d = core.dram
    core.plan("rwkv_in", d["w_in_2"], 0, Q0)
    core.plan("q2", d["w_in_2"], Q0, K0)
    core.plan("kv2", d["w_in_2"], K0, G0)
    core.plan("ga2", d["w_in_2"], G0, G0 + D)
    core.plan("pa2", d["w_branch_rwkv"], 0, D)
    core.plan("gb2", d["w_in_2"], G0 + D, G0 + 2 * D)
    core.plan("pb2", d["w_branch_attn"], 0, D)
    core.plan("wo2", d["w_out_2"], 0, D)
    core.plan("ff1", d["w_ff1"], 0, 4 * D)
    core.plan("ff2", d["w_ff2"], 0, D)


def laid_out_second(x, chunks):
    pad = lambda a: np.concatenate([a, np.zeros((2048 - a.shape[-1],), a.dtype)])
    twice = lambda a: np.concatenate([a[0], a[0]])
    mu = x["rwkv_shift_2"][0]
    p2 = [x["mix_norm_g_2"], pad(mu[0]), pad(mu[1]), x["decay_w0_2"], x["icl_a0_2"], x["k_k_2"], x["k_a_2"], x["r_k_2"],
          x["lnx_g_2"], x["lnx_b_2"], twice(x["q_norm_g_2"]), twice(x["k_norm_g_2"]), x["ffn_norm_g_2"], x["final_norm_g_2"]]
    return {
        "meta": np.ascontiguousarray(x["meta_tokens_2"].reshape(META, KC, P).transpose(2, 1, 0)),
        "w_in_2": x["w_in_2"][0], "w_branch_rwkv": x["w_branch_rwkv_2"][0], "w_branch_attn": x["w_branch_attn_2"][0],
        "w_out_2": x["w_out_2"][0], "w_ff1": x["w_ff1_2"][0], "w_ff2": x["w_ff2_2"][0],
        "decay_w2": x["decay_w2_2"][0].reshape(P, RW), "icl_a2": x["icl_a2_2"][0].reshape(P, RW), "gate_w2": x["gate_w2_2"][0],
        "p2": np.ascontiguousarray(np.concatenate([chunks(a) for a in p2], 1)),
        "second": packed(second_constants()), "grid": packed(grid_tables()),
    }


def second_block(core):
    nc, dram = core.nc, core.dram
    X, H, S2, S3, S4, S5, S6 = [s.rearrange("p (k t) -> p k t", k=KC) for s in core.slab]
    T = TOK2
    np2 = core.use_params("p2")
    consts = second_constants()
    core.place("second", consts, core.area)
    load(core, [(X[:, :, 0:META], dram["meta"]), (core.param[:, 0:np2], dram["p2"]),
                (core.area[:, 0:columns(consts)[1]], dram["second"])])
    mix = lambda k: core.col("mix_g", k)
    rms_norm(core, X, KC, T, S2, H, mix, D)

    raw = [S2, S3]
    z = [S4, S5]
    dense(core, "rwkv_in", H, T, lambda eng, ps, ch, t0, t1: nc.scalar.copy(raw[ch // KC][0:ps.shape[0], ch % KC, t0:t1], ps))
    with core.stage() as block:
        @block.vector
        def _(dve):
            step = Chain(dve, core.dve_step)
            mu = lambda name: core.param[:, core.pcols[name]:core.pcols[name] + 16]
            own = core.small[:, 0:16]
            step(nc.vector.tensor_tensor(own, mu("mu0"), mu("mu1"), ALU.add))
            step(nc.vector.tensor_scalar(own, own, -1.0, 1.0, ALU.mult, ALU.add))
            for ch in range(16):
                rows = slice(0, P if ch < 15 else 32)
                p_, z_ = raw[ch // KC][rows, ch % KC, :], z[ch // KC][rows, ch % KC, :]
                step(nc.vector.tensor_scalar(z_, p_, own[rows, ch:ch + 1], None, ALU.mult))
                step(nc.vector.scalar_tensor_tensor(out=z_[:, 1:T], in0=p_[:, 0:T - 1], scalar=core.col("mu0", ch, rows),
                                                    in1=z_[:, 1:T], op0=ALU.mult, op1=ALU.add))
                step(nc.vector.scalar_tensor_tensor(out=z_[:, 0:T - 1], in0=p_[:, 1:T], scalar=core.col("mu1", ch, rows),
                                                    in1=z_[:, 0:T - 1], op0=ALU.mult, op1=ALU.add))

    lora = core.work[:, 0:2 * RW].rearrange("p (j c) -> p j c", j=2)
    gw = core.slab[1][:, 0:2 * RW].rearrange("p (j c) -> p j c", j=2)
    load(core, [(lora[:, 0], dram["decay_w2"]), (lora[:, 1], dram["icl_a2"]), (gw[:, 0], dram["gate_w2"][0:P]),
                (gw[0:32, 1], dram["gate_w2"][P:P + 32])])
    g = S6[:, 0:4]
    halves = splits_of(T)
    with core.stage() as block:
        @block.scalar
        def _(act):
            nc.scalar.activation(S5[:, 4, :], S5[:, 4, :], ACT.Tanh)
            nc.scalar.activation(S5[:, 6, :], S5[:, 6, :], ACT.Sigmoid)
            nc.scalar.activation(S5[0:32, 7, :], S5[0:32, 7, :], ACT.Sigmoid).then_inc(core.a2p.sem, core.a2p.add(1))
            for c in range(4):
                for s, (a, b) in enumerate(halves):
                    act.wait_ge(core.p2a.sem, core.p2a.at(2 * c + s + 1))
                    nc.scalar.copy(g[:, c, a:b], core.bank[2 * c + s][:, 0:b - a])

        @block.tensor
        def _(pe):
            pe.wait_ge(core.a2p.sem, core.a2p.at(1))
            for c in range(4):
                for s, (a, b) in enumerate(halves):
                    out = core.bank[2 * c + s][:, 0:b - a]
                    nc.tensor.matmul(out, gw[:, 0, c * P:(c + 1) * P], S5[:, 6, a:b], start=True, stop=False)
                    nc.tensor.matmul(out, gw[0:32, 1, c * P:(c + 1) * P], S5[0:32, 7, a:b], start=False, stop=True).then_inc(core.p2a.sem, core.p2a.add(1))

    for m in range(4):
        rwkv_heads(core, m, S4[:, m, :], S4[:, 4 + m, :], S5[:, m, :], S5[:, 4, :], S5[:, 5, :], g[:, m, :], lora)
    ya = S5[:, 0:4]

    rms_norm(core, X, KC, T, S2, H, mix, D)
    core.place("grid", grid_tables(), core.area)
    load(core, [(core.area[:, 0:2 * TOK2], dram["grid"])])
    q, k, ks, yb = S2[:, 0:4], S2[:, 4:5], S2[:, 5:6], S4[:, 0:4]
    v = core.slab[3][:, 0:5 * P].rearrange("p (t c) -> p t c", t=5)
    dense(core, "q2", H, T, copy_to(core, q))

    def kv_groups(c0, cw):
        for a, b in halves:
            yield (P, b - a, lambda w, kc, kk, a=a, b=b: (w[:, kc, 0:P], H[:, kk, a:b]), "act",
                   lambda eng, ps, a=a, b=b: nc.scalar.copy(k[:, 0, a:b], ps))
        yield from token_groups(H, T, P, P, lambda eng, ps, t, c0: nc.vector.tensor_copy(v[0:ps.shape[0], t, :], ps), "dve")
    run_groups(core, "kv2", kv_groups)
    head = core.c("common", "head")
    head_norm(core, q, 4, T, S6, head, 64, 1e-6, lambda c: core.col("qg", 0), q)
    head_norm(core, k, 1, T, S6, head, 64, 1e-6, lambda c: core.col("kg", 0), k)
    cos, sin = core.c("grid", "cos"), core.c("grid", "sin")
    rope(core, q, 4, T, core.c("common", "rot16"), cos, sin)
    rope(core, k, 1, T, core.c("common", "rot16"), cos, sin)
    exchange_halves(core, k, ks, 1, T)
    units = []
    for hd in range(8):
        kv, rows = hd // 4, slice(64 * (hd % 2), 64 * (hd % 2) + 64)
        keys = k if hd % 2 == kv else ks
        for t0 in range(0, T, P):
            mq = min(P, T - t0)
            query = q[rows, hd // 2, t0:t0 + mq]
            segs = [([(query, keys[rows, 0, 0:SEQ])], SEQ, None), ([(query, keys[rows, 0, SEQ:T])], META, None)]
            blocks = [(v[0:min(P, T - b * P), b, kv * 64:kv * 64 + 64], min(P, T - b * P)) for b in range(5)]
            units.append((mq, segs, blocks, 64, 64 * (hd % 2), yb[rows, hd // 2, t0:t0 + mq], None))
    attention(core, units, 64 ** -0.5, core.slab[3][:, 640:2560], core.slab[3][:, 2560:3840])

    merge_branches(core, H, T, [("ga2", "pa2", ya, 0), ("gb2", "pb2", yb, 8)], S6, S2, None)
    add = lambda eng, ps, ch, t0, t1: nc.vector.tensor_tensor(X[:, ch, t0:t1], ps, X[:, ch, t0:t1], ALU.add)
    dense(core, "wo2", S6, T, add, by="dve")

    rms_norm(core, X, KC, T, S2, H, lambda c: core.col("ffn_g", c), D)
    hidden = core.slabs[:, 2 * core.slab_cols:6 * core.slab_cols].rearrange("p (k t) -> p k t", k=4 * KC)

    def relu_squared(eng, ps, ch, t0, t1):
        to = hidden[:, ch, t0:t1]
        nc.scalar.activation(to, ps, ACT.Relu).then_inc(core.act_step.sem, core.act_step.add(1))
        nc.scalar.wait_ge(core.act_step.sem, core.act_step.at(core.act_step.sent))
        return nc.scalar.activation(to, to, ACT.Square)
    dense(core, "ff1", H, T, relu_squared)
    dense(core, "ff2", hidden, T, add, by="dve")
    rms_norm(core, X, KC, T, S2, X, lambda c: core.col("final", c), D)


class Carve:

    def __init__(self, region):
        self.region, self.at = region, 0

    def __call__(self, n):
        self.at += n
        assert self.at <= self.region.shape[1]
        return self.region[:, self.at - n:self.at]


def rwkv_heads(core, m, r, k, v, wd, ad, g, lora):
    nc = core.nc
    T = TOK2
    halves = splits_of(T)
    head, ident, eye64 = core.c("common", "head"), core.c("common", "ident"), core.c("common", "eye64")
    c1, c2, c3 = Carve(core.slabs[:, core.slab_cols:4 * core.slab_cols]), Carve(core.slab[6][:, 4 * T:8 * T]), Carve(core.work[:, 2 * RW:2300])
    AR = c1(4 * WIDE).rearrange("p (d j t) -> p d j t", d=2, j=2)
    BK = c1(4 * WIDE).rearrange("p (d j t) -> p d j t", d=2, j=2)
    gh = c1(4 * NBLK * 64)
    G = gh[:, 0:2 * NBLK * 64].rearrange("p (d b c) -> p d b c", d=2, c=64)
    Hs = gh[:, 2 * NBLK * 64:].rearrange("p (d b c) -> p d b c", d=2, c=64)
    rz = c1(3 * WIDE)
    Rhat = rz[:, 0:2 * WIDE].rearrange("p (d t) -> p d t", d=2)
    Z = rz[:, 2 * WIDE:]
    Vp = c1(WIDE)
    PC = c1(2 * NBLK).rearrange("p (d b) -> p d b", d=2)
    square = lambda t: t.rearrange("p (u t) -> p u t", u=4)
    Xs, Ml, Dm = square(c1(512)), square(c1(512)), square(c1(512))
    DT, RB, RK, NT = (square(c2(512)) for _ in range(4))
    AU = NT
    BKc = square(c3(512))
    BT, KT, VT = c3(256).rearrange("p (d c) -> p d c", d=2), c3(256).rearrange("p (d c) -> p d c", d=2), c3(P)
    AUin = square(core.rstd[:, 0:512])
    lam, s1, s2, icl = (gh[:, i * 2 * WIDE:(i + 1) * 2 * WIDE].rearrange("p (d t) -> p d t", d=2) for i in range(4))
    kk, t1, t2 = rz[:, 0:WIDE], rz[:, WIDE:2 * WIDE], rz[:, 2 * WIDE:]
    A, R, B, K = AR[:, :, 0], AR[:, :, 1], BK[:, :, 0], BK[:, :, 1]
    col = lambda name, i=m: core.col(name, i)
    one_less = core.small[:, 0:1]

    with core.stage() as block:
        @block.tensor
        def _(pe):
            for j, src in enumerate((wd, ad)):
                for d in range(2):
                    rows = slice(64 * d, 64 * d + 64)
                    for s, (a, b) in enumerate(halves):
                        nc.tensor.matmul(core.bank[4 * j + 2 * d + s][:, 0:b - a], lora[rows, j, m * P:(m + 1) * P],
                                                      src[rows, a:b], start=True, stop=True).then_inc(core.p2a.sem, core.p2a.add(1))
            pe.wait_ge(core.v2p.sem, core.v2p.at(1))
            pe.wait_ge(core.a2p.sem, core.a2p.at(1))
            for s, (a, b) in enumerate(halves):
                nc.tensor.matmul(core.bank[s][:, 0:b - a], head, t1[:, a:b], start=True, stop=True).then_inc(core.p2a.sem, core.p2a.add(1))

        @block.scalar
        def _(act):
            for j, (dst, bias) in enumerate(((lam, "w0"), (icl, "a0"))):
                for d in range(2):
                    for s, (a, b) in enumerate(halves):
                        n = 4 * j + 2 * d + s
                        act.wait_ge(core.p2a.sem, core.p2a.at(n + 1))
                        ins = nc.scalar.activation(dst[:, d, a:b], core.bank[n][:, 0:b - a], ACT.Sigmoid, bias=core.col(bias, 4 * d + m))
            ins.then_inc(core.a2p.sem, core.a2p.add(1))
            act.wait_ge(core.p2a.sem, core.p2a.at(10))
            for s, (a, b) in enumerate(halves):
                ins = nc.scalar.activation(t2[:, a:b], core.bank[s][:, 0:b - a], ACT.Sqrt)
            ins.then_inc(core.a2v.sem, core.a2v.add(1))

        @block.vector
        def _(dve):
            step = Chain(dve, core.dve_step)
            for t in (A, R, B, K, lam):
                nc.vector.memset(t[:, :, T:WIDE], 0.0)
            nc.vector.memset(Vp[:, T:WIDE], 0.0)
            nc.vector.tensor_copy(Vp[:, 0:T], v)
            step(nc.vector.tensor_scalar(kk[:, 0:T], k, col("k_k"), None, ALU.mult))
            step(nc.vector.tensor_scalar(one_less, col("k_a"), -1.0, 1.0, ALU.mult, ALU.add))
            nc.vector.tensor_tensor(t1[:, 0:T], kk[:, 0:T], kk[:, 0:T], ALU.mult).then_inc(core.v2p.sem, core.v2p.add(1))
            dve.wait_ge(core.a2v.sem, core.a2v.at(1))
            step(nc.vector.tensor_scalar(t2[:, 0:T], t2[:, 0:T], 1e-12, None, ALU.max))
            step(nc.vector.reciprocal(t2[:, 0:T], t2[:, 0:T]))
            step(nc.vector.tensor_tensor(kk[:, 0:T], kk[:, 0:T], t2[:, 0:T], ALU.mult))

    blocks = lambda t: t.rearrange("p (b l) -> p b l", l=LB)
    with core.stage() as block:
        @block.vector
        def _(dve):
            step = Chain(dve, core.dve_step)
            src, dst, other = lam, s1, s2
            n = 1
            while n < LB:
                for d in range(2):
                    i, o = blocks(src[:, d, :]), blocks(dst[:, d, :])
                    if d == 0:
                        new, keep, back = slice(n, LB), slice(0, n), slice(0, LB - n)
                    else:
                        new, keep, back = slice(0, LB - n), slice(LB - n, LB), slice(n, LB)
                    step(nc.vector.tensor_copy(o[:, :, keep], i[:, :, keep]))
                    step(nc.vector.tensor_tensor(o[:, :, new], i[:, :, new], i[:, :, back], ALU.add))
                src, dst = dst, (other if dst is s1 else s1)
                n *= 2
            assert src is s1
            step(nc.vector.tensor_tensor(s2, s1, lam, ALU.subtract))
            nc.vector.tensor_copy(PC[:, 0, :], blocks(s1[:, 0, :])[:, :, LB - 1]).then_inc(core.v2a.sem, core.v2a.add(1))
            nc.vector.tensor_copy(PC[:, 1, :], blocks(s1[:, 1, :])[:, :, 0]).then_inc(core.v2a.sem, core.v2a.add(1))
            dve.wait_ge(core.a2v.sem, core.a2v.at(1))
            for d in range(2):
                a, r_, b, kd = (t[:, d, 0:T] for t in (A, R, B, K))
                step(nc.vector.scalar_tensor_tensor(out=a, in0=kk[:, 0:T], scalar=-1.0, in1=a, op0=ALU.mult, op1=ALU.mult))
                step(nc.vector.tensor_tensor(r_, r_, r, ALU.mult))
                step(nc.vector.tensor_scalar(t1[:, 0:T], icl[:, d, 0:T], col("k_a"), one_less, ALU.mult, ALU.add))
                step(nc.vector.tensor_tensor(t1[:, 0:T], t1[:, 0:T], k, ALU.mult))
                step(nc.vector.tensor_tensor(kd, t1[:, 0:T], b, ALU.mult))
                step(nc.vector.tensor_tensor(icl[:, d, 0:T], icl[:, d, 0:T], kk[:, 0:T], ALU.mult))
                step(nc.vector.tensor_tensor(b, b, icl[:, d, 0:T], ALU.mult))
                if d == 0:
                    step(nc.vector.tensor_copy(t2[:, 0:T], t1[:, 0:T]))
                else:
                    step(nc.vector.tensor_tensor(t2[:, 0:T], t1[:, 0:T], t2[:, 0:T], ALU.add))
            step(nc.vector.tensor_scalar(t2[:, 0:T], t2[:, 0:T], col("r_k"), 0.5, ALU.mult, ALU.mult))
            nc.vector.tensor_tensor(t2[:, 0:T], t2[:, 0:T], r, ALU.mult).then_inc(core.v2p.sem, core.v2p.add(1))
            dve.wait_ge(core.p2v.sem, core.p2v.at(1))
            for s, (a, b) in enumerate(halves):
                nc.vector.tensor_tensor(v[:, a:b], core.bank[s][:, 0:b - a], Vp[:, a:b], ALU.mult)

        @block.scalar
        def _(act):
            act.wait_ge(core.v2a.sem, core.v2a.at(2))
            nc.scalar.activation(PC, PC, ACT.Exp, scale=DECAY_SCALE)
            nc.scalar.activation(R[:, :, 0:T], s1[:, :, 0:T], ACT.Exp, scale=DECAY_SCALE)
            nc.scalar.activation(A[:, :, 0:T], s2[:, :, 0:T], ACT.Exp, scale=DECAY_SCALE)
            nc.scalar.activation(B[:, :, 0:T], s1[:, :, 0:T], ACT.Exp, scale=-DECAY_SCALE).then_inc(core.a2v.sem, core.a2v.add(1))

        @block.tensor
        def _(pe):
            pe.wait_ge(core.v2p.sem, core.v2p.at(1))
            for s, (a, b) in enumerate(halves):
                mm = nc.tensor.matmul(core.bank[s][:, 0:b - a], head, t2[:, a:b], start=True, stop=True)
            mm.then_inc(core.p2v.sem, core.p2v.add(1))

    strict, upto = (core.c("second", n).rearrange("p (d t) -> p d t", d=2) for n in ("strict", "upto"))
    level = {b: core.c("second", f"level{b}").rearrange("p (d t) -> p d t", d=2) for b in (1, 2, 4, 8, 16)}
    for t0 in range(0, WIDE, P):
        rwkv_tile(core, t0, min(P, WIDE - t0), AR, BK, PC, G, Hs, Rhat, Z, Vp, Xs, Ml, Dm, DT, RB, RK, NT, AU, AUin, BKc, BT, KT, VT,
                  strict, upto, level)

    S = [core.rstd[:, 128 * i:128 * (i + 1)].rearrange("p (d c) -> p d c", d=2) for i in range(2)]
    rows_of = [slice(0, 64), slice(64, P)]
    with core.stage() as block:
        @block.tensor
        def _(pe):
            for c in range(NBLK):
                pe.wait_ge(core.v2p.sem, core.v2p.at(c + 1))
                if c < NBLK - 1:
                    for d in range(2):
                        b = c if d == 0 else NBLK - 1 - c
                        for h, rows in enumerate(rows_of):
                            mm = nc.tensor.matmul(core.bank[4 + 2 * (c % 2) + h][rows, d * 64:d * 64 + 64], G[rows, d, b, :], S[c % 2][rows, d, :],
                                                  start=True, stop=True)
                    mm.then_inc(core.p2v.sem, core.p2v.add(1))
                for d in range(2):
                    b = c if d == 0 else NBLK - 1 - c
                    for h, rows in enumerate(rows_of):
                        mm = nc.tensor.matmul(core.bank[2 * h + b // 16][rows, (b % 16) * LB:(b % 16 + 1) * LB], S[c % 2][rows, d, :],
                                              Rhat[rows, d, b * LB:(b + 1) * LB], start=c == 0, stop=False, skip_group_check=True)
                mm.then_inc(core.p2a.sem, core.p2a.add(1))

        @block.vector
        def _(dve):
            step = Chain(dve, core.dve_step)
            nc.vector.memset(core.rstd[:, 0:128], 0.0).then_inc(core.v2p.sem, core.v2p.add(1))
            for c in range(NBLK - 1):
                dve.wait_ge(core.p2v.sem, core.p2v.at(c + 1))
                if c >= 1:
                    dve.wait_ge(core.p2a.sem, core.p2a.at(c))
                for h, rows in enumerate(rows_of):
                    for d, b in enumerate((c, NBLK - 1 - c)):
                        ins = nc.vector.tensor_tensor(S[(c + 1) % 2][rows, d, :], core.bank[4 + 2 * (c % 2) + h][rows, d * 64:d * 64 + 64],
                                                      Hs[rows, d, b, :], ALU.add)
                ins.then_inc(core.v2p.sem, core.v2p.add(1))
            dve.wait_ge(core.p2a.sem, core.p2a.at(NBLK))
            for h, rows in enumerate(rows_of):
                for part, (a, b) in enumerate(((0, 512), (512, WIDE))):
                    nc.vector.tensor_tensor(Z[rows, a:b], core.bank[2 * h + part][rows, 0:b - a], Z[rows, a:b], ALU.add)

    yc, sq = rz[:, 0:T], rz[:, WIDE:WIDE + T]
    y = Z[:, 0:T]
    with core.stage() as block:
        @block.tensor
        def _(pe):
            for s, (a, b) in enumerate(halves):
                mm = nc.tensor.matmul(core.bank[s][:, 0:b - a], head, y[:, a:b], start=True, stop=True)
            mm.then_inc(core.p2v.sem, core.p2v.add(1))
            pe.wait_ge(core.a2p.sem, core.a2p.at(1))
            for s, (a, b) in enumerate(halves):
                mm = nc.tensor.matmul(core.bank[2 + s][:, 0:b - a], head, sq[:, a:b], start=True, stop=True)
            mm.then_inc(core.p2a.sem, core.p2a.add(1))

        @block.scalar
        def _(act):
            act.wait_ge(core.v2a.sem, core.v2a.at(1))
            nc.scalar.activation(sq, yc, ACT.Square).then_inc(core.a2p.sem, core.a2p.add(1))
            act.wait_ge(core.p2a.sem, core.p2a.at(1))
            for s, (a, b) in enumerate(halves):
                ins = root(core, sq[:, a:b], core.bank[2 + s][:, 0:b - a], 64, 64e-5)
            ins.then_inc(core.a2v.sem, core.a2v.add(1))

        @block.vector
        def _(dve):
            step = Chain(dve, core.dve_step)
            dve.wait_ge(core.p2v.sem, core.p2v.at(1))
            for s, (a, b) in enumerate(halves):
                ins = nc.vector.scalar_tensor_tensor(out=yc[:, a:b], in0=core.bank[s][:, 0:b - a], scalar=-1.0 / 64, in1=y[:, a:b],
                                                     op0=ALU.mult, op1=ALU.add)
            ins.then_inc(core.v2a.sem, core.v2a.add(1))
            dve.wait_ge(core.a2v.sem, core.a2v.at(1))
            step(nc.vector.reciprocal(sq, sq))
            step(nc.vector.scalar_tensor_tensor(out=yc, in0=yc, scalar=col("lnx_g"), in1=sq, op0=ALU.mult, op1=ALU.mult))
            step(nc.vector.scalar_tensor_tensor(out=yc, in0=yc, scalar=col("lnx_b"), in1=v, op0=ALU.add, op1=ALU.add))
            nc.vector.tensor_tensor(v, yc, g, ALU.mult)


def rwkv_tile(core, t0, W, AR, BK, PC, G, Hs, Rhat, Z, Vp, Xs, Ml, Dm, DT, RB, RK, NT, AU, AUin, BKc, BT, KT, VT, strict, upto, level):
    nc, ident, eye64 = core.nc, core.c("common", "ident"), core.c("common", "eye64")
    tok, nb, b0 = slice(t0, t0 + W), W // LB, t0 // LB
    units = [(u, u // 2, slice(64 * (u % 2), 64 * (u % 2) + 64)) for u in range(4)]
    bank4 = [b[0:W, :].rearrange("p (u t) -> p u t", u=4) for b in core.bank]
    pairs = lambda t: t.rearrange("p (d h) t -> p d h t", d=2)[0:W, :, :, 0:W]
    of = lambda mask: mask[0:W, :, 0:W].unsqueeze(2).broadcast_to([W, 2, 2, W])
    w4 = lambda t: t[0:W, :, 0:W]
    levels = (2, 4, 8, 16)
    block_bank = (2, 3, 6, 7)
    with core.stage() as block:
        @block.tensor
        def _(pe):
            mm = nc.tensor.matmul
            for u, d, rows in sorted(units, key=lambda x: x[0] % 2):
                if u == 1:
                    last.then_inc(core.row_tile.sem, core.row_tile.add(1))
                    pe.wait_ge(core.row_tile.sem, core.row_tile.at(1))
                a, r, b, k = AR[rows, d, 0, tok], AR[rows, d, 1, tok], BK[rows, d, 0, tok], BK[rows, d, 1, tok]
                for bank, lhsT, rhs in ((0, b, a), (1, b, r), (2, k, a), (3, k, r), (4, a, b)):
                    last = mm(core.bank[bank][0:W, u * P:u * P + W], lhsT, rhs, start=True, stop=True)
            last.then_inc(core.p2v.sem, core.p2v.add(1))
            for i, src in enumerate((AR[:, 0, 0, tok], AR[:, 1, 0, tok], Vp[:, tok])):
                last = nc.tensor.transpose(core.bank[5][0:W, i * P:(i + 1) * P], src, ident)
            last.then_inc(core.p2a.sem, core.p2a.add(1))
            pe.wait_ge(core.v2p.sem, core.v2p.at(1))
            for i in range(4):
                last = nc.tensor.transpose(core.bank[6][0:W, i * P:(i + 1) * P], BKc[:, i, 0:W], ident)
            last.then_inc(core.p2a.sem, core.p2a.add(1))
            pe.wait_ge(core.v2p.sem, core.v2p.at(2))
            pe.wait_ge(core.a2p.sem, core.a2p.at(1))
            for u, d, rows in units:
                last = mm(core.bank[7][0:W, u * 64:u * 64 + 64], NT[0:W, u, 0:W], VT[0:W, rows], start=True, stop=True)
            last.then_inc(core.p2a.sem, core.p2a.add(1))
            for l in range(4):
                pe.wait_ge(core.v2p.sem, core.v2p.at(3 if l == 0 else 4 + l))
                for u, d, rows in units:
                    last = mm(core.bank[4][0:W, u * P:u * P + W], Ml[0:W, u, 0:W], Dm[0:W, u, 0:W], start=True, stop=True)
                last.then_inc(core.p2a.sem, core.p2a.add(1))
                pe.wait_ge(core.a2p.sem, core.a2p.at(4 + l))
                if l == 0:
                    pe.wait_ge(core.v2p.sem, core.v2p.at(4))
                for u, d, rows in units:
                    if l < 3:
                        mm(core.bank[2][0:W, u * P:u * P + W], DT[0:W, u, 0:W], Xs[0:W, u, 0:W], start=True, stop=True)
                    last = mm(core.bank[3][0:W, u * P:u * P + W], Xs[0:W, u, 0:W], DT[0:W, u, 0:W], start=True, stop=True)
                last.then_inc(core.p2v.sem, core.p2v.add(1))
            pe.wait_ge(core.v2p.sem, core.v2p.at(8))
            for u, d, rows in units:
                last = mm(core.bank[5][0:W, u * P:(u + 1) * P], DT[0:W, u, 0:W], AUin[0:W, u, :], start=True, stop=True)
            last.then_inc(core.p2a.sem, core.p2a.add(1))
            pe.wait_ge(core.a2p.sem, core.a2p.at(8))
            for u, d, rows in units:
                for b in range(nb):
                    t = slice(b * LB, (b + 1) * LB)
                    to = core.bank[block_bank[b]][rows, d * P:(d + 1) * P]
                    mm(to[:, 0:64], AU[t, u, 0:64], BT[t, d, rows], start=True, stop=True)
                    mm(to[:, 64:P], BT[t, d, rows], AU[t, u, 64:P], start=True, stop=False)
                    mm(to[:, 64:P], KT[t, d, rows], VT[t, rows], start=False, stop=True)
                mm(core.bank[0][rows, d * P:d * P + W], AU[0:W, u, 0:64], RB[0:W, u, 0:W], start=True, stop=True)
            for h in range(2):
                rows = slice(64 * h, 64 * h + 64)
                for i, d in enumerate(range(2)):
                    u = 2 * d + h
                    mm(core.bank[1][rows, 0:W], AU[0:W, u, 64:P], RB[0:W, u, 0:W], start=i == 0, stop=False)
                    last = mm(core.bank[1][rows, 0:W], VT[0:W, rows], RK[0:W, u, 0:W], start=False, stop=i == 1)
            last.then_inc(core.p2v.sem, core.p2v.add(1))

        @block.scalar
        def _(act):
            act.wait_ge(core.p2a.sem, core.p2a.at(1))
            nc.scalar.copy(AUin[0:W, :, 0:64], core.bank[5][0:W, 0:256].rearrange("p (u c) -> p u c", u=4))
            nc.scalar.copy(VT[0:W, :], core.bank[5][0:W, 256:384]).then_inc(core.a2p.sem, core.a2p.add(1))
            act.wait_ge(core.p2a.sem, core.p2a.at(2))
            nc.scalar.copy(BT[0:W], core.bank[6][0:W, 0:256].rearrange("p (d c) -> p d c", d=2))
            nc.scalar.copy(KT[0:W], core.bank[6][0:W, 256:512].rearrange("p (d c) -> p d c", d=2)).then_inc(core.a2p.sem, core.a2p.add(1))
            act.wait_ge(core.p2a.sem, core.p2a.at(3))
            nc.scalar.copy(AUin[0:W, :, 64:P], core.bank[7][0:W, 0:256].rearrange("p (u c) -> p u c", u=4)).then_inc(core.a2p.sem, core.a2p.add(1))
            for l in range(4):
                act.wait_ge(core.p2a.sem, core.p2a.at(4 + l))
                nc.scalar.copy(w4(Xs), w4(bank4[4])).then_inc(core.a2p.sem, core.a2p.add(1))
            act.wait_ge(core.p2a.sem, core.p2a.at(8))
            nc.scalar.copy(AU[0:W], bank4[5]).then_inc(core.a2p.sem, core.a2p.add(1))
            act.wait_ge(core.p2v.sem, core.p2v.at(6))
            nc.scalar.copy(Z[:, tok], core.bank[1][:, 0:W])

        @block.vector
        def _(dve):
            step = Chain(dve, core.dve_step)
            tt = nc.vector.tensor_tensor
            for i in range(4):
                j, d = i // 2, i % 2
                ins = tt(BKc[:, i, 0:W].rearrange("p (b l) -> p b l", l=LB), BK[:, d, j, tok].rearrange("p (b l) -> p b l", l=LB),
                         PC[:, d, b0:b0 + nb].unsqueeze(2).broadcast_to([P, nb, LB]), ALU.mult)
            ins.then_inc(core.v2p.sem, core.v2p.add(1))
            dve.wait_ge(core.p2v.sem, core.p2v.at(1))
            tt(pairs(NT), pairs(bank4[2]), of(strict), ALU.mult).then_inc(core.v2p.sem, core.v2p.add(1))
            eye = ident[0:W, 0:W].unsqueeze(1).broadcast_to([W, 4, W])
            step(tt(pairs(DT), pairs(bank4[0]), of(level[1]), ALU.mult))
            for d in range(2):
                step(tt(w4(Dm)[:, 2 * d:2 * d + 2], bank4[4][:, 2 * d:2 * d + 2, 0:W],
                        level[1][0:W, 1 - d, 0:W].unsqueeze(1).broadcast_to([W, 2, W]), ALU.mult))
            step(tt(w4(DT), w4(DT), eye, ALU.add))
            step(tt(w4(Dm), w4(Dm), eye, ALU.add))
            tt(pairs(Ml), pairs(bank4[0]), of(level[2]), ALU.mult).then_inc(core.v2p.sem, core.v2p.add(1))
            tt(pairs(RB), pairs(bank4[1]), of(upto), ALU.mult)
            tt(pairs(RK), pairs(bank4[3]), of(upto), ALU.mult).then_inc(core.v2p.sem, core.v2p.add(1))
            for l in range(4):
                if l < 3:
                    dve.wait_ge(core.p2a.sem, core.p2a.at(4 + l))
                    step(tt(pairs(Ml), pairs(bank4[0]), of(level[levels[l + 1]]), ALU.mult))
                dve.wait_ge(core.p2v.sem, core.p2v.at(2 + l))
                if l < 3:
                    step(tt(w4(Dm), w4(Dm), w4(bank4[2]), ALU.add))
                tt(w4(DT), w4(DT), w4(bank4[3]), ALU.add).then_inc(core.v2p.sem, core.v2p.add(1))
            dve.wait_ge(core.p2v.sem, core.p2v.at(6))
            for d in range(2):
                tt(Rhat[:, d, tok], core.bank[0][:, d * P:d * P + W], AR[:, d, 1, tok], ALU.add)
                for b in range(nb):
                    nc.vector.scalar_tensor_tensor(out=G[:, d, b0 + b, :], in0=eye64, scalar=PC[:, d, b0 + b:b0 + b + 1],
                                                   in1=core.bank[block_bank[b]][:, d * P:d * P + 64], op0=ALU.mult, op1=ALU.add)
            for b in range(nb):
                nc.vector.tensor_copy(Hs[:, :, b0 + b, :], core.bank[block_bank[b]][:, 0:2 * P].rearrange("p (d c) -> p d c", d=2)[:, :, 64:P])


HALF_PI = float(np.pi / 2)
ROUNDER = 1.5 * 2.0 ** 23
TURN = (6.28125, 0.0019350051879882812, float(2 * np.pi - 6.28125 - 0.0019350051879882812))


def plan_third(core):
    d = core.dram
    w = d["even_w_in"]
    at = 0
    for name, n in (("qk3", 1024), ("v3", D), ("gret", D), ("cb", D), ("cc", D), ("cx", D), ("gconv", D)):
        core.third_cols[name] = (at, at + n)
        at += n
    for name in ("qk3", "v3", "gret", "cc", "cx", "cb", "gconv"):
        core.plan(name, w, *core.third_cols[name])
    core.plan("wo3", d["even_w_out"], 0, D)
    w = d["odd_w_in"]
    core.plan("cq", w, 0, 384)
    core.plan("ckv", w, 384, 640)
    core.plan("kr", w, 640, 704)
    core.plan("qb", d["w_qb"], 0, 1536, wide=384)
    core.plan("kvb", d["w_kvb"], 0, 2048)
    core.plan("gate3", w, 704, 1728)
    core.plan("wo4", d["odd_w_out"], 0, D)


def laid_out_third(x, chunks):
    p3 = [x["pre_norm_3"], x["post_norm_3"], x["even_conv_w_3"][0].reshape(-1), x["even_conv_b_3"], x["ret_gn_3"], x["q_a_norm_3"],
          x["kv_a_norm_3"]]
    return {
        "positions": np.ascontiguousarray(x["positions_3"][0]), "even_w_in": x["even_w_in_3"][0], "even_w_out": x["even_w_out_3"][0],
        "odd_w_in": x["odd_w_in_3"][0], "w_qb": x["w_qb_3"][0], "w_kvb": x["w_kvb_3"][0], "odd_w_out": x["odd_w_out_3"][0],
        "p3": np.ascontiguousarray(np.concatenate([chunks(a) for a in p3], 1)), "third": packed(third_constants()),
    }


def each_chunk(core, op):
    with core.stage() as block:
        @block.vector
        def _(dve):
            for k in range(KC):
                op(k)


def add_normalised(core, x, y, squares, post):
    rms_norm(core, y, KC, SEQ, squares, y, post, D)
    each_chunk(core, lambda k: core.nc.vector.tensor_tensor(x[:, k, :], x[:, k, :], y[:, k, :], ALU.add))


def third_block(core):
    nc, dram = core.nc, core.dram
    slabs = [s.rearrange("p (k t) -> p k t", k=KC) for s in core.slab]
    x = slabs[0][:, :, META:]
    H, S2, S3, S4, S5, S6 = [s[:, :, 0:SEQ] for s in slabs[1:]]
    n3 = core.use_params("p3")
    consts = third_constants()
    core.place("third", consts, core.area)
    c = lambda name: core.c("third", name)
    where = core.slab[6][:, 0:SEQ].bitcast(I32)
    load(core, [(core.param[:, 0:n3], dram["p3"]), (core.area[:, 0:columns(consts)[1]], dram["third"]),
                (where, dram["positions"].partition_broadcast(P))])

    sin, cos = core.work[:, 1024:1536], core.work[:, 1536:2048]
    ang, turns = core.slab[6][:, SEQ:2 * SEQ], core.slab[6][:, 2 * SEQ:3 * SEQ]
    with core.stage() as block:
        @block.vector
        def _(dve):
            step = Chain(dve, core.dve_step)
            step(nc.vector.tensor_copy(ang, where))
            step(nc.vector.tensor_scalar(ang, ang, c("inv"), None, ALU.mult))
            for out, ahead in ((sin, 0.0), (cos, 0.25)):
                step(nc.vector.tensor_scalar(turns, ang, float(0.5 / np.pi), ahead, ALU.mult, ALU.add))
                step(nc.vector.tensor_scalar(turns, turns, ROUNDER, None, ALU.add))
                step(nc.vector.tensor_scalar(turns, turns, ROUNDER, None, ALU.subtract))
                step(nc.vector.scalar_tensor_tensor(out=out, in0=turns, scalar=-TURN[0], in1=ang, op0=ALU.mult, op1=ALU.add))
                for part in TURN[1:]:
                    step(nc.vector.scalar_tensor_tensor(out=out, in0=turns, scalar=-part, in1=out, op0=ALU.mult, op1=ALU.add))
                if ahead:
                    step(nc.vector.tensor_scalar(out, out, HALF_PI, None, ALU.add))
                step(nc.vector.tensor_scalar(out, out, 3.1415925, -3.1415925, ALU.min, ALU.max))
            nc.vector.tensor_copy(ang, ang).then_inc(core.v2a.sem, core.v2a.add(1))

        @block.scalar
        def _(act):
            act.wait_ge(core.v2a.sem, core.v2a.at(1))
            nc.scalar.activation(sin, sin, ACT.Sin)
            nc.scalar.activation(cos, cos, ACT.Sin)

    rms_norm(core, x, KC, SEQ, S2, H, lambda k: core.col("pre", k), D)
    qk, R = S2, S4
    v = core.slab[3][:, 0:4 * D].rearrange("p (t c) -> p t c", t=4)
    dense(core, "qk3", H, SEQ, copy_to(core, qk))
    run_groups(core, "v3", lambda c0, cw: token_groups(H, SEQ, 0, cw, lambda eng, ps, t, c0: nc.scalar.copy(v[:, t, c0:c0 + cw], ps), "act", c0))
    rope(core, qk, KC, SEQ, core.c("common", "rot32"), cos, sin)
    retention(core, qk[:, 0:4], qk[:, 4:8], v, R)
    head_norm(core, R, KC, SEQ, S6, core.c("common", "ones"), P, 1e-6, lambda k: core.col("gn", k), R)
    silu = lambda dst: (lambda eng, ps, ch, t0, t1: nc.scalar.activation(dst[:, ch, t0:t1], ps, ACT.Silu))
    dense(core, "gret", H, SEQ, silu(S6))
    each_chunk(core, lambda k: nc.vector.tensor_tensor(R[:, k, :], R[:, k, :], S6[:, k, :], ALU.mult))
    u, conv = S2, S5
    times = lambda dst: (lambda eng, ps, ch, t0, t1: nc.vector.tensor_tensor(dst[:, ch, t0:t1], ps, dst[:, ch, t0:t1], ALU.mult))
    dense(core, "cc", H, SEQ, copy_to(core, u))
    dense(core, "cx", H, SEQ, times(u), by="dve")
    with core.stage() as block:
        @block.vector
        def _(dve):
            step = Chain(dve, core.dve_step)
            for k in range(KC):
                tap = lambda j: core.col("conv_w", j * KC + k)
                step(nc.vector.tensor_scalar(conv[:, k, :], u[:, k, :], tap(2), core.col("conv_b", k), ALU.mult, ALU.add))
                for j, back in ((1, 1), (0, 2)):
                    step(nc.vector.scalar_tensor_tensor(out=conv[:, k, back:], in0=u[:, k, 0:SEQ - back], scalar=tap(j),
                                                        in1=conv[:, k, back:], op0=ALU.mult, op1=ALU.add))
    dense(core, "cb", H, SEQ, times(conv), by="dve")
    dense(core, "gconv", H, SEQ, silu(S6))
    each_chunk(core, lambda k: nc.vector.tensor_tensor(conv[:, k, :], conv[:, k, :], S6[:, k, :], ALU.mult))
    mix = core.slabs[:, 4 * core.slab_cols:6 * core.slab_cols].rearrange("p (k t) -> p k t", k=2 * KC)
    dense(core, "wo3", mix, SEQ, copy_to(core, S2))
    add_normalised(core, x, S2, S3, lambda k: core.col("post", k))

    rms_norm(core, x, KC, SEQ, S2, H, lambda k: core.col("pre", KC + k), D)
    cq, ckv, kr = S2[:, 0:3], S2[:, 3:5], S2[:, 5:6]
    dense(core, "cq", H, SEQ, copy_to(core, cq))
    dense(core, "ckv", H, SEQ, copy_to(core, ckv))
    dense(core, "kr", H, SEQ, copy_to(core, kr))
    rms_norm(core, cq, 3, SEQ, S6, cq, lambda k: core.col("qa", k), 384)
    rms_norm(core, ckv, 2, SEQ, S6, ckv, lambda k: core.col("kva", k), 256)
    qn, qr, kn = S3, S4, S5
    v = core.slab[6][:, 0:4 * D].rearrange("p (t c) -> p t c", t=4)

    def qb_groups(c0, cw):
        for h in range(2):
            for at, m, dst in ((192 * h, P, qn), (192 * h + P, 64, qr)):
                yield (m, SEQ, lambda w, k, kk, at=at, m=m: (w[:, k, at:at + m], cq[:, kk, :]), "act",
                       lambda eng, ps, dst=dst, m=m, h=c0 // 192 + h: nc.scalar.copy(dst[0:m, h, :], ps))
    run_groups(core, "qb", qb_groups)

    def kvb_groups(c0, cw):
        for h in range(2):
            yield (P, SEQ, lambda w, k, kk, h=h: (w[:, k, 256 * h:256 * h + P], ckv[:, kk, :]), "act",
                   lambda eng, ps, h=c0 // 256 + h: nc.scalar.copy(kn[:, h, :], ps))
            yield from token_groups(ckv, SEQ, 256 * h + P, P, lambda eng, ps, t, at: nc.vector.tensor_copy(v[:, t, at:at + P], ps), "dve",
                                    (c0 // 256 + h) * P)
    run_groups(core, "kvb", kvb_groups)
    rot = core.c("common", "rot32")[0:64, 0:64]
    rope(core, qr, KC, SEQ, rot, cos, sin, rows=64)
    rope(core, kr, 1, SEQ, rot, cos, sin, rows=64)
    units = []
    for h in range(8):
        for n in range(4):
            hi, t = (n + 1) * P, slice(n * P, (n + 1) * P)
            products = [(qn[:, h, t], kn[:, h, 0:hi]), (qr[0:64, h, t], kr[0:64, 0, 0:hi])]
            units.append((P, [(products, hi, c("causal")[:, SEQ - hi:])], [(v[:, b, h * P:(h + 1) * P], P) for b in range(n + 1)],
                          P, 0, qn[:, h, t], None))
    attention(core, units, 192 ** -0.5, core.slab[2][:, 0:1536], core.slab[2][:, 1536:2560], SEQ)
    dense(core, "gate3", H, SEQ, silu(S4))
    each_chunk(core, lambda k: nc.vector.tensor_tensor(qn[:, k, :], qn[:, k, :], S4[:, k, :], ALU.mult))
    dense(core, "wo4", qn, SEQ, copy_to(core, S5))
    add_normalised(core, x, S5, S2, lambda k: core.col("post", KC + k))


def retention(core, q, k, v, R):
    nc, ident = core.nc, core.c("common", "ident")
    c = lambda name: core.c("third", name)
    intra = c("intra").rearrange("p (m h i) -> p m h i", m=4, h=2)
    xi = c("xi").rearrange("p (m i) -> p m i", m=4)
    zeta, gamma = c("zeta"), c("gamma")
    kz = core.slab[5][:, 0:2048].rearrange("p (n c) -> p n c", n=4)
    qx = core.slab[5][:, 2048:4096].rearrange("p (m t) -> p m t", m=4)
    score = core.slab[6][:, 0:D].rearrange("p (h m i) -> p h m i", h=2, m=4)
    state = core.slab[6][:, D:D + 512].rearrange("p (m e) -> p m e", m=4)
    by4 = lambda t: t[:, :].rearrange("p (m i) -> p m i", m=4)
    B = core.bank
    with core.stage() as block:
        @block.tensor
        def _(pe):
            for n in range(4):
                for m in range(4):
                    last = nc.tensor.transpose(B[4 + n][:, m * P:(m + 1) * P], k[:, m, n * P:(n + 1) * P], ident)
                last.then_inc(core.p2v.sem, core.p2v.add(1))
            for n in range(4):
                t = slice(n * P, (n + 1) * P)
                if n >= 1:
                    pe.wait_ge(core.v2p.sem, core.v2p.at(2 * n))
                for h in range(2):
                    rows = slice(64 * h, 64 * h + 64)
                    for m in range(4):
                        last = nc.tensor.matmul(B[h][:, m * P:(m + 1) * P], k[rows, m, t], q[rows, m, t], start=True, stop=True)
                last.then_inc(core.p2v.sem, core.p2v.add(1))
                pe.wait_ge(core.v2p.sem, core.v2p.at(2 * n + 1))
                if n >= 1:
                    pe.wait_ge(core.a2p.sem, core.a2p.at(n))
                if n < 3:
                    for head in range(8):
                        rows = slice(64 * (head % 2), 64 * (head % 2) + 64)
                        last = nc.tensor.matmul(B[4][rows, (head // 2) * P:(head // 2 + 1) * P], kz[:, n, head * 64:head * 64 + 64],
                                                v[:, n, head * P:(head + 1) * P], start=True, stop=True)
                    last.then_inc(core.p2v.sem, core.p2v.add(1))
                for head in range(8):
                    h, m = head % 2, head // 2
                    rows = slice(64 * h, 64 * h + 64)
                    out = B[2 + h][:, m * P:(m + 1) * P]
                    last = nc.tensor.matmul(out, v[:, n, head * P:(head + 1) * P], score[:, h, m, :], start=True, stop=n == 0)
                    if n >= 1:
                        last = nc.tensor.matmul(out, state[rows, m, :], qx[rows, m, t], start=False, stop=True)
                last.then_inc(core.p2a.sem, core.p2a.add(1))

        @block.vector
        def _(dve):
            step = Chain(dve, core.dve_step)
            for m in range(4):
                nc.vector.tensor_tensor(qx[:, m].rearrange("p (n i) -> p n i", n=4), q[:, m].rearrange("p (n i) -> p n i", n=4),
                                        xi[:, m].unsqueeze(1).broadcast_to([P, 4, P]), ALU.mult)
            for n in range(4):
                dve.wait_ge(core.p2v.sem, core.p2v.at(n + 1))
                nc.vector.tensor_tensor(kz[:, n].rearrange("p (h c) -> p h c", h=8), B[4 + n][:, :].rearrange("p (h c) -> p h c", h=8),
                                        zeta.unsqueeze(2).broadcast_to([P, 8, 64]), ALU.mult)
            for n in range(4):
                dve.wait_ge(core.p2v.sem, core.p2v.at(5 + 2 * n))
                if n >= 1:
                    dve.wait_ge(core.p2a.sem, core.p2a.at(n))
                for h in range(2):
                    ins = nc.vector.tensor_tensor(score[:, h], by4(B[h]), intra[:, :, h, :], ALU.mult)
                ins.then_inc(core.v2p.sem, core.v2p.add(1))
                if n < 3:
                    dve.wait_ge(core.p2v.sem, core.p2v.at(6 + 2 * n))
                    if n == 0:
                        ins = nc.vector.tensor_copy(state, by4(B[4]))
                    else:
                        dve.wait_ge(core.p2a.sem, core.p2a.at(n + 1))
                        for m in range(4):
                            ins = nc.vector.scalar_tensor_tensor(out=state[:, m], in0=state[:, m], scalar=gamma[:, m:m + 1],
                                                                 in1=B[4][:, m * P:(m + 1) * P], op0=ALU.mult, op1=ALU.add)
                    ins.then_inc(core.v2p.sem, core.v2p.add(1))

        @block.scalar
        def _(act):
            for n in range(4):
                act.wait_ge(core.p2a.sem, core.p2a.at(n + 1))
                for h in range(2):
                    ins = nc.scalar.copy(R[:, h:8:2, n * P:(n + 1) * P], by4(B[2 + h]))
                ins.then_inc(core.a2p.sem, core.a2p.add(1))


def plan_rest(core):
    plan_second(core)
    plan_third(core)


def laid_out_rest(x, chunks):
    return {**laid_out_second(x, chunks), **laid_out_third(x, chunks)}


def program(nc, dram, out, stop_after=3):
    with ExitStack() as ctx:
        ctx.enter_context(nc.allow_non_contiguous_dma("parameters and tiles"))
        core = Core(nc, ctx, dram)
        core.place("common", common_constants(), core.common)
        w_in = dram["w_in"]
        core.plan("ada", dram["w_ada"], 0, 6 * D)
        core.plan("kv", w_in, 3 * D, 3 * D + 512)
        core.plan("q", w_in, 2 * D, 3 * D)
        core.plan("va", w_in, D, 2 * D)
        core.plan("u", w_in, 0, D)
        core.plan("ga", w_in, 3 * D + 512, 4 * D + 512)
        core.plan("pa", dram["w_proj_a"], 0, D)
        core.plan("gb", w_in, 4 * D + 512, 5 * D + 512)
        core.plan("pb", dram["w_proj_b"], 0, D)
        core.plan("wo", dram["w_out"], 0, D)
        core.expert_tile = len(core.tiles)
        for e in range(EXPERTS):
            for f in range(4):
                core.plan(f"gate{e}.{f}", dram["w_gate"][e], f * 512, f * 512 + 512)
                core.plan(f"up{e}.{f}", dram["w_up"][e], f * 512, f * 512 + 512)
            for rows in range(2):
                core.plan(f"down{e}.{rows}", dram["w_down"][e], 0, D, rows * D, (rows + 1) * D)
        plan_rest(core)
        first_block(core)
        if stop_after >= 2:
            second_block(core)
        if stop_after >= 3:
            third_block(core)
        with core.stage() as block:
            @block.sync
            def _(sp):
                sp.dma_start(out, core.slab[0].rearrange("p (k t) -> p k t", k=KC)[:, :, META:]).then_inc(core.stored.sem, core.stored.add(16))
                sp.wait_ge(core.stored.sem, core.stored.at(16))


def laid_out(inputs):
    chunks = lambda a: np.ascontiguousarray(np.asarray(a).reshape(-1, P).T)
    tokens = lambda a: np.ascontiguousarray(np.asarray(a).reshape(-1, KC, P).transpose(2, 1, 0))
    x = {k: np.asarray(v) for k, v in inputs.items()}
    c2 = np.stack([x["c"].reshape(KC, P), x["c_ctx"].reshape(KC, P)], 1)
    arrays = {
        "x": tokens(x["x"]), "ctx": tokens(x["ctx"]),
        "w_ada": x["w_ada"][0], "w_in": x["w_in"][0], "w_proj_a": x["w_proj_a"][0], "w_proj_b": x["w_proj_b"][0],
        "w_out": x["w_out"][0], "w_router": x["w_router"][0], "w_gate": x["w_exp_gate"][0], "w_up": x["w_exp_up"][0],
        "w_down": x["w_exp_down"][0], "gmlp_ln_g": x["gmlp_ln_g"][0], "gmlp_ln_b": x["gmlp_ln_b"][0],
        "b_spatial": x["b_spatial"][0].reshape(-1), "w_spatial": np.ascontiguousarray(x["w_spatial"][0].transpose(2, 0, 1)),
        "p1": np.ascontiguousarray(np.concatenate([
            chunks(c2), chunks(x["b_ada"]), chunks(x["norm1_g"]), chunks(x["b_merge_gate"]), chunks(x["norm2_g"]),
            chunks(x["final_g"]), np.broadcast_to(x["attn_sink"], (P, 16))], 1)),
        "common": packed(common_constants()), "first": packed(first_constants()),
    }
    arrays.update(laid_out_rest(x, chunks))
    return arrays


def kernel(**inputs):
    import concourse.bacc as _bacc
    from concourse.bass_utils import run_bass_kernel_spmd as _run

    nc = _bacc.Bacc("TRN2", target_bir_lowering=False, num_devices=1)
    arrays = laid_out(inputs)
    dram = {k: nc.dram_tensor(f"in_{k}", a.shape, mybir.dt.from_np(a.dtype), kind="ExternalInput").ap() for k, a in arrays.items()}
    out = nc.dram_tensor("out_channels", (P, KC, SEQ), F32, kind="ExternalOutput").ap()
    program(nc, dram, out)
    r = _run(nc, [{f"in_{k}": a for k, a in arrays.items()}], core_ids=[0])
    return np.ascontiguousarray(r.results[0]["out_channels"].transpose(2, 1, 0).reshape(1, SEQ, D))
```

```python
from contextlib import ExitStack, contextmanager

import numpy as np

import concourse.bass as bass
from concourse import mybir

ALU = mybir.AluOpType
ACT = mybir.ActivationFunctionType
AX = mybir.AxisListType
F32 = mybir.dt.float32
I32 = mybir.dt.int32

P = 128
D = 1024
KC = D // P
SEQ = 512
CTX = 256
META = 16
TOK2 = SEQ + META
SLOTS = 4
SLOT_COLS = 512
BANKS = 8
EXPERTS, CAP, DFF = 16, 64, 2048
LB = 32
NBLK = 17
WIDE = NBLK * LB


def common_constants():
    p = np.arange(P)
    ident = np.eye(P)
    ones = np.ones((P, P))
    head = (p[:, None] // 64 == p[None] // 64)
    rot16, rot32 = np.zeros((P, P)), np.zeros((P, P))
    for half, m in ((16, rot16), (32, rot32)):
        for d in range(P):
            if d % (2 * half) < half:
                m[d + half, d] = -1.0
            else:
                m[d - half, d] = 1.0
    swap = (p[:, None] == (p[None] + 64) % P)
    return [("ident", ident), ("ones", ones), ("head", head), ("rot16", rot16), ("rot32", rot32), ("swap", swap),
            ("eye64", p[:, None] % 64 == p[None, :64])]


def grid_tables():
    d = np.arange(P) % 64
    freq = (10000.0 ** (-(np.arange(0, 32, 2, dtype=np.float32)) / 32)).astype(np.float32)
    t = np.arange(SEQ)
    pos = np.where((d < 32)[:, None], t[None] // 64, t[None] % 64).astype(np.float32)
    ang = pos * freq[d % 16][:, None]
    cos = np.concatenate([np.ones((P, META)), np.cos(ang)], 1)
    sin = np.concatenate([np.zeros((P, META)), np.sin(ang)], 1)
    return [("cos", cos), ("sin", sin)]


def first_constants():
    a = np.arange(P)
    neg = np.float32(-1e30)
    before = np.where(a[None] >= a[:, None], 0, neg)
    after = np.where(a[None] <= a[:, None], 0, neg)
    return [*grid_tables(), ("window", np.concatenate([before, np.zeros((P, P)), after], 1)),
            ("earlier", (a[:, None] < a[None])), ("iota", np.tile(np.arange(CAP), (P, 1)))]


def second_constants():
    p, f = np.arange(P)[:, None], np.arange(P)[None]
    same = p // LB == f // LB
    before = [p < f, p > f]
    out = [("strict", np.stack([same & o for o in before], 1)),
           ("upto", np.stack([same & (o | (p == f)) for o in before], 1))]
    b = 1
    while b < LB:
        pair = (p // (2 * b) == f // (2 * b)) & (p // b != f // b)
        out.append((f"level{b}", np.stack([pair & o for o in before], 1)))
        b *= 2
    return [(n, a.reshape(P, -1)) for n, a in out]


LOG_GAMMA = np.log1p(-np.exp2(-5.0 - np.arange(8)))


def third_constants():
    a = np.arange(P)
    neg = np.float32(-1e30)
    causal = np.concatenate([np.zeros((P, 3 * P)), np.where(a[None] <= a[:, None], 0, neg)], 1)
    rel = a[None] - a[:, None]
    intra = [np.where(rel >= 0, np.exp(g * np.maximum(rel, 0)), 0) / 8 for g in LOG_GAMMA]
    xi = [np.exp(LOG_GAMMA[2 * m + a // 64][:, None] * (a[None] + 1.0)) for m in range(4)]
    zeta = np.exp(LOG_GAMMA[None] * (P - 1.0 - a[:, None])) / 8
    gamma = np.exp(np.stack([LOG_GAMMA[2 * m + a // 64] for m in range(4)], 1) * P)
    inv = (10000.0 ** (-(np.arange(0, 64, 2, dtype=np.float32)) / 64)).astype(np.float32)
    return [("causal", causal), ("intra", np.concatenate(intra, 1)), ("xi", np.concatenate(xi, 1)),
            ("zeta", zeta), ("gamma", gamma), ("inv", inv[a % 32][:, None])]


def packed(parts):
    return np.ascontiguousarray(np.concatenate([np.asarray(a, np.float32) for _, a in parts], 1))


def columns(parts):
    at, where = 0, {}
    for name, a in parts:
        where[name] = (at, at + a.shape[1])
        at += a.shape[1]
    return where, at


PARAMS = {
    "p1": [("cc", 16), ("b_ada", 48), ("g1", 8), ("b_gate", 16), ("g2", 8), ("final", 8), ("sink", 16)],
    "p2": [("mix_g", 8), ("mu0", 16), ("mu1", 16), ("w0", 8), ("a0", 8), ("k_k", 4), ("k_a", 4), ("r_k", 4),
           ("lnx_g", 4), ("lnx_b", 4), ("qg", 1), ("kg", 1), ("ffn_g", 8), ("final", 8)],
    "p3": [("pre", 16), ("post", 16), ("conv_w", 24), ("conv_b", 8), ("gn", 8), ("qa", 3), ("kva", 2)],
}


class Count:

    def __init__(self, sem):
        self.sem, self.base, self.sent = sem, 0, 0

    def add(self, by):
        self.sent += by
        return by

    def at(self, n):
        return self.base + n

    def close(self):
        self.base += self.sent
        self.sent = 0


class Chain:

    def __init__(self, engine, count):
        self.engine, self.count = engine, count

    def __call__(self, ins):
        ins.then_inc(self.count.sem, self.count.add(1))
        self.engine.wait_ge(self.count.sem, self.count.at(self.count.sent))


class Core:

    def __init__(self, nc, ctx, dram):
        self.nc, self.dram = nc, dram
        sb = lambda name, shape, dt=F32: ctx.enter_context(nc.sbuf_tensor(name, shape, dt))
        self.ring = [sb(f"ring{i}", [P, KC, SLOT_COLS]) for i in range(SLOTS)]
        self.slab_cols = KC * TOK2
        self.slabs = sb("slabs", [P, 7 * self.slab_cols])
        self.slab = [self.slabs[:, i * self.slab_cols:(i + 1) * self.slab_cols] for i in range(7)]
        self.common = sb("common", [P, columns(common_constants())[1]])
        self.area = sb("area", [P, 2560])
        self.param = sb("param", [P, 120])
        self.mod = sb("mod", [P, 48, 2])
        self.gains = sb("gains", [P, 24])
        self.rstd = sb("rstd", [P, TOK2])
        self.small = sb("small", [P, 64])
        self.work = sb("work", [P, 2300])
        self.bank = [ctx.enter_context(nc.psum_tensor(f"bank{i}", [P, 512], F32)) for i in range(BANKS)]
        self.eps = {e: self.small[:, 60 + i:61 + i] for i, e in enumerate((1e-6, 64e-5))}
        self.counts = []

        def count(name):
            s = Count(ctx.enter_context(nc.semaphore(name)))
            self.counts.append(s)
            return s

        self.group_full = count("group_full")
        self.read_act, self.read_dve = count("read_by_act"), count("read_by_dve")
        self.dve_step, self.act_step, self.pool_step = count("dve_step"), count("act_step"), count("pool_step")
        self.a2p, self.v2p, self.p2v, self.p2a = count("act_to_pe"), count("dve_to_pe"), count("pe_to_dve"), count("pe_to_act")
        self.v2a, self.a2v = count("dve_to_act"), count("act_to_dve")
        self.loaded, self.stored = count("inputs_loaded"), count("outputs_stored")
        self.att = {k: count(f"att_{k}") for k in ("s_ready", "s_read", "m_ready", "e_ready", "n_ready", "t_ready", "t_read", "o_ready", "o_read")}
        self.moe = {k: count(f"moe_{k}") for k in ("fetched", "silu", "hidden", "turned", "turned_read", "result_read")}
        self.rwkv = [[count(f"rwkv{s}_{k}") for k in ("pe_to_dve", "pe_to_act", "dve_to_pe", "act_to_pe", "row_tile", "dve_to_act",
                                                      "act_to_dve", "dve_step")] for s in range(2)]
        self.weight_in = [count(f"weight_in_slot{i}") for i in range(SLOTS)]
        self.weight_used = count("weight_used")
        self.tiles, self.named, self.issued, self.done = [], {}, 0, 0
        self.weight_limit = None
        self.maps, self.third_cols = {}, {}

    def place(self, name, parts, tensor):
        self.maps[name] = (columns(parts)[0], tensor)

    def c(self, area, name, rows=slice(0, P)):
        where, tensor = self.maps[area]
        a, b = where[name]
        return tensor[rows, a:b]

    def col(self, name, i, rows=slice(0, P)):
        at = self.pcols[name] + i
        return self.param[rows, at:at + 1]

    def use_params(self, which):
        at, self.pcols = 0, {}
        for name, n in PARAMS[which]:
            self.pcols[name] = at
            at += n
        return at

    def plan(self, name, w, c0, c1, k0=0, k1=None, wide=SLOT_COLS):
        k1 = w.shape[0] if k1 is None else k1
        groups = []
        for c in range(c0, c1, wide):
            cw = min(wide, c1 - c)
            group = []
            for k in range(k0, k1, KC * P):
                rows = min(KC * P, k1 - k)
                src = w[k:k + rows, c:c + cw].rearrange("(k p) c -> p k c", p=P)
                group.append((len(self.tiles), (k - k0) // P, rows // P, cw))
                self.tiles.append((src, rows // P, cw))
            groups.append((c - c0, cw, group))
        self.named[name] = groups

    def issue_weights(self, engine, upto):
        upto = min(upto + SLOTS, len(self.tiles) if self.weight_limit is None else self.weight_limit)
        while self.issued < upto:
            n = self.issued
            src, kc, cw = self.tiles[n]
            if n >= SLOTS:
                engine.wait_ge(self.weight_used.sem, n - SLOTS + 1)
            engine.dma_start(self.ring[n % SLOTS][:, 0:kc, 0:cw], src).then_inc(self.weight_in[n % SLOTS].sem, 16)
            self.issued += 1

    def weight_ready(self, engine, n):
        engine.wait_ge(self.weight_in[n % SLOTS].sem, 16 * (n // SLOTS + 1))

    @contextmanager
    def stage(self):
        with self.nc.Block() as block:
            yield block
        for s in self.counts:
            s.close()


def splits_of(tokens):
    return [(0, tokens)] if tokens <= SEQ else [(0, tokens // 2), (tokens // 2, tokens)]


def run_groups(core, name, groups_for, also=None):
    nc = core.nc
    work, count, full = [], {"act": 0, "dve": 0}, 0
    for c0, cw, group in core.named[name]:
        gs = []
        todo = list(groups_for(c0, cw))
        for i, g in enumerate(todo):
            count[g[3]] += 1
            last = i == len(todo) - 1
            full += not last
            gs.append((*g, count[g[3]], group[-1][0] + 1 if last else None, full))
        work.append((group, gs))
    flat = [g for _, gs in work for g in gs]
    reads = {"act": core.read_act, "dve": core.read_dve}
    with core.stage() as block:
        @block.tensor
        def _(pe):
            at = 0
            for group, gs in work:
                kcs = sum(kc for _, _, kc, _ in group)
                assert len(group) == 1 or len(gs) <= BANKS
                for n, kk0, kc, cw in group:
                    core.weight_ready(pe, n)
                    w = core.ring[n % SLOTS]
                    for i, (m, nn, operands, *_) in enumerate(gs):
                        out = core.bank[(at + i) % BANKS][0:m, 0:nn]
                        if kk0 == 0 and at + i >= BANKS:
                            old = flat[at + i - BANKS]
                            pe.wait_ge(reads[old[3]].sem, reads[old[3]].at(old[5]))
                        for k in range(kc):
                            lhsT, rhs = operands(w, k, kk0 + k)
                            mm = nc.tensor.matmul(out, lhsT, rhs, start=(kk0 + k == 0), stop=(kk0 + k == kcs - 1))
                        if kk0 + kc == kcs and i < len(gs) - 1:
                            mm.then_inc(core.group_full.sem, core.group_full.add(1))
                    mm.then_inc(core.weight_used.sem, 1)
                at += len(gs)

        @block.sync
        def _(sp):
            core.done = core.named[name][-1][2][-1][0] + 1
            core.issue_weights(sp, core.done)

        def reader(which, engine):
            for i, g in enumerate(flat):
                if g[3] == which:
                    if g[6] is None:
                        engine.wait_ge(core.group_full.sem, core.group_full.at(g[7]))
                    else:
                        engine.wait_ge(core.weight_used.sem, g[6])
                    g[4](which, core.bank[i % BANKS][0:g[0], 0:g[1]]).then_inc(reads[which].sem, reads[which].add(1))

        @block.scalar
        def _(act):
            reader("act", act)
            if also and count["act"] == 0:
                also(act)

        @block.vector
        def _(dve):
            reader("dve", dve)
            if also and count["dve"] == 0:
                also(dve)


def dense(core, name, x, tokens, read, by="act", width=P, also=None):
    def groups_for(c0, cw):
        for c in range(0, cw, width):
            for t0, t1 in splits_of(tokens):
                m = min(width, cw - c)
                yield (m, t1 - t0,
                       lambda w, k, kk, c=c, m=m, t0=t0, t1=t1: (w[:, k, c:c + m], x[:, kk, t0:t1]),
                       by(((c0 + c) // width)) if callable(by) else by,
                       lambda eng, ps, ch=(c0 + c) // width, t0=t0, t1=t1: read(eng, ps, ch, t0, t1))
    run_groups(core, name, groups_for, also)


def also_square(core, out, x, tokens, by):
    reads, per = {"act": core.read_act, "dve": core.read_dve}[by], len(splits_of(tokens))

    def run(engine):
        for k in range(KC):
            engine.wait_ge(reads.sem, reads.at(per * (k + 1)))
            to, of = out[:, k, 0:tokens], x[:, k, 0:tokens]
            if by == "dve":
                core.nc.scalar.activation(to, of, ACT.Square)
            else:
                core.nc.vector.tensor_tensor(to, of, of, ALU.mult)
    return run


def also_gate(core, x, gate):
    def run(engine):
        for k in range(KC):
            engine.wait_ge(core.read_act.sem, core.read_act.at(k + 1))
            core.nc.vector.tensor_tensor(x[:, k, :], x[:, k, :], gate[:, k, :], ALU.mult)
    return run


def token_groups(x, tokens, c, cw, read, by, c0=0):
    for t in range(0, tokens, P):
        m = min(P, tokens - t)
        yield (m, cw, lambda w, k, kk, t=t, m=m: (x[:, kk, t:t + m], w[:, k, c:c + cw]), by,
               lambda eng, ps, t=t // P: read(eng, ps, t, c0))


def copy_to(core, dst):
    def read(eng, ps, ch, t0, t1):
        to = dst[0:ps.shape[0], ch, t0:t1]
        if eng == "act":
            return core.nc.scalar.copy(to, ps)
        return core.nc.vector.tensor_copy(to, ps)
    return read


def root(core, out, sums, n, eps):
    return core.nc.scalar.activation(out, sums, ACT.Sqrt, scale=1.0 / n, bias=core.eps[eps][0:out.shape[0]])


def rms_norm(core, x, kc, tokens, squares, out, gain, n, eps=1e-6, shift=None, post=None, squared=False):
    nc, ones, sp_ = core.nc, core.c("common", "ones"), splits_of(tokens)
    rstd = core.rstd[:, 0:tokens]
    with core.stage() as block:
        @block.scalar
        def _(act):
            for k in range(0 if squared else kc):
                nc.scalar.activation(squares[:, k, 0:tokens], x[:, k, 0:tokens], ACT.Square).then_inc(core.a2p.sem, core.a2p.add(1))
            act.wait_ge(core.p2a.sem, core.p2a.at(1))
            for s, (a, b) in enumerate(sp_):
                root(core, rstd[:, a:b], core.bank[s][:, 0:b - a], n, eps).then_inc(core.a2v.sem, core.a2v.add(1))
            if shift is not None:
                for k in range(kc):
                    act.wait_ge(core.v2a.sem, core.v2a.at(k + 1))
                    nc.scalar.activation(out[:, k, 0:tokens], out[:, k, 0:tokens], ACT.Identity, bias=shift(k))

        @block.tensor
        def _(pe):
            for k in range(kc):
                if not squared:
                    pe.wait_ge(core.a2p.sem, core.a2p.at(k + 1))
                for s, (a, b) in enumerate(sp_):
                    mm = nc.tensor.matmul(core.bank[s][:, 0:b - a], ones, squares[:, k, a:b], start=k == 0, stop=k == kc - 1)
            mm.then_inc(core.p2a.sem, core.p2a.add(1))

        @block.vector
        def _(dve):
            step = Chain(dve, core.dve_step)
            dve.wait_ge(core.a2v.sem, core.a2v.at(len(sp_)))
            step(nc.vector.reciprocal(rstd, rstd))
            for k in range(kc):
                nc.vector.scalar_tensor_tensor(out=out[:, k, 0:tokens], in0=x[:, k, 0:tokens], scalar=gain(k),
                                                            in1=rstd, op0=ALU.mult, op1=ALU.mult).then_inc(core.v2a.sem, core.v2a.add(1))
                if post is not None:
                    dve.wait_ge(core.v2a.sem, core.v2a.at(core.v2a.sent))
                    post(k)


def head_norm(core, x, chunks, tokens, squares, lhs, n, eps, gain, out, mean=False):
    nc, sp_ = core.nc, splits_of(tokens)
    per = len(sp_)
    roots = [core.work[:, 512 * i:512 * i + 512] for i in range(2)]
    with core.stage() as block:
        @block.scalar
        def _(act):
            for c in range(chunks):
                nc.scalar.activation(squares[:, c, 0:tokens], x[:, c, 0:tokens], ACT.Square).then_inc(core.a2p.sem, core.a2p.add(1))
            for g in range(chunks * per):
                a, b = sp_[g % per]
                act.wait_ge(core.p2a.sem, core.p2a.at(g + 1))
                if g >= 2:
                    act.wait_ge(core.v2p.sem, core.v2p.at(g - 1))
                root(core, roots[g % 2][:, 0:b - a], core.bank[g % BANKS][:, 0:b - a], n, eps).then_inc(core.a2v.sem, core.a2v.add(1))

        @block.tensor
        def _(pe):
            for c in range(chunks):
                pe.wait_ge(core.a2p.sem, core.a2p.at(c + 1))
                for s, (a, b) in enumerate(sp_):
                    g = c * per + s
                    if g >= BANKS:
                        pe.wait_ge(core.v2p.sem, core.v2p.at(g - BANKS + 1))
                    nc.tensor.matmul(core.bank[g % BANKS][:, 0:b - a], lhs, squares[:, c, a:b], start=True, stop=True).then_inc(core.p2a.sem, core.p2a.add(1))

        @block.vector
        def _(dve):
            step = Chain(dve, core.dve_step)
            for c in range(chunks):
                for s, (a, b) in enumerate(sp_):
                    g = c * per + s
                    r = roots[g % 2][:, 0:b - a]
                    dve.wait_ge(core.a2v.sem, core.a2v.at(g + 1))
                    step(nc.vector.reciprocal(r, r))
                    ins = nc.vector.scalar_tensor_tensor(out=out[:, c, a:b], in0=x[:, c, a:b], scalar=gain(c),
                                                         in1=r, op0=ALU.mult, op1=ALU.mult)
                    ins.then_inc(core.v2p.sem, core.v2p.add(1))
                    dve.wait_ge(core.v2p.sem, core.v2p.at(core.v2p.sent))


def rope(core, x, chunks, tokens, rot, cos, sin, rows=P):
    nc, sp_ = core.nc, splits_of(tokens)
    per = len(sp_)
    tmp = core.work[:, 0:2 * 512].rearrange("p (b n) -> p b n", b=2)
    with core.stage() as block:
        @block.tensor
        def _(pe):
            for c in range(chunks):
                for s, (a, b) in enumerate(sp_):
                    g = c * per + s
                    if g >= BANKS:
                        pe.wait_ge(core.v2p.sem, core.v2p.at(g - BANKS + 1))
                    nc.tensor.matmul(core.bank[g % BANKS][0:rows, 0:b - a], rot, x[0:rows, c, a:b], start=True, stop=True).then_inc(core.p2v.sem, core.p2v.add(1))

        @block.vector
        def _(dve):
            step = Chain(dve, core.dve_step)
            for c in range(chunks):
                for s, (a, b) in enumerate(sp_):
                    g = c * per + s
                    t = tmp[0:rows, g % 2, 0:b - a]
                    dve.wait_ge(core.p2v.sem, core.p2v.at(g + 1))
                    nc.vector.tensor_tensor(t, core.bank[g % BANKS][0:rows, 0:b - a], sin[0:rows, a:b], ALU.mult).then_inc(core.v2p.sem, core.v2p.add(1))
                    dve.wait_ge(core.v2p.sem, core.v2p.at(core.v2p.sent))
                    step(nc.vector.tensor_tensor(x[0:rows, c, a:b], x[0:rows, c, a:b], cos[0:rows, a:b], ALU.mult))
                    step(nc.vector.tensor_tensor(x[0:rows, c, a:b], x[0:rows, c, a:b], t, ALU.add))


def exchange_halves(core, x, out, chunks, tokens):
    nc, sp_ = core.nc, splits_of(tokens)
    with core.stage() as block:
        @block.tensor
        def _(pe):
            for c in range(chunks):
                for s, (a, b) in enumerate(sp_):
                    nc.tensor.matmul(core.bank[c * len(sp_) + s][:, 0:b - a], core.c("common", "swap"), x[:, c, a:b],
                                                  start=True, stop=True).then_inc(core.p2v.sem, core.p2v.add(1))

        @block.vector
        def _(dve):
            for c in range(chunks):
                for s, (a, b) in enumerate(sp_):
                    g = c * len(sp_) + s
                    dve.wait_ge(core.p2v.sem, core.p2v.at(g + 1))
                    nc.vector.tensor_copy(out[:, c, a:b], core.bank[g][:, 0:b - a])


def load(core, pairs):
    with core.stage() as block:
        @block.sync
        def _(sp):
            for dst, src in pairs:
                sp.dma_start(dst, src).then_inc(core.loaded.sem, core.loaded.add(16))
            core.issue_weights(sp, core.done)
            sp.wait_ge(core.loaded.sem, core.loaded.at(16 * len(pairs)))


def attention(core, units, scale, scores_at, probs_at, wide=640):
    nc, ident = core.nc, core.c("common", "ident")
    n = len(units)
    row = [scores_at[:, wide * i:wide * (i + 1)] for i in range(3)]
    prob = [probs_at[:, wide * i:wide * (i + 1)] for i in range(2)]
    stat = [core.small[:, 8 * i:8 * i + 8] for i in range(3)]
    s_ready, s_read, m_ready, e_ready, n_ready, t_ready, t_read, o_ready, o_read = (
        core.att[k] for k in ("s_ready", "s_read", "m_ready", "e_ready", "n_ready", "t_ready", "t_read", "o_ready", "o_read"))
    with core.stage() as block:
        @block.tensor
        def _(pe):
            def scores(i):
                m, segs = units[i][0], units[i][1]
                if i >= 2:
                    pe.wait_ge(s_read.sem, s_read.at(i - 1))
                for s, (products, cols, _) in enumerate(segs):
                    for j, (lhsT, rhs) in enumerate(products):
                        mm = nc.tensor.matmul(core.bank[2 * (i % 2) + s][0:m, 0:cols], lhsT, rhs, start=j == 0,
                                              stop=j == len(products) - 1)
                mm.then_inc(s_ready.sem, s_ready.add(1))

            def turn(i):
                m, blocks = units[i][0], units[i][2]
                pe.wait_ge(n_ready.sem, n_ready.at(i + 1))
                if i >= 1:
                    pe.wait_ge(t_read.sem, t_read.at(i))
                for b, (_, kp) in enumerate(blocks):
                    out = core.bank[4 + b // 4][0:kp, (b % 4) * P:(b % 4) * P + m]
                    mm = nc.tensor.transpose(out, row[i % 3][0:m, b * P:b * P + kp], ident[0:m, 0:m])
                mm.then_inc(t_ready.sem, t_ready.add(1))

            def values(i):
                m, _, blocks, dv, po = units[i][:5]
                pe.wait_ge(t_read.sem, t_read.at(i + 1))
                if i >= 2:
                    pe.wait_ge(o_read.sem, o_read.at(i - 1))
                for b, (v, kp) in enumerate(blocks):
                    mm = nc.tensor.matmul(core.bank[6 + i % 2][po:po + dv, 0:m], v, prob[i % 2][0:kp, b * P:b * P + m],
                                          start=b == 0, stop=b == len(blocks) - 1)
                mm.then_inc(o_ready.sem, o_ready.add(1))

            scores(0)
            scores(1)
            for i in range(n):
                if i + 2 < n:
                    scores(i + 2)
                turn(i)
                if i >= 1:
                    values(i - 1)
            values(n - 1)

        @block.vector
        def _(dve):
            step = Chain(dve, core.dve_step)

            def take(i):
                m, segs, _, _, _, _, sink = units[i]
                dve.wait_ge(s_ready.sem, s_ready.at(i + 1))
                if i >= 3:
                    dve.wait_ge(t_ready.sem, t_ready.at(i - 2))
                at = 0
                for s, (_, cols, mask) in enumerate(segs):
                    to, ps = row[i % 3][0:m, at:at + cols], core.bank[2 * (i % 2) + s][0:m, 0:cols]
                    ins = nc.vector.tensor_tensor(to, ps, mask, ALU.add) if mask is not None else nc.vector.tensor_copy(to, ps)
                    at += cols
                ins.then_inc(s_read.sem, s_read.add(1))
                dve.wait_ge(s_read.sem, s_read.at(s_read.sent))
                st = stat[i % 3]
                step(nc.vector.reduce_max(st[0:m, 0:1], row[i % 3][0:m, 0:at], AX.X))
                if sink is None:
                    nc.vector.tensor_scalar(st[0:m, 1:2], st[0:m, 0:1], -scale, None, ALU.mult).then_inc(m_ready.sem, m_ready.add(1))
                else:
                    step(nc.vector.tensor_scalar(st[0:m, 2:3], st[0:m, 0:1], scale, sink[0:m], ALU.mult, ALU.max))
                    nc.vector.tensor_scalar(st[0:m, 1:2], st[0:m, 2:3], -1.0, None, ALU.mult).then_inc(m_ready.sem, m_ready.add(1))

            def normalise(i):
                m, segs, _, _, _, _, sink = units[i]
                cols = sum(s[1] for s in segs)
                st = stat[i % 3]
                dve.wait_ge(e_ready.sem, e_ready.at(i + 1))
                if sink is not None:
                    step(nc.vector.tensor_tensor(st[0:m, 3:4], st[0:m, 3:4], st[0:m, 4:5], ALU.add))
                step(nc.vector.reciprocal(st[0:m, 5:6], st[0:m, 3:4]))
                nc.vector.tensor_scalar(row[i % 3][0:m, 0:cols], row[i % 3][0:m, 0:cols], st[0:m, 5:6], None, ALU.mult).then_inc(n_ready.sem, n_ready.add(1))

            def keep(i):
                m, _, _, dv, po, dest, _ = units[i]
                dve.wait_ge(o_ready.sem, o_ready.at(i + 1))
                nc.vector.tensor_copy(dest, core.bank[6 + i % 2][po:po + dv, 0:m]).then_inc(o_read.sem, o_read.add(1))

            take(0)
            take(1)
            normalise(0)
            for i in range(n):
                if i + 2 < n:
                    take(i + 2)
                if i + 1 < n:
                    normalise(i + 1)
                if i >= 2:
                    keep(i - 2)
            keep(n - 2)
            keep(n - 1)

        @block.scalar
        def _(act):
            def exponentials(i):
                m, segs, _, _, _, _, sink = units[i]
                cols = sum(s[1] for s in segs)
                st, r = stat[i % 3], row[i % 3]
                act.wait_ge(m_ready.sem, m_ready.at(i + 1))
                if sink is not None:
                    nc.scalar.activation(st[0:m, 4:5], sink[0:m], ACT.Exp, bias=st[0:m, 1:2])
                nc.scalar.activation(r[0:m, 0:cols], r[0:m, 0:cols], ACT.Exp, bias=st[0:m, 1:2], scale=scale,
                                                 accum_out=st[0:m, 3:4]).then_inc(e_ready.sem, e_ready.add(1))

            def copy_turned(i):
                m, blocks = units[i][0], units[i][2]
                act.wait_ge(t_ready.sem, t_ready.at(i + 1))
                if i >= 2:
                    act.wait_ge(o_ready.sem, o_ready.at(i - 1))
                for b, (_, kp) in enumerate(blocks):
                    if b == 0 or b == 4 or kp < P:
                        run = 1
                        while kp == P and b + run < min(len(blocks), 4 * (b // 4 + 1)) and blocks[b + run][1] == P and m == P:
                            run += 1
                        lo = (b % 4) * P
                        ins = nc.scalar.copy(prob[i % 2][0:kp, b * P:(b + run - 1) * P + m], core.bank[4 + b // 4][0:kp, lo:lo + (run - 1) * P + m])
                    elif m < P:
                        lo = (b % 4) * P
                        ins = nc.scalar.copy(prob[i % 2][0:kp, b * P:b * P + m], core.bank[4 + b // 4][0:kp, lo:lo + m])
                ins.then_inc(t_read.sem, t_read.add(1))

            exponentials(0)
            for i in range(n):
                if i + 1 < n:
                    exponentials(i + 1)
                copy_turned(i)


def first_block(core):
    nc, dram = core.nc, core.dram
    X, H, S2, S3, S4, S5, S6 = [s[:, :].rearrange("p (k t) -> p k t", k=KC) for s in core.slab]
    x, h = X[:, :, META:], H[:, :, 0:SEQ]
    flat = [s[:, :] for s in core.slab]
    ones, ident = core.c("common", "ones"), core.c("common", "ident")
    core.use_params("p1")
    cols = lambda name, i0, i1: core.param[:, core.pcols[name] + i0:core.pcols[name] + i1]

    consts = first_constants()
    where, width = columns(consts)
    core.place("first", consts, core.area)
    grid = grid_tables()
    ctx_x = S2[:, :, 0:CTX]
    with core.stage() as block:
        @block.sync
        def _(sp):
            pairs = [(core.common[:, :], dram["common"]), (core.area[:, 0:width], dram["first"]), (core.param[:, :], dram["p1"]),
                     (x, dram["x"]), (ctx_x, dram["ctx"])]
            for dst, src in pairs:
                sp.dma_start(dst, src).then_inc(core.loaded.sem, core.loaded.add(16))
            core.issue_weights(sp, 0)
            sp.wait_ge(core.loaded.sem, core.loaded.at(16 * len(pairs)))

        @block.vector
        def _(dve):
            for e, at in core.eps.items():
                nc.vector.memset(at, e)

    cc = core.small[:, 0:16]
    with core.stage() as block:
        @block.scalar
        def _(act):
            nc.scalar.activation(cc, cols("cc", 0, 16), ACT.Silu)
    silu_c = cc.rearrange("p (k j) -> p k j", j=2)
    bada = cols("b_ada", 0, 48)
    rows = core.slabs[0:2, 3 * core.slab_cols:3 * core.slab_cols + 6 * D]
    run_groups(core, "ada", lambda c0, cw: [(2, cw, lambda w, k, kk: (silu_c[:, kk, :], w[:, k, 0:cw]), "act",
                                             lambda eng, ps: nc.scalar.copy(rows[:, c0:c0 + cw], ps))])
    with core.stage() as block:
        @block.tensor
        def _(pe):
            for j in range(6 * KC):
                last = nc.tensor.transpose(core.bank[0][:, 2 * j:2 * j + 2], rows[:, j * P:(j + 1) * P], ident[0:2, 0:2])
            last.then_inc(core.p2v.sem, core.p2v.add(1))

        @block.vector
        def _(dve):
            dve.wait_ge(core.p2v.sem, core.p2v.at(1))
            nc.vector.tensor_tensor(core.mod[:, :, :], core.bank[0][:, 0:12 * KC].rearrange("p (j i) -> p j i", i=2),
                                    bada.unsqueeze(2).broadcast_to([P, 6 * KC, 2]), ALU.add)
    with core.stage() as block:
        @block.vector
        def _(dve):
            for at, j, chunk, gain in ((0, 0, 8, "g1"), (8, 1, 8, "g1"), (16, 0, 32, "g2")):
                nc.vector.scalar_tensor_tensor(out=core.gains[:, at:at + 8], in0=core.mod[:, chunk:chunk + 8, j], scalar=1.0,
                                               in1=cols(gain, 0, 8), op0=ALU.add, op1=ALU.mult)
    gain = lambda at: (lambda k: core.gains[:, at + k:at + k + 1])
    shift = lambda chunk, j: (lambda k: core.mod[:, chunk + k, j:j + 1])

    hc = S2[:, :, 264:264 + CTX]
    rms_norm(core, x, KC, SEQ, S3, h, gain(0), D, shift=shift(0, 0))
    rms_norm(core, ctx_x, KC, CTX, S3, hc, gain(8), D, shift=shift(0, 1))

    kT = S3[:, 0:2, 0:SEQ]
    kS = S3[:, 2:4, 0:SEQ]
    kcT, kcS = S3[:, 4:6, 0:CTX], S3[:, 6:8, 0:CTX]
    v = S3[:, 4:6, 264:264 + CTX]
    vtok = flat[4][:, 0:4 * CTX].rearrange("p (t c) -> p t c", t=4)
    vctx = flat[4][:, 4 * CTX:6 * CTX].rearrange("p (t c) -> p t c", t=2)

    def kv_groups(c0, cw):
        for c in range(2):
            for src, n, dst in ((h, SEQ, kT), (hc, CTX, kcT)):
                yield (P, n, lambda w, k, kk, c=c, src=src, n=n: (w[:, k, c * P:(c + 1) * P], src[:, kk, 0:n]), "act",
                       lambda eng, ps, c=c, n=n, dst=dst: nc.scalar.copy(dst[:, c, 0:n], ps))
        for src, n, dst in ((h, SEQ, vtok), (hc, CTX, vctx)):
            yield from token_groups(src, n, 2 * P, CTX, lambda eng, ps, t, c0, dst=dst: nc.vector.tensor_copy(dst[:, t, :], ps), "dve")
    run_groups(core, "kv", kv_groups)

    q = S5[:, :, 0:SEQ]
    dense(core, "q", h, SEQ, copy_to(core, q))
    cos, sin = core.c("first", "cos")[:, META:], core.c("first", "sin")[:, META:]
    rope(core, q, KC, SEQ, core.c("common", "rot16"), cos, sin)
    rope(core, kT, 2, SEQ, core.c("common", "rot16"), cos, sin)
    exchange_halves(core, kT, kS, 2, SEQ)
    exchange_halves(core, kcT, kcS, 2, CTX)

    yb = S6[:, :, 0:SEQ]
    window = core.c("first", "window")
    units = []
    for head in range(16):
        kv, po = head // 4, 64 * (head % 2)
        same = head % 2 == kv % 2
        keys, ckeys = (kT, kcT) if same else (kS, kcS)
        rows = slice(po, po + 64)
        for n in range(4):
            lo, hi = max(n - 1, 0), min(n + 1, 3)
            query = q[rows, head // 2, n * P:(n + 1) * P]
            segs = [([(query, keys[rows, kv // 2, lo * P:(hi + 1) * P])], (hi + 1 - lo) * P, window[:, (lo - n + 1) * P:(hi - n + 2) * P]),
                    ([(query, ckeys[rows, kv // 2, :])], CTX, None)]
            blocks = [(vtok[:, b, kv * 64:kv * 64 + 64], P) for b in range(lo, hi + 1)] + \
                     [(vctx[:, b, kv * 64:kv * 64 + 64], P) for b in range(2)]
            units.append((P, segs, blocks, 64, po, yb[rows, head // 2, n * P:(n + 1) * P], core.col("sink", head)))
    attention(core, units, 64 ** -0.5, flat[2], flat[4][:, 6 * CTX:6 * CTX + 1280])

    va = flat[2][:, 0:4 * D].rearrange("p (t c) -> p t c", t=4)
    u = S3[:, :, 0:SEQ]
    tables = flat[4]
    gB, bB, bsB = tables[:, 0:D], tables[:, D:2 * D], tables[:, 2 * D:3 * D]
    scratch = tables[:, 3 * D:4 * D]
    ws = flat[5][:, 0:D].rearrange("p (g q) -> p g q", g=8)
    load(core, [(gB, dram["gmlp_ln_g"].partition_broadcast(P)), (bB, dram["gmlp_ln_b"].partition_broadcast(P)),
                (bsB, dram["b_spatial"].partition_broadcast(P)), (ws, dram["w_spatial"])])
    sums = core.small[:, 16:24]
    run_groups(core, "va", lambda c0, cw: token_groups(h, SEQ, 0, cw, lambda eng, ps, t, c0: nc.scalar.activation(
        va[:, t, c0:c0 + SLOT_COLS], ps, ACT.Gelu_apprx_tanh,
        accum_out=sums[:, 2 * t + c0 // SLOT_COLS:2 * t + c0 // SLOT_COLS + 1]), "act", c0))
    dense(core, "u", h, SEQ, lambda eng, ps, ch, t0, t1: nc.scalar.activation(u[:, ch, t0:t1], ps, ACT.Gelu_apprx_tanh))
    mean, var = core.small[:, 24:28], core.small[:, 28:32]
    with core.stage() as block:
        @block.vector
        def _(dve):
            step = Chain(dve, core.dve_step)
            s3 = sums.rearrange("p (t j) -> p t j", j=2)
            step(nc.vector.tensor_tensor(mean, s3[:, :, 0], s3[:, :, 1], ALU.add))
            step(nc.vector.tensor_scalar(mean, mean, 1.0 / D, None, ALU.mult))
            for t in range(4):
                nc.vector.tensor_scalar(va[:, t, :], va[:, t, :], mean[:, t:t + 1], None, ALU.subtract).then_inc(core.v2a.sem, core.v2a.add(1))
            dve.wait_ge(core.a2v.sem, core.a2v.at(5))
            step(nc.vector.reciprocal(var, var))
            for t in range(4):
                step(nc.vector.scalar_tensor_tensor(out=va[:, t, :], in0=va[:, t, :], scalar=var[:, t:t + 1], in1=gB,
                                                    op0=ALU.mult, op1=ALU.mult))
                nc.vector.tensor_tensor(va[:, t, :], va[:, t, :], bB, ALU.add).then_inc(core.v2p.sem, core.v2p.add(1))
            for g in range(8):
                dve.wait_ge(core.p2v.sem, core.p2v.at(g + 1))
                mixed = scratch[:, 0:SEQ].rearrange("p (n q) -> p n q", n=4)
                step(nc.vector.tensor_tensor(mixed, core.bank[g][:, :].rearrange("p (n q) -> p n q", n=4),
                                             bsB[:, g * P:(g + 1) * P].unsqueeze(1).broadcast_to([P, 4, P]), ALU.add))
                step(nc.vector.tensor_tensor(u[:, g, :], u[:, g, :], scratch[:, 0:SEQ], ALU.mult))

        @block.scalar
        def _(act):
            for t in range(4):
                act.wait_ge(core.v2a.sem, core.v2a.at(t + 1))
                nc.scalar.activation(flat[5][:, D:2 * D], va[:, t, :], ACT.Square, accum_out=var[:, t:t + 1]).then_inc(core.a2v.sem, core.a2v.add(1))
                act.wait_ge(core.a2v.sem, core.a2v.at(core.a2v.sent))
            root(core, var, var, D, 1e-6).then_inc(core.a2v.sem, core.a2v.add(1))

        @block.tensor
        def _(pe):
            pe.wait_ge(core.v2p.sem, core.v2p.at(4))
            for g in range(8):
                for n in range(4):
                    mm = nc.tensor.matmul(core.bank[g][:, n * P:(n + 1) * P], va[:, n, g * P:(g + 1) * P], ws[:, g, :], start=True, stop=True)
                mm.then_inc(core.p2v.sem, core.p2v.add(1))

    bg = cols("b_gate", 0, 16)
    merge_branches(core, h, SEQ, [("ga", "pa", u, 0), ("gb", "pb", yb, 8)], S4[:, :, 0:SEQ], S5[:, :, 0:SEQ],
                   lambda i: bg[:, i:i + 1])
    dense(core, "wo", S4[:, :, 0:SEQ], SEQ, lambda eng, ps, ch, t0, t1: nc.vector.scalar_tensor_tensor(
        out=x[:, ch, t0:t1], in0=ps, scalar=core.mod[:, 16 + ch, 0:1], in1=x[:, ch, t0:t1], op0=ALU.mult, op1=ALU.add), by="dve",
          also=also_square(core, S2, x, SEQ, "dve"))
    rms_norm(core, x, KC, SEQ, S2, h, gain(16), D, shift=shift(24, 0), squared=True)
    expert_choice(core, x, h)
    rms_norm(core, x, KC, SEQ, S2, x, lambda k: core.col("final", k), D)


def merge_branches(core, h, tokens, branches, merged, gate, bias):
    nc = core.nc
    for i, (gname, pname, y, g0) in enumerate(branches):
        dense(core, gname, h, tokens, lambda eng, ps, ch, t0, t1: nc.scalar.activation(
            gate[:, ch, t0:t1], ps, ACT.Sigmoid, bias=0.0 if bias is None else bias(g0 + ch)))

        def join(eng, ps, ch, t0, t1):
            if i == 0:
                return nc.vector.tensor_tensor(merged[:, ch, t0:t1], ps, gate[:, ch, t0:t1], ALU.mult)
            nc.vector.tensor_tensor(gate[:, ch, t0:t1], ps, gate[:, ch, t0:t1], ALU.mult).then_inc(core.dve_step.sem, core.dve_step.add(1))
            nc.vector.wait_ge(core.dve_step.sem, core.dve_step.at(core.dve_step.sent))
            return nc.vector.tensor_tensor(merged[:, ch, t0:t1], merged[:, ch, t0:t1], gate[:, ch, t0:t1], ALU.add)
        dense(core, pname, y, tokens, join, by="dve")


def expert_choice(core, x, h):
    nc, dram = core.nc, core.dram
    flat = [s[:, :] for s in core.slab]
    ones, ident = core.c("common", "ones"), core.c("common", "ident")
    earlier, iota = core.c("first", "earlier"), core.c("first", "iota")
    htok = flat[2][:, 0:4 * D].rearrange("p (t c) -> p t c", t=4)
    wr = core.work[:, 0:P].rearrange("p (k e) -> p k e", k=KC)
    aff = core.work[:, 128:192].rearrange("p (t e) -> p t e", t=4)
    chosen = core.work[:, 192:256].rearrange("p (t e) -> p t e", t=4)
    rank = core.work[:, 256:320].rearrange("p (t e) -> p t e", t=4)
    tmax = core.work[:, 320:336]
    by_expert = core.work[0:EXPERTS, 512:1024]
    left = core.work[0:EXPERTS, 1024:1536]
    best = core.work[0:EXPERTS, 1536:1544]
    load(core, [(wr, dram["w_router"].rearrange("(k p) e -> p k e", p=P))])
    lb = core.bank[0][:, 0:64].rearrange("p (t e) -> p t e", t=4)
    with core.stage() as block:
        @block.tensor
        def _(pe):
            for t in range(4):
                for k in range(KC):
                    mm = nc.tensor.matmul(lb[:, t, :], h[:, k, t * P:(t + 1) * P], wr[:, k, :], start=k == 0, stop=k == KC - 1)
            mm.then_inc(core.p2v.sem, core.p2v.add(1))
            for t in range(4):
                for half in range(2):
                    b = 1 + (2 * t + half) % 4
                    if 2 * t + half >= 4:
                        pe.wait_ge(core.a2p.sem, core.a2p.at(2 * t + half - 3))
                    for c in range(4):
                        mm = nc.tensor.transpose(core.bank[b][:, c * P:(c + 1) * P], h[:, 4 * half + c, t * P:(t + 1) * P], ident)
                    mm.then_inc(core.p2a.sem, core.p2a.add(1))
            pe.wait_ge(core.v2p.sem, core.v2p.at(1))
            for t in range(4):
                mm = nc.tensor.transpose(core.bank[5][0:EXPERTS, t * P:(t + 1) * P], aff[:, t, :], ident)
            mm.then_inc(core.p2v.sem, core.p2v.add(1))
            pe.wait_ge(core.v2p.sem, core.v2p.at(2))
            for t in range(4):
                mm = nc.tensor.transpose(core.bank[6][:, t * EXPERTS:(t + 1) * EXPERTS], by_expert[:, t * P:(t + 1) * P], ident[0:EXPERTS, 0:EXPERTS])
            mm.then_inc(core.p2v.sem, core.p2v.add(1))
            pe.wait_ge(core.v2p.sem, core.v2p.at(3))
            for t in range(4):
                for s in range(t + 1):
                    mm = nc.tensor.matmul(core.bank[7][:, t * EXPERTS:(t + 1) * EXPERTS], earlier if s == t else ones, chosen[:, s, :],
                                          start=s == 0, stop=s == t)
            mm.then_inc(core.p2v.sem, core.p2v.add(1))

        @block.scalar
        def _(act):
            for g in range(8):
                act.wait_ge(core.p2a.sem, core.p2a.at(g + 1))
                nc.scalar.copy(htok[:, g // 2, (g % 2) * 512:(g % 2) * 512 + 512], core.bank[1 + g % 4][:, :]).then_inc(core.a2p.sem, core.a2p.add(1))
            act.wait_ge(core.v2a.sem, core.v2a.at(1))
            nc.scalar.activation(aff, aff, ACT.Exp).then_inc(core.a2v.sem, core.a2v.add(1))

        @block.vector
        def _(dve):
            step = Chain(dve, core.dve_step)
            dve.wait_ge(core.p2v.sem, core.p2v.at(1))
            step(nc.vector.tensor_reduce(tmax[:, 0:4], lb, AX.X, ALU.max))
            nc.vector.tensor_tensor(aff, lb, tmax[:, 0:4].unsqueeze(2).broadcast_to([P, 4, EXPERTS]), ALU.subtract).then_inc(core.v2a.sem, core.v2a.add(1))
            dve.wait_ge(core.a2v.sem, core.a2v.at(1))
            step(nc.vector.tensor_reduce(tmax[:, 4:8], aff, AX.X, ALU.add))
            step(nc.vector.reciprocal(tmax[:, 8:12], tmax[:, 4:8]))
            nc.vector.tensor_tensor(aff, aff, tmax[:, 8:12].unsqueeze(2).broadcast_to([P, 4, EXPERTS]), ALU.mult).then_inc(core.v2p.sem, core.v2p.add(1))
            dve.wait_ge(core.p2v.sem, core.p2v.at(2))
            step(nc.vector.tensor_copy(left, core.bank[5][0:EXPERTS, :]))
            for r in range(CAP // 8):
                step(nc.vector.max(best, left))
                step(nc.vector.match_replace(left, best, left, -1.0))
            nc.vector.tensor_scalar(by_expert, left, 0.0, None, ALU.is_lt).then_inc(core.v2p.sem, core.v2p.add(1))
            dve.wait_ge(core.p2v.sem, core.p2v.at(3))
            nc.vector.tensor_copy(chosen, core.bank[6][:, 0:64].rearrange("p (t e) -> p t e", t=4)).then_inc(core.v2p.sem, core.v2p.add(1))
            dve.wait_ge(core.v2p.sem, core.v2p.at(3))
            dve.wait_ge(core.p2v.sem, core.p2v.at(4))
            step(nc.vector.tensor_scalar(rank, core.bank[7][:, 0:64].rearrange("p (t e) -> p t e", t=4), 1.0, None, ALU.add))
            step(nc.vector.tensor_tensor(rank, rank, chosen, ALU.mult))
            step(nc.vector.tensor_scalar(rank, rank, -1.0, None, ALU.add))

    onehot = flat[3][:, 0:4 * D].rearrange("p (t e s) -> p t e s", t=4, e=EXPERTS)
    xe = core.slabs[:, 4 * core.slab_cols:4 * core.slab_cols + 8 * D].rearrange("p (k s) -> p k s", k=KC)
    with core.stage() as block:
        @block.vector
        def _(dve):
            for t in range(4):
                nc.vector.tensor_tensor(onehot[:, t], iota.unsqueeze(1).broadcast_to([P, EXPERTS, CAP]),
                                                     rank[:, t, :].unsqueeze(2).broadcast_to([P, EXPERTS, CAP]), ALU.is_equal).then_inc(core.v2p.sem, core.v2p.add(1))
            dve.wait_ge(core.p2a.sem, core.p2a.at(16))
            for t in range(4):
                nc.vector.tensor_tensor(onehot[:, t], onehot[:, t], aff[:, t, :].unsqueeze(2).broadcast_to([P, EXPERTS, CAP]), ALU.mult).then_inc(core.v2p.sem, core.v2p.add(1))

        @block.tensor
        def _(pe):
            for t in range(4):
                pe.wait_ge(core.v2p.sem, core.v2p.at(t + 1))
            g = 0
            for c in range(KC):
                for half in range(2):
                    if g >= BANKS:
                        pe.wait_ge(core.a2p.sem, core.a2p.at(g - BANKS + 1))
                    for t in range(4):
                        mm = nc.tensor.matmul(core.bank[g % BANKS][:, :], htok[:, t, c * P:(c + 1) * P],
                                              flat[3][:, t * D + half * 512:t * D + half * 512 + 512], start=t == 0, stop=t == 3)
                    mm.then_inc(core.p2a.sem, core.p2a.add(1))
                    g += 1
            pe.wait_ge(core.v2p.sem, core.v2p.at(8))
            for pair in range(8):
                if g >= BANKS:
                    pe.wait_ge(core.a2p.sem, core.a2p.at(g - BANKS + 1))
                for t in range(4):
                    mm = nc.tensor.transpose(core.bank[g % BANKS][:, t * P:(t + 1) * P], flat[3][:, t * D + pair * P:t * D + (pair + 1) * P], ident)
                mm.then_inc(core.p2a.sem, core.p2a.add(1))
                g += 1

        @block.scalar
        def _(act):
            for g in range(16):
                act.wait_ge(core.p2a.sem, core.p2a.at(g + 1))
                nc.scalar.copy(xe[:, g // 2, (g % 2) * 512:(g % 2 + 1) * 512], core.bank[g % BANKS][:, :]).then_inc(core.a2p.sem, core.a2p.add(1))
            for pair in range(8):
                act.wait_ge(core.p2a.sem, core.p2a.at(16 + pair + 1))
                nc.scalar.copy(flat[2][:, pair * 512:(pair + 1) * 512], core.bank[(16 + pair) % BANKS][:, :]).then_inc(core.a2p.sem, core.a2p.add(1))

    y = [flat[3][:, 0:4 * D].rearrange("p (e c) -> p e c", e=8), flat[1][:, 0:4 * D].rearrange("p (e c) -> p e c", e=8)]
    experts(core, xe, y)

    with core.stage() as block:
        @block.tensor
        def _(pe):
            for ch in range(KC):
                for pair in range(8):
                    mm = nc.tensor.matmul(core.bank[ch][:, :], y[ch // 4][:, pair, (ch % 4) * P:(ch % 4 + 1) * P],
                                          flat[2][:, pair * 512:(pair + 1) * 512], start=pair == 0, stop=pair == 7)
                mm.then_inc(core.p2v.sem, core.p2v.add(1))

        @block.vector
        def _(dve):
            for ch in range(KC):
                dve.wait_ge(core.p2v.sem, core.p2v.at(ch + 1))
                nc.vector.scalar_tensor_tensor(out=x[:, ch, :], in0=core.bank[ch][:, :], scalar=core.mod[:, 40 + ch, 0:1],
                                               in1=x[:, ch, :], op0=ALU.mult, op1=ALU.add)


def experts(core, xe, y):
    nc, dram = core.nc, core.dram
    ident = core.c("common", "ident")
    flat = [s[:, :] for s in core.slab]
    TILES, PAIRS, CREDIT = 12, EXPERTS // 2, 2
    n0 = core.expert_tile
    xcur = [flat[6][:, 512 * i:512 * (i + 1)].rearrange("p (k s) -> p k s", k=KC) for i in range(2)]
    sg = [flat[6][0:CAP, 1024 + 512 * i:1536 + 512 * i] for i in range(2)]
    hid = [core.work[:, 512 * i:512 * i + 512] for i in range(2)]
    hT = [flat[6][:, 2048 + 1024 * i:3072 + 1024 * i].rearrange("p (f s) -> p f s", s=CAP) for i in range(2)]
    pairs = {k: dram[k].rearrange("(a s) k c -> a s k c", s=2) for k in ("w_gate", "w_up", "w_down")}
    used, moe = core.weight_used, core.moe
    G, U, T, Y = core.bank[0:2], core.bank[2:4], core.bank[4:6], core.bank[6:8]
    slot = lambda j: (n0 + j) % SLOTS

    def at_least(engine, raised, pair, per, n):
        engine.wait_ge(raised.sem, pair * per + (n + CREDIT))

    with core.stage() as block:
        @block.sync
        def _(sp):
            def issue(pair, s, j):
                if j < 8:
                    w = pairs[("w_gate", "w_up")[j % 2]]
                    src = w[bass.ds(pair, 1), s, :, (j // 2) * 512:(j // 2 + 1) * 512]
                else:
                    rows, half = (j - 8) // 2, (j - 8) % 2
                    src = pairs["w_down"][bass.ds(pair, 1), s, rows * D:(rows + 1) * D, half * 512:(half + 1) * 512]
                sp.wait_ge(used.sem, pair * (2 * TILES) + (n0 + s * TILES + j - SLOTS + 1))
                sp.dma_start(core.ring[slot(j)][:, :, :], src.rearrange("a (k p) c -> p (a k) c", p=P)).then_inc(
                    core.weight_in[slot(j)].sem, 16)

            for j in range(SLOTS, TILES):
                issue(0, 0, j)
            for j in range(TILES):
                issue(0, 1, j)
            with sp.Fori(1, PAIRS) as pair:
                for s in range(2):
                    for j in range(TILES):
                        issue(pair, s, j)
            core.issued = n0 + EXPERTS * TILES
            core.done = n0 + EXPERTS * TILES
            core.issue_weights(sp, core.done)

        @block.tensor
        def _(pe):
            def product(pair, s, j, out, lhsT, first, last):
                pe.wait_ge(core.weight_in[slot(j)].sem, pair * (2 * TILES // SLOTS * 16) + 16 * ((n0 + s * TILES + j) // SLOTS + 1))
                for k in range(KC):
                    mm = nc.tensor.matmul(out, lhsT[:, k, :], core.ring[slot(j)][:, k, :], start=first and k == 0,
                                          stop=last and k == KC - 1)
                mm.then_inc(used.sem, 1)

            def turn(pair, s, h):
                at_least(pe, moe["hidden"], pair, 8, 4 * s + 2 * h + 2)
                at_least(pe, moe["turned_read"], pair, 4, 2 * s + h - 1)
                for c in range(4):
                    mm = nc.tensor.transpose(T[h][:, c * P:(c + 1) * P], hid[h][:, c * P:(c + 1) * P], ident)
                mm.then_inc(moe["turned"].sem, 1)

            with pe.Fori(0, PAIRS) as pair:
                for s in range(2):
                    at_least(pe, moe["fetched"], pair, 2, s + 1)
                    for f in range(4):
                        at_least(pe, moe["hidden"], pair, 8, 4 * s + f - 1)
                        product(pair, s, 2 * f, G[f % 2][0:CAP, :], xcur[s], True, True)
                        product(pair, s, 2 * f + 1, U[f % 2][0:CAP, :], xcur[s], True, True)
                        if f == 2:
                            turn(pair, s, 0)
                    at_least(pe, moe["result_read"], pair, 2, s - 1)
                    for rows in range(2):
                        if rows == 1:
                            turn(pair, s, 1)
                        at_least(pe, moe["turned_read"], pair, 4, 2 * s + rows + 1)
                        for half in range(2):
                            product(pair, s, 8 + 2 * rows + half, Y[half][64 * s:64 * s + CAP, :], hT[s][:, 8 * rows:8 * rows + 8, :],
                                    rows == 0, rows == 1)

        @block.scalar
        def _(act):
            def turned(pair, s, h):
                at_least(act, moe["turned"], pair, 4, 2 * s + h + 1)
                if h == 0:
                    at_least(act, moe["result_read"], pair, 2, s - 1)
                nc.scalar.copy(hT[s][:, 8 * h:8 * h + 8, :].rearrange("p (f c) s -> p c f s", f=2),
                               T[h][:, :].rearrange("p (c f s) -> p c f s", c=4, f=2)).then_inc(moe["turned_read"].sem, 1)

            act.sem_inc(moe["turned_read"].sem, CREDIT)
            act.sem_inc(moe["silu"].sem, CREDIT)
            with act.Fori(0, PAIRS) as pair:
                for s in range(2):
                    for f in range(4):
                        g = 4 * s + f
                        act.wait_ge(used.sem, pair * (2 * TILES) + (n0 + s * TILES + 2 * f + 1))
                        at_least(act, moe["hidden"], pair, 8, g - 1)
                        nc.scalar.activation(sg[f % 2], G[f % 2][0:CAP, :], ACT.Silu).then_inc(moe["silu"].sem, 1)
                        if f == 2:
                            turned(pair, s, 0)
                    turned(pair, s, 1)

        @block.vector
        def _(dve):
            dve.sem_inc(moe["fetched"].sem, CREDIT)
            dve.sem_inc(moe["hidden"].sem, CREDIT)
            dve.sem_inc(moe["result_read"].sem, CREDIT)
            with dve.Fori(0, PAIRS) as pair:
                for s in range(2):
                    dve.wait_ge(used.sem, pair * (2 * TILES) + (n0 + (s - 2) * TILES + 8))
                    nc.vector.tensor_copy(xcur[s], xe[:, :, bass.ds(pair * (2 * CAP) + s * CAP, CAP)]).then_inc(moe["fetched"].sem, 1)
                    for f in range(4):
                        g = 4 * s + f
                        dve.wait_ge(used.sem, pair * (2 * TILES) + (n0 + s * TILES + 2 * f + 2))
                        at_least(dve, moe["silu"], pair, 8, g + 1)
                        at_least(dve, moe["turned"], pair, 4, 2 * s + f // 2 - 1)
                        nc.vector.tensor_tensor(hid[f // 2][64 * (f % 2):64 * (f % 2) + CAP, :], sg[f % 2], U[f % 2][0:CAP, :], ALU.mult).then_inc(moe["hidden"].sem, 1)
                    dve.wait_ge(used.sem, pair * (2 * TILES) + (n0 + (s + 1) * TILES))
                    for half in range(2):
                        ins = nc.vector.tensor_copy(y[half][64 * s:64 * s + CAP, bass.ds(pair, 1), :],
                                                    Y[half][64 * s:64 * s + CAP, :].unsqueeze(1))
                    ins.then_inc(moe["result_read"].sem, 1)
            dve.wait_ge(moe["result_read"].sem, CREDIT + EXPERTS)

        @block.gpsimd
        def _(pool):
            pool.sem_inc(moe["turned"].sem, CREDIT)


RW, LORA = 512, 64
Q0, K0, G0 = 1952, 2464, 2720
DECAY_SCALE = -float(np.exp(-0.5))


def plan_second(core):
    d = core.dram
    core.plan("rwkv_in", d["w_in_2"], 0, Q0)
    core.plan("q2", d["w_in_2"], Q0, K0)
    core.plan("kv2", d["w_in_2"], K0, G0)
    core.plan("ga2", d["w_in_2"], G0, G0 + D)
    core.plan("pa2", d["w_branch_rwkv"], 0, D)
    core.plan("gb2", d["w_in_2"], G0 + D, G0 + 2 * D)
    core.plan("pb2", d["w_branch_attn"], 0, D)
    core.plan("wo2", d["w_out_2"], 0, D)
    core.plan("ff1", d["w_ff1"], 0, 4 * D)
    core.plan("ff2", d["w_ff2"], 0, D)


def laid_out_second(x, chunks):
    pad = lambda a: np.concatenate([a, np.zeros((2048 - a.shape[-1],), a.dtype)])
    twice = lambda a: np.concatenate([a[0], a[0]])
    mu = x["rwkv_shift_2"][0]
    p2 = [x["mix_norm_g_2"], pad(mu[0]), pad(mu[1]), x["decay_w0_2"], x["icl_a0_2"], x["k_k_2"], x["k_a_2"], x["r_k_2"],
          x["lnx_g_2"], x["lnx_b_2"], twice(x["q_norm_g_2"]), twice(x["k_norm_g_2"]), x["ffn_norm_g_2"], x["final_norm_g_2"]]
    return {
        "meta": np.ascontiguousarray(x["meta_tokens_2"].reshape(META, KC, P).transpose(2, 1, 0)),
        "w_in_2": x["w_in_2"][0], "w_branch_rwkv": x["w_branch_rwkv_2"][0], "w_branch_attn": x["w_branch_attn_2"][0],
        "w_out_2": x["w_out_2"][0], "w_ff1": x["w_ff1_2"][0], "w_ff2": x["w_ff2_2"][0],
        "decay_w2": x["decay_w2_2"][0].reshape(P, RW), "icl_a2": x["icl_a2_2"][0].reshape(P, RW), "gate_w2": x["gate_w2_2"][0],
        "p2": np.ascontiguousarray(np.concatenate([chunks(a) for a in p2], 1)),
        "second": packed(second_constants()), "grid": packed(grid_tables()),
    }


def second_block(core):
    nc, dram = core.nc, core.dram
    X, H, S2, S3, S4, S5, S6 = [s.rearrange("p (k t) -> p k t", k=KC) for s in core.slab]
    T = TOK2
    np2 = core.use_params("p2")
    consts = second_constants()
    core.place("second", consts, core.area)
    load(core, [(X[:, :, 0:META], dram["meta"]), (core.param[:, 0:np2], dram["p2"]),
                (core.area[:, 0:columns(consts)[1]], dram["second"])])
    mix = lambda k: core.col("mix_g", k)
    rms_norm(core, X, KC, T, S2, H, mix, D)

    raw = [S2, S3]
    z = [S4, S5]
    def shift(dve):
        step = Chain(dve, core.dve_step)
        mu = lambda name: core.param[:, core.pcols[name]:core.pcols[name] + 16]
        own = core.small[:, 0:16]
        step(nc.vector.tensor_tensor(own, mu("mu0"), mu("mu1"), ALU.add))
        step(nc.vector.tensor_scalar(own, own, -1.0, 1.0, ALU.mult, ALU.add))
        for ch in range(16):
            dve.wait_ge(core.read_act.sem, core.read_act.at(2 * (ch + 1)))
            rows = slice(0, P if ch < 15 else 32)
            p_, z_ = raw[ch // KC][rows, ch % KC, :], z[ch // KC][rows, ch % KC, :]
            step(nc.vector.tensor_scalar(z_, p_, own[rows, ch:ch + 1], None, ALU.mult))
            step(nc.vector.scalar_tensor_tensor(out=z_[:, 1:T], in0=p_[:, 0:T - 1], scalar=core.col("mu0", ch, rows),
                                                in1=z_[:, 1:T], op0=ALU.mult, op1=ALU.add))
            step(nc.vector.scalar_tensor_tensor(out=z_[:, 0:T - 1], in0=p_[:, 1:T], scalar=core.col("mu1", ch, rows),
                                                in1=z_[:, 0:T - 1], op0=ALU.mult, op1=ALU.add))
    dense(core, "rwkv_in", H, T, lambda eng, ps, ch, t0, t1: nc.scalar.copy(raw[ch // KC][0:ps.shape[0], ch % KC, t0:t1], ps), also=shift)

    lora = core.work[:, 0:2 * RW].rearrange("p (j c) -> p j c", j=2)
    gw = core.slab[1][:, 0:2 * RW].rearrange("p (j c) -> p j c", j=2)
    load(core, [(lora[:, 0], dram["decay_w2"]), (lora[:, 1], dram["icl_a2"]), (gw[:, 0], dram["gate_w2"][0:P]),
                (gw[0:32, 1], dram["gate_w2"][P:P + 32])])
    g = S6[:, 0:4]
    halves = splits_of(T)
    with core.stage() as block:
        @block.scalar
        def _(act):
            nc.scalar.activation(S5[:, 4, :], S5[:, 4, :], ACT.Tanh)
            nc.scalar.activation(S5[:, 6, :], S5[:, 6, :], ACT.Sigmoid)
            nc.scalar.activation(S5[0:32, 7, :], S5[0:32, 7, :], ACT.Sigmoid).then_inc(core.a2p.sem, core.a2p.add(1))
            for c in range(4):
                for s, (a, b) in enumerate(halves):
                    act.wait_ge(core.p2a.sem, core.p2a.at(2 * c + s + 1))
                    nc.scalar.copy(g[:, c, a:b], core.bank[2 * c + s][:, 0:b - a])

        @block.tensor
        def _(pe):
            pe.wait_ge(core.a2p.sem, core.a2p.at(1))
            for c in range(4):
                for s, (a, b) in enumerate(halves):
                    out = core.bank[2 * c + s][:, 0:b - a]
                    nc.tensor.matmul(out, gw[:, 0, c * P:(c + 1) * P], S5[:, 6, a:b], start=True, stop=False)
                    nc.tensor.matmul(out, gw[0:32, 1, c * P:(c + 1) * P], S5[0:32, 7, a:b], start=False, stop=True).then_inc(core.p2a.sem, core.p2a.add(1))

    pieces = [RwkvMemory(core, s, S4, S5, g, lora) for s in range(2)]
    for m in (0, 2):
        for i, w in enumerate(pieces):
            w.take(m + i)
        rwkv_heads(core, pieces)
    core.weight_limit = None
    ya = S5[:, 0:4]

    rms_norm(core, X, KC, T, S2, H, mix, D)
    core.place("grid", grid_tables(), core.area)
    load(core, [(core.area[:, 0:2 * TOK2], dram["grid"])])
    q, k, ks, yb = S2[:, 0:4], S2[:, 4:5], S2[:, 5:6], S4[:, 0:4]
    v = core.slab[3][:, 0:5 * P].rearrange("p (t c) -> p t c", t=5)
    dense(core, "q2", H, T, copy_to(core, q))

    def kv_groups(c0, cw):
        for a, b in halves:
            yield (P, b - a, lambda w, kc, kk, a=a, b=b: (w[:, kc, 0:P], H[:, kk, a:b]), "act",
                   lambda eng, ps, a=a, b=b: nc.scalar.copy(k[:, 0, a:b], ps))
        yield from token_groups(H, T, P, P, lambda eng, ps, t, c0: nc.vector.tensor_copy(v[0:ps.shape[0], t, :], ps), "dve")
    run_groups(core, "kv2", kv_groups)
    head = core.c("common", "head")
    qk = S2[:, 0:5]
    head_norm(core, qk, 5, T, S6, head, 64, 1e-6, lambda c: core.col("qg" if c < 4 else "kg", 0), qk)
    cos, sin = core.c("grid", "cos"), core.c("grid", "sin")
    rope(core, qk, 5, T, core.c("common", "rot16"), cos, sin)
    exchange_halves(core, k, ks, 1, T)
    units = []
    for hd in range(8):
        kv, rows = hd // 4, slice(64 * (hd % 2), 64 * (hd % 2) + 64)
        keys = k if hd % 2 == kv else ks
        for t0 in range(0, T, P):
            mq = min(P, T - t0)
            query = q[rows, hd // 2, t0:t0 + mq]
            segs = [([(query, keys[rows, 0, 0:SEQ])], SEQ, None), ([(query, keys[rows, 0, SEQ:T])], META, None)]
            blocks = [(v[0:min(P, T - b * P), b, kv * 64:kv * 64 + 64], min(P, T - b * P)) for b in range(5)]
            units.append((mq, segs, blocks, 64, 64 * (hd % 2), yb[rows, hd // 2, t0:t0 + mq], None))
    attention(core, units, 64 ** -0.5, core.slab[3][:, 640:2560], core.slab[3][:, 2560:3840])

    merge_branches(core, H, T, [("ga2", "pa2", ya, 0), ("gb2", "pb2", yb, 8)], S6, S2, None)
    add = lambda eng, ps, ch, t0, t1: nc.vector.tensor_tensor(X[:, ch, t0:t1], ps, X[:, ch, t0:t1], ALU.add)
    dense(core, "wo2", S6, T, add, by="dve", also=also_square(core, S2, X, T, "dve"))

    rms_norm(core, X, KC, T, S2, H, lambda c: core.col("ffn_g", c), D, squared=True)
    hidden = core.slabs[:, 2 * core.slab_cols:6 * core.slab_cols].rearrange("p (k t) -> p k t", k=4 * KC)

    def relu_squared(eng, ps, ch, t0, t1):
        to = hidden[:, ch, t0:t1]
        nc.scalar.activation(to, ps, ACT.Relu).then_inc(core.act_step.sem, core.act_step.add(1))
        nc.scalar.wait_ge(core.act_step.sem, core.act_step.at(core.act_step.sent))
        return nc.scalar.activation(to, to, ACT.Square)
    dense(core, "ff1", H, T, relu_squared)
    dense(core, "ff2", hidden, T, add, by="dve", also=also_square(core, S6, X, T, "dve"))
    rms_norm(core, X, KC, T, S6, X, lambda c: core.col("final", c), D, squared=True)


class Carve:

    def __init__(self, region):
        self.region, self.at = region, 0

    def __call__(self, n):
        self.at += n
        assert self.at <= self.region.shape[1]
        return self.region[:, self.at - n:self.at]


def in_turn(steps, streams):
    running = [steps(w) for w in streams]
    while running:
        running = [r for r in running if next(r, "end") != "end"]


class RwkvMemory:

    def __init__(self, core, s, S4, S5, g, lora):
        self.core, self.S4, self.S5, self.g_all, self.lora = core, S4, S5, g, lora
        self.q = core.bank[4 * s:4 * s + 4]
        (self.to_dve, self.to_act, self.from_dve, self.from_act, self.row_tile, self.dve_to_act, self.act_to_dve,
         self.dve_step) = core.rwkv[s]
        if s == 0:
            c = Carve(core.slabs[:, core.slab_cols:4 * core.slab_cols])
            c1, c2 = Carve(core.slab[6][:, 4 * TOK2:]), Carve(core.work[:, 2 * RW:2300])
            masks = columns(second_constants())[1]
            at_area, at_rstd = Carve(core.area[:, masks:masks + 512]), Carve(core.rstd[:, 0:512])
            homes = {"AR": c, "BK": c, "G": c, "H": c, "rz": c, "Vp": c, "PC": c, "X": c, "M": c, "D": c, "DT": c1, "RB": c1, "RK": c1,
                     "N": c1, "BKc": c2, "BT": c2, "KT": c2, "VT": c2, "AU": at_area, "AUin": at_rstd}
        else:
            r = [Carve(t[:, :, :].rearrange("p k c -> p (k c)")) for t in core.ring]
            spare = Carve(core.slab[5][:, 6 * TOK2:])
            homes = {"AR": r[0], "rz": r[0], "BK": r[1], "Vp": r[1], "PC": r[1], "X": r[1], "M": r[1], "G": r[2], "D": r[2], "DT": r[2],
                     "RB": r[2], "H": r[3], "RK": r[3], "N": r[3], "BKc": r[3], "BT": r[1], "KT": r[0], "VT": r[2], "AU": spare,
                     "AUin": spare}
        sizes = {"AR": 4 * WIDE, "BK": 4 * WIDE, "G": 2 * NBLK * 64, "H": 2 * NBLK * 64, "rz": 3 * WIDE, "Vp": WIDE, "PC": 2 * NBLK,
                 "BT": 256, "KT": 256, "VT": P}
        m = {name: home(sizes.get(name, 512)) for name, home in homes.items()}
        square = lambda t: t.rearrange("p (u t) -> p u t", u=4)
        self.AR, self.BK = (m[n].rearrange("p (d j t) -> p d j t", d=2, j=2) for n in ("AR", "BK"))
        self.G, self.Hs = (m[n].rearrange("p (d b c) -> p d b c", d=2, c=64) for n in ("G", "H"))
        self.rz, self.Vp, self.VT = m["rz"], m["Vp"], m["VT"]
        self.Rhat, self.Z = self.rz[:, 0:2 * WIDE].rearrange("p (d t) -> p d t", d=2), self.rz[:, 2 * WIDE:]
        self.PC = m["PC"].rearrange("p (d b) -> p d b", d=2)
        self.Xs, self.Ml, self.Dm, self.DT, self.RB, self.RK, self.NT, self.AU, self.AUin, self.BKc = (
            square(m[n]) for n in ("X", "M", "D", "DT", "RB", "RK", "N", "AU", "AUin", "BKc"))
        self.BT, self.KT = (m[n].rearrange("p (d c) -> p d c", d=2) for n in ("BT", "KT"))
        both = lambda t, i: t[:, i * 2 * WIDE:(i + 1) * 2 * WIDE].rearrange("p (d t) -> p d t", d=2)
        self.lam, self.s1, self.s2, self.icl = both(m["G"], 0), both(m["G"], 1), both(m["H"], 0), both(m["H"], 1)
        self.kk, self.t1, self.t2 = (self.rz[:, i * WIDE:(i + 1) * WIDE] for i in range(3))
        self.one_less = core.small[:, s:s + 1]

    def take(self, m):
        self.m = m
        self.r, self.k, self.v, self.g = self.S4[:, m, :], self.S4[:, 4 + m, :], self.S5[:, m, :], self.g_all[:, m, :]
        self.wd, self.ad = self.S5[:, 4, :], self.S5[:, 5, :]

    def col(self, name):
        return self.core.col(name, self.m)


def rwkv_heads(core, pieces):
    nc = core.nc
    T = TOK2
    halves = splits_of(T)
    head = core.c("common", "head")

    with core.stage() as block:
        @block.tensor
        def _(pe):
            def steps(w):
                for j, src in enumerate((w.wd, w.ad)):
                    for d in range(2):
                        rows = slice(64 * d, 64 * d + 64)
                        for s, (a, b) in enumerate(halves):
                            if j == 1:
                                pe.wait_ge(w.from_act.sem, w.from_act.at(2 * d + s + 1))
                            nc.tensor.matmul(w.q[2 * d + s][:, 0:b - a], w.lora[rows, j, w.m * P:(w.m + 1) * P],
                                             src[rows, a:b], start=True, stop=True).then_inc(w.to_act.sem, w.to_act.add(1))
                    yield
                pe.wait_ge(w.from_dve.sem, w.from_dve.at(1))
                pe.wait_ge(w.from_act.sem, w.from_act.at(6))
                for s, (a, b) in enumerate(halves):
                    nc.tensor.matmul(w.q[s][:, 0:b - a], head, w.t1[:, a:b], start=True, stop=True).then_inc(w.to_act.sem, w.to_act.add(1))
                yield
            in_turn(steps, pieces)

        @block.scalar
        def _(act):
            def steps(w):
                for j, (dst, bias) in enumerate(((w.lam, "w0"), (w.icl, "a0"))):
                    for d in range(2):
                        for s, (a, b) in enumerate(halves):
                            act.wait_ge(w.to_act.sem, w.to_act.at(4 * j + 2 * d + s + 1))
                            nc.scalar.activation(dst[:, d, a:b], w.q[2 * d + s][:, 0:b - a], ACT.Sigmoid,
                                                 bias=core.col(bias, 4 * d + w.m)).then_inc(w.from_act.sem, w.from_act.add(1))
                    yield
            in_turn(steps, pieces)

            def roots(w):
                act.wait_ge(w.to_act.sem, w.to_act.at(10))
                for s, (a, b) in enumerate(halves):
                    ins = nc.scalar.activation(w.t2[:, a:b], w.q[s][:, 0:b - a], ACT.Sqrt)
                ins.then_inc(w.act_to_dve.sem, w.act_to_dve.add(1))
                yield
            in_turn(roots, pieces)

        @block.vector
        def _(dve):
            def steps(w):
                step = Chain(dve, w.dve_step)
                step(nc.vector.tensor_scalar(w.kk[:, 0:T], w.k, w.col("k_k"), None, ALU.mult))
                nc.vector.tensor_tensor(w.t1[:, 0:T], w.kk[:, 0:T], w.kk[:, 0:T], ALU.mult).then_inc(w.from_dve.sem, w.from_dve.add(1))
                for t in (w.AR[:, :, 0], w.AR[:, :, 1], w.BK[:, :, 0], w.BK[:, :, 1], w.lam):
                    nc.vector.memset(t[:, :, T:WIDE], 0.0)
                nc.vector.memset(w.Vp[:, T:WIDE], 0.0)
                nc.vector.tensor_copy(w.Vp[:, 0:T], w.v)
                nc.vector.tensor_scalar(w.one_less, w.col("k_a"), -1.0, 1.0, ALU.mult, ALU.add)
                yield
                dve.wait_ge(w.act_to_dve.sem, w.act_to_dve.at(1))
                step(nc.vector.tensor_scalar(w.t2[:, 0:T], w.t2[:, 0:T], 1e-12, None, ALU.max))
                step(nc.vector.reciprocal(w.t2[:, 0:T], w.t2[:, 0:T]))
                step(nc.vector.tensor_tensor(w.kk[:, 0:T], w.kk[:, 0:T], w.t2[:, 0:T], ALU.mult))
                yield
            in_turn(steps, pieces)

    blocks = lambda t: t.rearrange("p (b l) -> p b l", l=LB)
    with core.stage() as block:
        @block.vector
        def _(dve):
            def sums(w):
                step = Chain(dve, w.dve_step)
                goes_on = w.s2[:, 0, :]
                step(nc.vector.memset(goes_on, 1.0))
                step(nc.vector.memset(blocks(goes_on)[:, :, 0:1], 0.0))
                nc.vector.tensor_tensor_scan(w.s1[:, 0, :], goes_on, w.lam[:, 0, :], 0.0, ALU.mult, ALU.add)
                step(nc.vector.tensor_tensor_scan(w.s1[:, 1, ::-1], goes_on, w.lam[:, 1, ::-1], 0.0, ALU.mult, ALU.add))
                yield
                nc.vector.tensor_tensor(w.s2, w.s1, w.lam, ALU.subtract)
                nc.vector.tensor_copy(w.PC[:, 0, :], blocks(w.s1[:, 0, :])[:, :, LB - 1])
                nc.vector.tensor_copy(w.PC[:, 1, :], blocks(w.s1[:, 1, :])[:, :, 0]).then_inc(w.dve_to_act.sem, w.dve_to_act.add(1))
                yield
            in_turn(sums, pieces)

            def factors(w):
                step = Chain(dve, w.dve_step)
                t1, t2 = w.t1[:, 0:T], w.t2[:, 0:T]
                dve.wait_ge(w.act_to_dve.sem, w.act_to_dve.at(2))
                nc.vector.tensor_tensor(t1, t1, w.k, ALU.mult)
                step(nc.vector.tensor_tensor(t2, t2, w.k, ALU.mult))
                for d in range(2):
                    a, r_, b, kd = (t[:, d, j, 0:T] for t, j in ((w.AR, 0), (w.AR, 1), (w.BK, 0), (w.BK, 1)))
                    icl, kk = w.icl[:, d, 0:T], w.kk[:, 0:T]
                    nc.vector.tensor_tensor(kd, (t2, t1)[d], b, ALU.mult)
                    step(nc.vector.tensor_tensor(icl, icl, kk, ALU.mult))
                    nc.vector.tensor_tensor(r_, r_, w.r, ALU.mult)
                    nc.vector.scalar_tensor_tensor(out=a, in0=kk, scalar=-1.0, in1=a, op0=ALU.mult, op1=ALU.mult)
                    nc.vector.tensor_tensor(b, b, icl, ALU.mult)
                    yield
                step(nc.vector.tensor_tensor(t2, t1, t2, ALU.add))
                nc.vector.scalar_tensor_tensor(out=t2, in0=t2, scalar=w.col("r_k"), in1=w.r, op0=ALU.mult,
                                               op1=ALU.mult).then_inc(w.from_dve.sem, w.from_dve.add(1))
                yield
            in_turn(factors, pieces)

            def bonus(w):
                dve.wait_ge(w.to_dve.sem, w.to_dve.at(1))
                for s, (a, b) in enumerate(halves):
                    nc.vector.scalar_tensor_tensor(out=w.v[:, a:b], in0=w.q[s][:, 0:b - a], scalar=0.5, in1=w.Vp[:, a:b],
                                                   op0=ALU.mult, op1=ALU.mult)
                yield
            in_turn(bonus, pieces)

        @block.scalar
        def _(act):
            for w in pieces:
                for d, to in enumerate((w.t2, w.t1)):
                    ins = nc.scalar.activation(to[:, 0:T], w.icl[:, d, 0:T], ACT.Identity, bias=w.one_less, scale=w.col("k_a"))
                ins.then_inc(w.act_to_dve.sem, w.act_to_dve.add(1))

            def steps(w):
                act.wait_ge(w.dve_to_act.sem, w.dve_to_act.at(1))
                nc.scalar.activation(w.PC, w.PC, ACT.Exp, scale=DECAY_SCALE)
                nc.scalar.activation(w.AR[:, :, 1, 0:T], w.s1[:, :, 0:T], ACT.Exp, scale=DECAY_SCALE)
                nc.scalar.activation(w.AR[:, :, 0, 0:T], w.s2[:, :, 0:T], ACT.Exp, scale=DECAY_SCALE)
                nc.scalar.activation(w.BK[:, :, 0, 0:T], w.s1[:, :, 0:T], ACT.Exp, scale=-DECAY_SCALE).then_inc(w.act_to_dve.sem, w.act_to_dve.add(1))
                yield
            in_turn(steps, pieces)

        @block.tensor
        def _(pe):
            def steps(w):
                pe.wait_ge(w.from_dve.sem, w.from_dve.at(1))
                for s, (a, b) in enumerate(halves):
                    mm = nc.tensor.matmul(w.q[s][:, 0:b - a], head, w.t2[:, a:b], start=True, stop=True)
                mm.then_inc(w.to_dve.sem, w.to_dve.add(1))
                yield
            in_turn(steps, pieces)

    strict, upto = (core.c("second", n).rearrange("p (d t) -> p d t", d=2) for n in ("strict", "upto"))
    level = {b: core.c("second", f"level{b}").rearrange("p (d t) -> p d t", d=2) for b in (1, 2, 4, 8, 16)}
    for t0 in range(0, WIDE, P):
        rwkv_tile(core, pieces, t0, min(P, WIDE - t0), strict, upto, level)

    rows_of = [slice(0, 64), slice(64, P)]
    LAST = NBLK - 1
    with core.stage() as block:
        @block.tensor
        def _(pe):
            def steps(w):
                def outputs(b, bank, at):
                    for h, rows in enumerate(rows_of):
                        before = [(0, b - 1)] * (b > 0) + [(1, b + 1)] * (b < LAST)
                        for i, (d, src) in enumerate(before):
                            mm = nc.tensor.matmul(w.q[bank + h][rows, at:at + LB], w.Hs[rows, d, src, :], w.Rhat[rows, d, b * LB:(b + 1) * LB],
                                                  start=i == 0, stop=i == len(before) - 1)
                    return mm

                for c in range(1, LAST + 1):
                    if c > 1:
                        pe.wait_ge(w.from_dve.sem, w.from_dve.at(c - 1))
                    if c < LAST:
                        for h, rows in enumerate(rows_of):
                            for d, (b, src) in enumerate(((c, c - 1), (LAST - c, LAST - c + 1))):
                                mm = nc.tensor.matmul(w.q[h][rows, d * 64:d * 64 + 64], w.G[rows, d, b, :], w.Hs[rows, d, src, :],
                                                      start=True, stop=True)
                        mm.then_inc(w.to_dve.sem, w.to_dve.add(1))
                    else:
                        mm = outputs(LAST, 0, 0)
                    if 2 * c >= LAST:
                        for b in sorted({c, LAST - c} - {LAST}):
                            mm = outputs(b, 2, b * LB)
                    yield
                mm.then_inc(w.to_dve.sem, w.to_dve.add(1))
            in_turn(steps, pieces)

        @block.vector
        def _(dve):
            def steps(w):
                for c in range(1, LAST):
                    dve.wait_ge(w.to_dve.sem, w.to_dve.at(c))
                    for h, rows in enumerate(rows_of):
                        for d, b in enumerate((c, LAST - c)):
                            state = w.Hs[rows, d, b, :]
                            ins = nc.vector.tensor_tensor(state, w.q[h][rows, d * 64:d * 64 + 64], state, ALU.add)
                    ins.then_inc(w.from_dve.sem, w.from_dve.add(1))
                    yield
                dve.wait_ge(w.to_dve.sem, w.to_dve.at(LAST))
                for h, rows in enumerate(rows_of):
                    nc.vector.tensor_tensor(w.Z[rows, 0:SEQ], w.q[2 + h][rows, :], w.Z[rows, 0:SEQ], ALU.add)
                    nc.vector.tensor_tensor(w.Z[rows, SEQ:WIDE], w.q[h][rows, 0:LB], w.Z[rows, SEQ:WIDE], ALU.add)
                yield
            in_turn(steps, pieces)

    with core.stage() as block:
        @block.tensor
        def _(pe):
            def steps(w):
                for s, (a, b) in enumerate(halves):
                    mm = nc.tensor.matmul(w.q[s][:, 0:b - a], head, w.Z[:, a:b], start=True, stop=True)
                mm.then_inc(w.to_dve.sem, w.to_dve.add(1))
                yield
                pe.wait_ge(w.from_act.sem, w.from_act.at(1))
                for s, (a, b) in enumerate(halves):
                    mm = nc.tensor.matmul(w.q[2 + s][:, 0:b - a], head, w.t1[:, a:b], start=True, stop=True)
                mm.then_inc(w.to_act.sem, w.to_act.add(1))
                yield
            in_turn(steps, pieces)

        @block.scalar
        def _(act):
            def steps(w):
                act.wait_ge(w.dve_to_act.sem, w.dve_to_act.at(1))
                nc.scalar.activation(w.t1[:, 0:T], w.kk[:, 0:T], ACT.Square).then_inc(w.from_act.sem, w.from_act.add(1))
                yield
                act.wait_ge(w.to_act.sem, w.to_act.at(1))
                for s, (a, b) in enumerate(halves):
                    ins = root(core, w.t1[:, a:b], w.q[2 + s][:, 0:b - a], 64, 64e-5)
                ins.then_inc(w.act_to_dve.sem, w.act_to_dve.add(1))
                yield
            in_turn(steps, pieces)

        @block.vector
        def _(dve):
            def steps(w):
                step = Chain(dve, w.dve_step)
                yc, sq = w.kk[:, 0:T], w.t1[:, 0:T]
                dve.wait_ge(w.to_dve.sem, w.to_dve.at(1))
                for s, (a, b) in enumerate(halves):
                    ins = nc.vector.scalar_tensor_tensor(out=yc[:, a:b], in0=w.q[s][:, 0:b - a], scalar=-1.0 / 64, in1=w.Z[:, a:b],
                                                         op0=ALU.mult, op1=ALU.add)
                ins.then_inc(w.dve_to_act.sem, w.dve_to_act.add(1))
                yield
                dve.wait_ge(w.act_to_dve.sem, w.act_to_dve.at(1))
                step(nc.vector.reciprocal(sq, sq))
                step(nc.vector.scalar_tensor_tensor(out=yc, in0=yc, scalar=w.col("lnx_g"), in1=sq, op0=ALU.mult, op1=ALU.mult))
                step(nc.vector.scalar_tensor_tensor(out=yc, in0=yc, scalar=w.col("lnx_b"), in1=w.v, op0=ALU.add, op1=ALU.add))
                nc.vector.tensor_tensor(w.v, yc, w.g, ALU.mult)
                yield
            in_turn(steps, pieces)


def rwkv_tile(core, pieces, t0, W, strict, upto, level):
    nc, ident, eye64 = core.nc, core.c("common", "ident"), core.c("common", "eye64")
    tok, nb, b0 = slice(t0, t0 + W), W // LB, t0 // LB
    units = [(u, u // 2, slice(64 * (u % 2), 64 * (u % 2) + 64)) for u in range(4)]
    by4 = lambda bank: bank[0:W, :].rearrange("p (u t) -> p u t", u=4)
    pairs = lambda t: t.rearrange("p (d h) t -> p d h t", d=2)[0:W, :, :, 0:W]
    of = lambda mask: mask[0:W, :, 0:W].unsqueeze(2).broadcast_to([W, 2, 2, W])
    w4 = lambda t: t[0:W, :, 0:W]
    levels = (2, 4, 8, 16)
    block_bank = (1, 3, 0, 2)
    with core.stage() as block:
        @block.tensor
        def _(pe):
            mm = nc.tensor.matmul

            def steps(w):
                q = w.q

                def products(h, pairs_of):
                    for u, d, rows in units[h::2]:
                        side = {"a": w.AR[rows, d, 0, tok], "r": w.AR[rows, d, 1, tok], "b": w.BK[rows, d, 0, tok], "k": w.BK[rows, d, 1, tok]}
                        for bank, lhsT, rhs in pairs_of:
                            last = mm(q[bank][0:W, u * P:u * P + W], side[lhsT], side[rhs], start=True, stop=True)
                    return last

                first = ((0, "b", "a"), (1, "a", "b"), (2, "k", "a"))
                products(0, first).then_inc(w.row_tile.sem, w.row_tile.add(1))
                yield
                pe.wait_ge(w.row_tile.sem, w.row_tile.at(1))
                products(1, first).then_inc(w.to_dve.sem, w.to_dve.add(1))
                for i, src in enumerate((w.AR[:, 0, 0, tok], w.AR[:, 1, 0, tok], w.Vp[:, tok])):
                    last = nc.tensor.transpose(q[3][0:W, i * P:(i + 1) * P], src, ident)
                last.then_inc(w.to_act.sem, w.to_act.add(1))
                yield
                pe.wait_ge(w.from_dve.sem, w.from_dve.at(1))
                pe.wait_ge(w.from_act.sem, w.from_act.at(1))
                for i in range(4):
                    last = nc.tensor.transpose(q[3][0:W, i * P:(i + 1) * P], w.BKc[:, i, 0:W], ident)
                last.then_inc(w.to_act.sem, w.to_act.add(1))
                yield
                pe.wait_ge(w.from_dve.sem, w.from_dve.at(3))
                second = ((1, "b", "r"), (2, "k", "r"))
                products(0, second).then_inc(w.row_tile.sem, w.row_tile.add(1))
                yield
                pe.wait_ge(w.row_tile.sem, w.row_tile.at(2))
                products(1, second).then_inc(w.to_dve.sem, w.to_dve.add(1))
                pe.wait_ge(w.from_act.sem, w.from_act.at(2))
                for u, d, rows in units:
                    last = mm(q[3][0:W, u * 64:u * 64 + 64], w.NT[0:W, u, 0:W], w.VT[0:W, rows], start=True, stop=True)
                last.then_inc(w.to_act.sem, w.to_act.add(1))
                yield
                for l in range(4):
                    pe.wait_ge(w.from_dve.sem, w.from_dve.at(5 + l))
                    for u, d, rows in units:
                        last = mm(q[1][0:W, u * P:u * P + W], w.Ml[0:W, u, 0:W], w.Dm[0:W, u, 0:W], start=True, stop=True)
                    last.then_inc(w.to_act.sem, w.to_act.add(1))
                    yield
                    pe.wait_ge(w.from_act.sem, w.from_act.at(4 + l))
                    for u, d, rows in units:
                        if l < 3:
                            mm(q[2][0:W, u * P:u * P + W], w.DT[0:W, u, 0:W], w.Xs[0:W, u, 0:W], start=True, stop=True)
                        last = mm(q[3][0:W, u * P:u * P + W], w.Xs[0:W, u, 0:W], w.DT[0:W, u, 0:W], start=True, stop=True)
                    last.then_inc(w.to_dve.sem, w.to_dve.add(1))
                    yield
                pe.wait_ge(w.from_dve.sem, w.from_dve.at(9))
                for u, d, rows in units:
                    last = mm(q[1][0:W, u * P:(u + 1) * P], w.DT[0:W, u, 0:W], w.AUin[0:W, u, :], start=True, stop=True)
                last.then_inc(w.to_act.sem, w.to_act.add(1))
                yield
                pe.wait_ge(w.from_act.sem, w.from_act.at(8))
                for u, d, rows in units:
                    last = mm(q[0][rows, d * P:d * P + W], w.AU[0:W, u, 0:64], w.RB[0:W, u, 0:W], start=True, stop=True)
                last.then_inc(w.to_dve.sem, w.to_dve.add(1))
                for h in range(2):
                    rows = slice(64 * h, 64 * h + 64)
                    for d in range(2):
                        mm(q[2][rows, 0:W], w.AU[0:W, 2 * d + h, 64:P], w.RB[0:W, 2 * d + h, 0:W], start=d == 0, stop=False)
                        last = mm(q[2][rows, 0:W], w.VT[0:W, rows], w.RK[0:W, 2 * d + h, 0:W], start=False, stop=d == 1)
                last.then_inc(w.to_act.sem, w.to_act.add(1))

                def block_maps(b):
                    t = slice(b * LB, (b + 1) * LB)
                    for u, d, rows in units:
                        to = q[block_bank[b]][rows, d * P:(d + 1) * P]
                        mm(to[:, 0:64], w.AU[t, u, 0:64], w.BT[t, d, rows], start=True, stop=True)
                        mm(to[:, 64:P], w.BT[t, d, rows], w.AU[t, u, 64:P], start=True, stop=False)
                        last = mm(to[:, 64:P], w.KT[t, d, rows], w.VT[t, rows], start=False, stop=True)
                    last.then_inc(w.to_dve.sem, w.to_dve.add(1))
                for b in range(min(nb, 2)):
                    block_maps(b)
                yield
                if nb > 2:
                    pe.wait_ge(w.from_dve.sem, w.from_dve.at(10))
                    block_maps(2)
                    pe.wait_ge(w.from_act.sem, w.from_act.at(9))
                    block_maps(3)
                yield
            in_turn(steps, pieces)

        @block.scalar
        def _(act):
            def steps(w):
                q = w.q
                act.wait_ge(w.to_act.sem, w.to_act.at(1))
                nc.scalar.copy(w.AUin[0:W, :, 0:64], q[3][0:W, 0:256].rearrange("p (u c) -> p u c", u=4))
                nc.scalar.copy(w.VT[0:W, :], q[3][0:W, 256:384]).then_inc(w.from_act.sem, w.from_act.add(1))
                yield
                act.wait_ge(w.to_act.sem, w.to_act.at(2))
                nc.scalar.copy(w.BT[0:W], q[3][0:W, 0:256].rearrange("p (d c) -> p d c", d=2))
                nc.scalar.copy(w.KT[0:W], q[3][0:W, 256:512].rearrange("p (d c) -> p d c", d=2)).then_inc(w.from_act.sem, w.from_act.add(1))
                yield
                act.wait_ge(w.to_act.sem, w.to_act.at(3))
                nc.scalar.copy(w.AUin[0:W, :, 64:P], q[3][0:W, 0:256].rearrange("p (u c) -> p u c", u=4)).then_inc(w.from_act.sem, w.from_act.add(1))
                yield
                for l in range(4):
                    act.wait_ge(w.to_act.sem, w.to_act.at(4 + l))
                    nc.scalar.copy(w4(w.Xs), w4(by4(q[1]))).then_inc(w.from_act.sem, w.from_act.add(1))
                    yield
                act.wait_ge(w.to_act.sem, w.to_act.at(8))
                nc.scalar.copy(w.AU[0:W], by4(q[1])).then_inc(w.from_act.sem, w.from_act.add(1))
                yield
                act.wait_ge(w.to_act.sem, w.to_act.at(9))
                nc.scalar.copy(w.Z[:, tok], q[2][:, 0:W]).then_inc(w.from_act.sem, w.from_act.add(1))
                yield
            in_turn(steps, pieces)

        @block.vector
        def _(dve):
            tt = nc.vector.tensor_tensor
            by_block = lambda t: t.rearrange("p (b l) -> p b l", l=LB)

            def steps(w):
                q = w.q
                step = Chain(dve, w.dve_step)
                for i in range(4):
                    j, d = i // 2, i % 2
                    ins = tt(by_block(w.BKc[:, i, 0:W]), by_block(w.BK[:, d, j, tok]),
                             w.PC[:, d, b0:b0 + nb].unsqueeze(2).broadcast_to([P, nb, LB]), ALU.mult)
                ins.then_inc(w.from_dve.sem, w.from_dve.add(1))
                yield
                dve.wait_ge(w.to_dve.sem, w.to_dve.at(1))
                tt(pairs(w.NT), pairs(by4(q[2])), of(strict), ALU.mult).then_inc(w.from_dve.sem, w.from_dve.add(1))
                for d in range(2):
                    ins = tt(w4(w.Dm)[:, 2 * d:2 * d + 2], by4(q[1])[:, 2 * d:2 * d + 2, 0:W],
                             level[1][0:W, 1 - d, 0:W].unsqueeze(1).broadcast_to([W, 2, W]), ALU.mult)
                ins.then_inc(w.from_dve.sem, w.from_dve.add(1))
                eye = ident[0:W, 0:W].unsqueeze(1).broadcast_to([W, 4, W])
                dve.wait_ge(w.from_dve.sem, w.from_dve.at(3))
                tt(w4(w.Dm), w4(w.Dm), eye, ALU.add)
                step(tt(pairs(w.DT), pairs(by4(q[0])), of(level[1]), ALU.mult))
                tt(pairs(w.Ml), pairs(by4(q[0])), of(level[2]), ALU.mult)
                tt(w4(w.DT), w4(w.DT), eye, ALU.add).then_inc(w.from_dve.sem, w.from_dve.add(1))
                yield
                dve.wait_ge(w.to_dve.sem, w.to_dve.at(2))
                tt(pairs(w.RB), pairs(by4(q[1])), of(upto), ALU.mult)
                tt(pairs(w.RK), pairs(by4(q[2])), of(upto), ALU.mult).then_inc(w.from_dve.sem, w.from_dve.add(1))
                yield
                for l in range(4):
                    if l < 3:
                        dve.wait_ge(w.to_act.sem, w.to_act.at(4 + l))
                        tt(pairs(w.Ml), pairs(by4(q[0])), of(level[levels[l + 1]]), ALU.mult)
                    dve.wait_ge(w.to_dve.sem, w.to_dve.at(3 + l))
                    if l < 3:
                        tt(w4(w.Dm), w4(w.Dm), w4(by4(q[2])), ALU.add)
                    tt(w4(w.DT), w4(w.DT), w4(by4(q[3])), ALU.add).then_inc(w.from_dve.sem, w.from_dve.add(1))
                    yield
                dve.wait_ge(w.to_dve.sem, w.to_dve.at(7))
                tt(w.Rhat[:, :, tok], q[0][:, 0:2 * P].rearrange("p (d t) -> p d t", d=2)[:, :, 0:W], w.AR[:, :, 1, tok],
                   ALU.add).then_inc(w.from_dve.sem, w.from_dve.add(1))
                yield
                for b in range(nb):
                    dve.wait_ge(w.to_dve.sem, w.to_dve.at(8 + b))
                    from_ = q[block_bank[b]][:, 0:2 * P].rearrange("p (d c) -> p d c", d=2)
                    for d in range(2):
                        nc.vector.scalar_tensor_tensor(out=w.G[:, d, b0 + b, :], in0=eye64, scalar=w.PC[:, d, b0 + b:b0 + b + 1],
                                                       in1=from_[:, d, 0:64], op0=ALU.mult, op1=ALU.add)
                    nc.vector.tensor_copy(w.Hs[:, :, b0 + b, :], from_[:, :, 64:P])
                    if b % 2 == 1:
                        yield
                yield
            in_turn(steps, pieces)


HALF_PI = float(np.pi / 2)
ROUNDER = 1.5 * 2.0 ** 23
TURN = (6.28125, 0.0019350051879882812, float(2 * np.pi - 6.28125 - 0.0019350051879882812))


def plan_third(core):
    d = core.dram
    w = d["even_w_in"]
    at = 0
    for name, n in (("qk3", 1024), ("v3", D), ("gret", D), ("cb", D), ("cc", D), ("cx", D), ("gconv", D)):
        core.third_cols[name] = (at, at + n)
        at += n
    for name in ("qk3", "v3", "gret", "cc", "cx", "gconv", "cb"):
        core.plan(name, w, *core.third_cols[name])
    core.plan("wo3", d["even_w_out"], 0, D)
    w = d["odd_w_in"]
    core.plan("cq", w, 0, 384)
    core.plan("ckv", w, 384, 640)
    core.plan("kr", w, 640, 704)
    core.plan("qb", d["w_qb"], 0, 1536, wide=384)
    core.plan("kvb", d["w_kvb"], 0, 2048)
    core.plan("gate3", w, 704, 1728)
    core.plan("wo4", d["odd_w_out"], 0, D)


def laid_out_third(x, chunks):
    p3 = [x["pre_norm_3"], x["post_norm_3"], x["even_conv_w_3"][0].reshape(-1), x["even_conv_b_3"], x["ret_gn_3"], x["q_a_norm_3"],
          x["kv_a_norm_3"]]
    return {
        "positions": np.ascontiguousarray(x["positions_3"][0]), "even_w_in": x["even_w_in_3"][0], "even_w_out": x["even_w_out_3"][0],
        "odd_w_in": x["odd_w_in_3"][0], "w_qb": x["w_qb_3"][0], "w_kvb": x["w_kvb_3"][0], "odd_w_out": x["odd_w_out_3"][0],
        "p3": np.ascontiguousarray(np.concatenate([chunks(a) for a in p3], 1)), "third": packed(third_constants()),
    }


def add_normalised(core, x, y, squares, gain):
    rms_norm(core, y, KC, SEQ, squares, y, gain, D, squared=True,
             post=lambda k: core.nc.vector.tensor_tensor(x[:, k, :], x[:, k, :], y[:, k, :], ALU.add))


def third_block(core):
    nc, dram = core.nc, core.dram
    slabs = [s.rearrange("p (k t) -> p k t", k=KC) for s in core.slab]
    x = slabs[0][:, :, META:]
    H, S2, S3, S4, S5, S6 = [s[:, :, 0:SEQ] for s in slabs[1:]]
    n3 = core.use_params("p3")
    consts = third_constants()
    core.place("third", consts, core.area)
    c = lambda name: core.c("third", name)
    where = core.slab[6][:, 0:SEQ].bitcast(I32)
    load(core, [(core.param[:, 0:n3], dram["p3"]), (core.area[:, 0:columns(consts)[1]], dram["third"]),
                (where, dram["positions"].partition_broadcast(P))])

    sin, cos = core.work[:, 1024:1536], core.work[:, 1536:2048]
    ang, turns = core.slab[6][:, SEQ:2 * SEQ], core.slab[6][:, 2 * SEQ:3 * SEQ]
    with core.stage() as block:
        @block.vector
        def _(dve):
            step = Chain(dve, core.dve_step)
            step(nc.vector.tensor_copy(ang, where))
            step(nc.vector.tensor_scalar(ang, ang, c("inv"), None, ALU.mult))
            for out, ahead in ((sin, 0.0), (cos, 0.25)):
                step(nc.vector.tensor_scalar(turns, ang, float(0.5 / np.pi), ahead, ALU.mult, ALU.add))
                step(nc.vector.tensor_scalar(turns, turns, ROUNDER, None, ALU.add))
                step(nc.vector.tensor_scalar(turns, turns, ROUNDER, None, ALU.subtract))
                step(nc.vector.scalar_tensor_tensor(out=out, in0=turns, scalar=-TURN[0], in1=ang, op0=ALU.mult, op1=ALU.add))
                for part in TURN[1:]:
                    step(nc.vector.scalar_tensor_tensor(out=out, in0=turns, scalar=-part, in1=out, op0=ALU.mult, op1=ALU.add))
                if ahead:
                    step(nc.vector.tensor_scalar(out, out, HALF_PI, None, ALU.add))
                step(nc.vector.tensor_scalar(out, out, 3.1415925, -3.1415925, ALU.min, ALU.max))
            nc.vector.tensor_copy(ang, ang).then_inc(core.v2a.sem, core.v2a.add(1))

        @block.scalar
        def _(act):
            act.wait_ge(core.v2a.sem, core.v2a.at(1))
            nc.scalar.activation(sin, sin, ACT.Sin)
            nc.scalar.activation(cos, cos, ACT.Sin)

    rms_norm(core, x, KC, SEQ, S2, H, lambda k: core.col("pre", k), D)
    qk, R = S2, S4
    v = core.slab[3][:, 0:4 * D].rearrange("p (t c) -> p t c", t=4)
    dense(core, "qk3", H, SEQ, copy_to(core, qk))
    run_groups(core, "v3", lambda c0, cw: token_groups(H, SEQ, 0, cw, lambda eng, ps, t, c0: nc.scalar.copy(v[:, t, c0:c0 + cw], ps), "act", c0))
    rope(core, qk, KC, SEQ, core.c("common", "rot32"), cos, sin)
    retention(core, qk[:, 0:4], qk[:, 4:8], v, R)
    head_norm(core, R, KC, SEQ, S6, core.c("common", "ones"), P, 1e-6, lambda k: core.col("gn", k), R)
    silu = lambda dst: (lambda eng, ps, ch, t0, t1: nc.scalar.activation(dst[:, ch, t0:t1], ps, ACT.Silu))
    dense(core, "gret", H, SEQ, silu(S6), also=also_gate(core, R, S6))
    u, conv = S2, S5
    times = lambda dst: (lambda eng, ps, ch, t0, t1: nc.vector.tensor_tensor(dst[:, ch, t0:t1], ps, dst[:, ch, t0:t1], ALU.mult))
    dense(core, "cc", H, SEQ, copy_to(core, u))
    dense(core, "cx", H, SEQ, times(u), by="dve")

    def convolve(dve):
        step = Chain(dve, core.dve_step)
        for k in range(KC):
            tap = lambda j: core.col("conv_w", j * KC + k)
            step(nc.vector.tensor_scalar(conv[:, k, :], u[:, k, :], tap(2), core.col("conv_b", k), ALU.mult, ALU.add))
            for j, back in ((1, 1), (0, 2)):
                step(nc.vector.scalar_tensor_tensor(out=conv[:, k, back:], in0=u[:, k, 0:SEQ - back], scalar=tap(j),
                                                    in1=conv[:, k, back:], op0=ALU.mult, op1=ALU.add))
        for k in range(KC):
            dve.wait_ge(core.read_act.sem, core.read_act.at(k + 1))
            nc.vector.tensor_tensor(conv[:, k, :], conv[:, k, :], S6[:, k, :], ALU.mult)
    dense(core, "gconv", H, SEQ, silu(S6), also=convolve)
    dense(core, "cb", H, SEQ, times(conv), by="dve")
    mix = core.slabs[:, 4 * core.slab_cols:6 * core.slab_cols].rearrange("p (k t) -> p k t", k=2 * KC)
    dense(core, "wo3", mix, SEQ, copy_to(core, S2), also=also_square(core, S3, S2, SEQ, "act"))
    add_normalised(core, x, S2, S3, lambda k: core.col("post", k))

    rms_norm(core, x, KC, SEQ, S2, H, lambda k: core.col("pre", KC + k), D)
    cq, ckv, kr = S2[:, 0:3], S2[:, 3:5], S2[:, 5:6]
    dense(core, "cq", H, SEQ, copy_to(core, cq))
    dense(core, "ckv", H, SEQ, copy_to(core, ckv))
    dense(core, "kr", H, SEQ, copy_to(core, kr))
    rms_norm(core, cq, 3, SEQ, S6, cq, lambda k: core.col("qa", k), 384)
    rms_norm(core, ckv, 2, SEQ, S6, ckv, lambda k: core.col("kva", k), 256)
    qn, qr, kn = S3, S4, S5
    v = core.slab[6][:, 0:4 * D].rearrange("p (t c) -> p t c", t=4)

    def qb_groups(c0, cw):
        for h in range(2):
            for at, m, dst in ((192 * h, P, qn), (192 * h + P, 64, qr)):
                yield (m, SEQ, lambda w, k, kk, at=at, m=m: (w[:, k, at:at + m], cq[:, kk, :]), "act",
                       lambda eng, ps, dst=dst, m=m, h=c0 // 192 + h: nc.scalar.copy(dst[0:m, h, :], ps))
    run_groups(core, "qb", qb_groups)

    def kvb_groups(c0, cw):
        for h in range(2):
            yield (P, SEQ, lambda w, k, kk, h=h: (w[:, k, 256 * h:256 * h + P], ckv[:, kk, :]), "act",
                   lambda eng, ps, h=c0 // 256 + h: nc.scalar.copy(kn[:, h, :], ps))
            yield from token_groups(ckv, SEQ, 256 * h + P, P, lambda eng, ps, t, at: nc.vector.tensor_copy(v[:, t, at:at + P], ps), "dve",
                                    (c0 // 256 + h) * P)
    run_groups(core, "kvb", kvb_groups)
    rot = core.c("common", "rot32")[0:64, 0:64]
    rope(core, qr, KC, SEQ, rot, cos, sin, rows=64)
    rope(core, kr, 1, SEQ, rot, cos, sin, rows=64)
    units = []
    for h in range(8):
        for n in range(4):
            hi, t = (n + 1) * P, slice(n * P, (n + 1) * P)
            products = [(qn[:, h, t], kn[:, h, 0:hi]), (qr[0:64, h, t], kr[0:64, 0, 0:hi])]
            units.append((P, [(products, hi, c("causal")[:, SEQ - hi:])], [(v[:, b, h * P:(h + 1) * P], P) for b in range(n + 1)],
                          P, 0, qn[:, h, t], None))
    attention(core, units, 192 ** -0.5, core.slab[2][:, 0:1536], core.slab[2][:, 1536:2560], SEQ)
    dense(core, "gate3", H, SEQ, silu(S4), also=also_gate(core, qn, S4))
    dense(core, "wo4", qn, SEQ, copy_to(core, S5), also=also_square(core, S2, S5, SEQ, "act"))
    add_normalised(core, x, S5, S2, lambda k: core.col("post", KC + k))


def retention(core, q, k, v, R):
    nc, ident = core.nc, core.c("common", "ident")
    c = lambda name: core.c("third", name)
    intra = c("intra").rearrange("p (m h i) -> p m h i", m=4, h=2)
    xi = c("xi").rearrange("p (m i) -> p m i", m=4)
    zeta, gamma = c("zeta"), c("gamma")
    kz = core.slab[5][:, 0:2048].rearrange("p (n c) -> p n c", n=4)
    qx = core.slab[5][:, 2048:4096].rearrange("p (m t) -> p m t", m=4)
    score = core.slab[6][:, 0:D].rearrange("p (h m i) -> p h m i", h=2, m=4)
    state = core.slab[6][:, D:D + 512].rearrange("p (m e) -> p m e", m=4)
    by4 = lambda t: t[:, :].rearrange("p (m i) -> p m i", m=4)
    B = core.bank
    with core.stage() as block:
        @block.tensor
        def _(pe):
            for n in range(4):
                for m in range(4):
                    last = nc.tensor.transpose(B[4 + n][:, m * P:(m + 1) * P], k[:, m, n * P:(n + 1) * P], ident)
                last.then_inc(core.p2v.sem, core.p2v.add(1))
            for n in range(4):
                t = slice(n * P, (n + 1) * P)
                if n >= 1:
                    pe.wait_ge(core.v2p.sem, core.v2p.at(2 * n))
                for h in range(2):
                    rows = slice(64 * h, 64 * h + 64)
                    for m in range(4):
                        last = nc.tensor.matmul(B[h][:, m * P:(m + 1) * P], k[rows, m, t], q[rows, m, t], start=True, stop=True)
                last.then_inc(core.p2v.sem, core.p2v.add(1))
                pe.wait_ge(core.v2p.sem, core.v2p.at(2 * n + 1))
                if n >= 1:
                    pe.wait_ge(core.a2p.sem, core.a2p.at(n))
                if n < 3:
                    for head in range(8):
                        rows = slice(64 * (head % 2), 64 * (head % 2) + 64)
                        last = nc.tensor.matmul(B[4][rows, (head // 2) * P:(head // 2 + 1) * P], kz[:, n, head * 64:head * 64 + 64],
                                                v[:, n, head * P:(head + 1) * P], start=True, stop=True)
                    last.then_inc(core.p2v.sem, core.p2v.add(1))
                for head in range(8):
                    h, m = head % 2, head // 2
                    rows = slice(64 * h, 64 * h + 64)
                    out = B[2 + h][:, m * P:(m + 1) * P]
                    last = nc.tensor.matmul(out, v[:, n, head * P:(head + 1) * P], score[:, h, m, :], start=True, stop=n == 0)
                    if n >= 1:
                        last = nc.tensor.matmul(out, state[rows, m, :], qx[rows, m, t], start=False, stop=True)
                last.then_inc(core.p2a.sem, core.p2a.add(1))

        @block.vector
        def _(dve):
            step = Chain(dve, core.dve_step)
            for m in range(4):
                nc.vector.tensor_tensor(qx[:, m].rearrange("p (n i) -> p n i", n=4), q[:, m].rearrange("p (n i) -> p n i", n=4),
                                        xi[:, m].unsqueeze(1).broadcast_to([P, 4, P]), ALU.mult)
            for n in range(4):
                dve.wait_ge(core.p2v.sem, core.p2v.at(n + 1))
                nc.vector.tensor_tensor(kz[:, n].rearrange("p (h c) -> p h c", h=8), B[4 + n][:, :].rearrange("p (h c) -> p h c", h=8),
                                        zeta.unsqueeze(2).broadcast_to([P, 8, 64]), ALU.mult)
            for n in range(4):
                dve.wait_ge(core.p2v.sem, core.p2v.at(5 + 2 * n))
                if n >= 1:
                    dve.wait_ge(core.p2a.sem, core.p2a.at(n))
                for h in range(2):
                    ins = nc.vector.tensor_tensor(score[:, h], by4(B[h]), intra[:, :, h, :], ALU.mult)
                ins.then_inc(core.v2p.sem, core.v2p.add(1))
                if n < 3:
                    dve.wait_ge(core.p2v.sem, core.p2v.at(6 + 2 * n))
                    if n == 0:
                        ins = nc.vector.tensor_copy(state, by4(B[4]))
                    else:
                        dve.wait_ge(core.p2a.sem, core.p2a.at(n + 1))
                        for m in range(4):
                            ins = nc.vector.scalar_tensor_tensor(out=state[:, m], in0=state[:, m], scalar=gamma[:, m:m + 1],
                                                                 in1=B[4][:, m * P:(m + 1) * P], op0=ALU.mult, op1=ALU.add)
                    ins.then_inc(core.v2p.sem, core.v2p.add(1))

        @block.scalar
        def _(act):
            for n in range(4):
                act.wait_ge(core.p2a.sem, core.p2a.at(n + 1))
                for h in range(2):
                    ins = nc.scalar.copy(R[:, h:8:2, n * P:(n + 1) * P], by4(B[2 + h]))
                ins.then_inc(core.a2p.sem, core.a2p.add(1))


def plan_rest(core):
    plan_second(core)
    plan_third(core)


def laid_out_rest(x, chunks):
    return {**laid_out_second(x, chunks), **laid_out_third(x, chunks)}


def program(nc, dram, out, stop_after=3):
    with ExitStack() as ctx:
        ctx.enter_context(nc.allow_non_contiguous_dma("parameters and tiles"))
        core = Core(nc, ctx, dram)
        core.place("common", common_constants(), core.common)
        w_in = dram["w_in"]
        core.plan("ada", dram["w_ada"], 0, 6 * D)
        core.plan("kv", w_in, 3 * D, 3 * D + 512)
        core.plan("q", w_in, 2 * D, 3 * D)
        core.plan("va", w_in, D, 2 * D)
        core.plan("u", w_in, 0, D)
        core.plan("ga", w_in, 3 * D + 512, 4 * D + 512)
        core.plan("pa", dram["w_proj_a"], 0, D)
        core.plan("gb", w_in, 4 * D + 512, 5 * D + 512)
        core.plan("pb", dram["w_proj_b"], 0, D)
        core.plan("wo", dram["w_out"], 0, D)
        core.expert_tile = len(core.tiles)
        for e in range(EXPERTS):
            for f in range(4):
                core.plan(f"gate{e}.{f}", dram["w_gate"][e], f * 512, f * 512 + 512)
                core.plan(f"up{e}.{f}", dram["w_up"][e], f * 512, f * 512 + 512)
            for rows in range(2):
                core.plan(f"down{e}.{rows}", dram["w_down"][e], 0, D, rows * D, (rows + 1) * D)
        plan_rest(core)
        if "rwkv_in" in core.named:
            core.weight_limit = core.named["rwkv_in"][-1][2][-1][0] + 1
        first_block(core)
        if stop_after >= 2:
            second_block(core)
        if stop_after >= 3:
            third_block(core)
        with core.stage() as block:
            @block.sync
            def _(sp):
                sp.dma_start(out, core.slab[0].rearrange("p (k t) -> p k t", k=KC)[:, :, META:]).then_inc(core.stored.sem, core.stored.add(16))
                sp.wait_ge(core.stored.sem, core.stored.at(16))


def laid_out(inputs):
    chunks = lambda a: np.ascontiguousarray(np.asarray(a).reshape(-1, P).T)
    tokens = lambda a: np.ascontiguousarray(np.asarray(a).reshape(-1, KC, P).transpose(2, 1, 0))
    x = {k: np.asarray(v) for k, v in inputs.items()}
    c2 = np.stack([x["c"].reshape(KC, P), x["c_ctx"].reshape(KC, P)], 1)
    arrays = {
        "x": tokens(x["x"]), "ctx": tokens(x["ctx"]),
        "w_ada": x["w_ada"][0], "w_in": x["w_in"][0], "w_proj_a": x["w_proj_a"][0], "w_proj_b": x["w_proj_b"][0],
        "w_out": x["w_out"][0], "w_router": x["w_router"][0], "w_gate": x["w_exp_gate"][0], "w_up": x["w_exp_up"][0],
        "w_down": x["w_exp_down"][0], "gmlp_ln_g": x["gmlp_ln_g"][0], "gmlp_ln_b": x["gmlp_ln_b"][0],
        "b_spatial": x["b_spatial"][0].reshape(-1), "w_spatial": np.ascontiguousarray(x["w_spatial"][0].transpose(2, 0, 1)),
        "p1": np.ascontiguousarray(np.concatenate([
            chunks(c2), chunks(x["b_ada"]), chunks(x["norm1_g"]), chunks(x["b_merge_gate"]), chunks(x["norm2_g"]),
            chunks(x["final_g"]), np.broadcast_to(x["attn_sink"], (P, 16))], 1)),
        "common": packed(common_constants()), "first": packed(first_constants()),
    }
    arrays.update(laid_out_rest(x, chunks))
    return arrays


def kernel(**inputs):
    import concourse.bacc as _bacc
    from concourse.bass_utils import run_bass_kernel_spmd as _run

    nc = _bacc.Bacc("TRN2", target_bir_lowering=False, num_devices=1)
    arrays = laid_out(inputs)
    dram = {k: nc.dram_tensor(f"in_{k}", a.shape, mybir.dt.from_np(a.dtype), kind="ExternalInput").ap() for k, a in arrays.items()}
    out = nc.dram_tensor("out_channels", (P, KC, SEQ), F32, kind="ExternalOutput").ap()
    program(nc, dram, out)
    r = _run(nc, [{f"in_{k}": a for k, a in arrays.items()}], core_ids=[0])
    return np.ascontiguousarray(r.results[0]["out_channels"].transpose(2, 1, 0).reshape(1, SEQ, D))
```
